# Optimizing a Trainium2 kernel written in Bass

```python
import math
import jax
import jax.numpy as jnp
from jax import lax
import numpy as np

D_MODEL = 1024
BATCH = 1
SEQ = 512
DEPTH = 2

RMS_EPS = 1e-6
LN_EPS = 1e-5
NEG_INF = -1e30

NSA_HEADS = 8
NSA_KV_HEADS = 2
NSA_GROUP = NSA_HEADS // NSA_KV_HEADS
HEAD_DIM = 64
CMP_BLOCK = 32
CMP_STRIDE = 16
CMP_HIDDEN = 256
SEL_BLOCK = 64
SEL_TOPK = 16
WINDOW = 512
Q_BLOCK = 64
FORCE_BONUS = 1e4

SSM_HEADS = 8
SSM_HEAD_DIM = 64
SSM_D_INNER = SSM_HEADS * SSM_HEAD_DIM
SSM_GROUPS = 2
SSM_STATE = 128
SSM_CONV = 4
SSM_CHUNK = 128
SSM_BC_DIM = SSM_GROUPS * SSM_STATE
SSM_CONV_DIM = SSM_D_INNER + 2 * SSM_BC_DIM

GMLP_WIDTH = 2 * D_MODEL
GMLP_GROUPS = 8
GMLP_GROUP_DIM = GMLP_WIDTH // GMLP_GROUPS
GMLP_CHUNK = 128

FFN_HIDDEN = -(-8 * D_MODEL // (3 * 256)) * 256

NSA_Q_DIM = NSA_HEADS * HEAD_DIM
NSA_KV_DIM = NSA_KV_HEADS * HEAD_DIM
NSA_GATE_DIM = 3 * NSA_HEADS
EVEN_SPLITS = (NSA_Q_DIM,) + (NSA_KV_DIM,) * 6 + (NSA_GATE_DIM, SSM_D_INNER, SSM_CONV_DIM, SSM_HEADS)
EVEN_SPLIT_POINTS = [int(v) for v in np.cumsum(EVEN_SPLITS)[:-1]]
EVEN_IN_DIM = int(sum(EVEN_SPLITS))
EVEN_MIX_DIM = NSA_Q_DIM + SSM_D_INNER

kernel_name = 'hybrid_nsa_ssd_gmlp_trunk'

def rms_norm(x, w):
    xf = x.astype(jnp.float32)
    y = xf * lax.rsqrt(jnp.mean(jnp.square(xf), axis=-1, keepdims=True) + RMS_EPS)
    return (y * w.astype(jnp.float32)).astype(x.dtype)

def layer_norm(x, w, b):
    xf = x.astype(jnp.float32)
    mu = jnp.mean(xf, axis=-1, keepdims=True)
    var = jnp.mean(jnp.square(xf - mu), axis=-1, keepdims=True)
    y = (xf - mu) * lax.rsqrt(var + LN_EPS) * w.astype(jnp.float32) + b.astype(jnp.float32)
    return y.astype(x.dtype)

def masked_softmax(scores, mask):
    p = jax.nn.softmax(jnp.where(mask, scores, NEG_INF), axis=-1)
    return jnp.where(mask, p, 0.0)

def alibi_slopes(n):
    return (2.0 ** (-8.0 * np.arange(1, n + 1) / n)).astype(np.float32)

def compress_blocks(kv, pe, w1, w2):
    s = kv.shape[2]
    n_cmp = (s - CMP_BLOCK) // CMP_STRIDE + 1
    idx = np.arange(n_cmp)[:, None] * CMP_STRIDE + np.arange(CMP_BLOCK)[None, :]
    blocks = kv[:, :, idx] + pe
    blocks = blocks.reshape(blocks.shape[:3] + (CMP_BLOCK * HEAD_DIM,))
    return jax.nn.silu(blocks @ w1) @ w2

def selection_overlap(n_cmp, n_sel):
    cs = np.arange(n_cmp)[:, None] * CMP_STRIDE
    ss = np.arange(n_sel)[None, :] * SEL_BLOCK
    ov = np.minimum(cs + CMP_BLOCK, ss + SEL_BLOCK) - np.maximum(cs, ss)
    return (np.clip(ov, 0, None) / CMP_BLOCK).astype(np.float32)

def nsa_attention(q, kc, vc, ks, vs, kw, vw, gate_logits, cmp_pe, cmp_w1, cmp_w2):
    b, s = q.shape[0], q.shape[1]
    dtype = q.dtype
    f32 = jnp.float32
    g, r, hd = NSA_KV_HEADS, NSA_GROUP, HEAD_DIM
    qg = (q * (hd ** -0.5)).transpose(0, 2, 1, 3).reshape(b, g, r, s, hd)
    kc, vc, ks, vs, kw, vw = [t.transpose(0, 2, 1, 3) for t in (kc, vc, ks, vs, kw, vw)]
    slopes = jnp.asarray(alibi_slopes(NSA_HEADS).reshape(g, r))[:, :, None, None]
    pos = np.arange(s)

    kcb = compress_blocks(kc, cmp_pe[0], cmp_w1[0], cmp_w2[0])
    vcb = compress_blocks(vc, cmp_pe[1], cmp_w1[1], cmp_w2[1])
    n_cmp = kcb.shape[2]
    cmp_end = np.arange(n_cmp) * CMP_STRIDE + CMP_BLOCK - 1
    d_cmp = (pos[:, None] - cmp_end[None, :]).astype(np.float32)
    s_cmp = jnp.einsum('bgrtd,bgcd->bgrtc', qg, kcb).astype(f32) - slopes * d_cmp
    p_cmp = masked_softmax(s_cmp, d_cmp >= 0)
    o_cmp = jnp.einsum('bgrtc,bgcd->bgrtd', p_cmp.astype(dtype), vcb)

    n_sel = s // SEL_BLOCK
    top_k = min(SEL_TOPK, n_sel)
    imp = jnp.einsum('bgrtc,cj->bgtj', p_cmp, jnp.asarray(selection_overlap(n_cmp, n_sel)))
    blk = np.arange(n_sel)[None, :]
    cur = (pos // SEL_BLOCK)[:, None]
    forced = ((blk == 0) | (blk == cur) | (blk == cur - 1)).astype(np.float32) * FORCE_BONUS
    eligible = blk * SEL_BLOCK <= pos[:, None]
    imp = jnp.where(eligible, imp + forced, -1.0)
    _, sel_idx = lax.top_k(imp, top_k)

    nqb = s // Q_BLOCK
    q_blocks = qg.reshape(b, g, r, nqb, Q_BLOCK, hd).transpose(3, 0, 1, 2, 4, 5)
    idx_blocks = sel_idx.reshape(b, g, nqb, Q_BLOCK, top_k).transpose(2, 0, 1, 3, 4)
    ks_blk = ks.reshape(b, g, n_sel, SEL_BLOCK, hd)
    vs_blk = vs.reshape(b, g, n_sel, SEL_BLOCK, hd)
    pad = ((0, 0), (0, 0), (WINDOW, 0), (0, 0))
    kw_pad = jnp.pad(kw, pad)
    vw_pad = jnp.pad(vw, pad)
    gather_blocks = jax.vmap(jax.vmap(lambda kv, ix: kv[ix]))
    n_key_sel = top_k * SEL_BLOCK
    n_key_win = Q_BLOCK + WINDOW

    def query_block(args):
        qi, q_blk, ix = args
        start = qi * Q_BLOCK
        t = start + jnp.arange(Q_BLOCK)
        k_sel = gather_blocks(ks_blk, ix).reshape(b, g, Q_BLOCK, n_key_sel, hd)
        v_sel = gather_blocks(vs_blk, ix).reshape(b, g, Q_BLOCK, n_key_sel, hd)
        s_pos = (ix[..., None] * SEL_BLOCK + jnp.arange(SEL_BLOCK)).reshape(b, g, Q_BLOCK, n_key_sel)
        d_sel = (t[:, None] - s_pos)[:, :, None]
        s_sel = jnp.einsum('bgrqd,bgqkd->bgrqk', q_blk, k_sel).astype(f32) - slopes * d_sel.astype(f32)
        o_sel = jnp.einsum('bgrqk,bgqkd->bgrqd', masked_softmax(s_sel, d_sel >= 0).astype(dtype), v_sel)
        k_win = lax.dynamic_slice_in_dim(kw_pad, start, n_key_win, axis=2)
        v_win = lax.dynamic_slice_in_dim(vw_pad, start, n_key_win, axis=2)
        w_pos = start - WINDOW + jnp.arange(n_key_win)
        d_win = t[:, None] - w_pos[None, :]
        s_win = jnp.einsum('bgrqd,bgkd->bgrqk', q_blk, k_win).astype(f32) - slopes * d_win.astype(f32)
        win_mask = (d_win >= 0) & (d_win < WINDOW) & (w_pos >= 0)[None, :]
        o_win = jnp.einsum('bgrqk,bgkd->bgrqd', masked_softmax(s_win, win_mask).astype(dtype), v_win)
        return o_sel, o_win

    o_sel, o_win = lax.map(query_block, (jnp.arange(nqb), q_blocks, idx_blocks))
    o_sel = o_sel.transpose(1, 2, 3, 0, 4, 5).reshape(b, g, r, s, hd)
    o_win = o_win.transpose(1, 2, 3, 0, 4, 5).reshape(b, g, r, s, hd)

    gates = jax.nn.sigmoid(gate_logits.astype(f32)).astype(dtype).transpose(0, 2, 1, 3).reshape(b, g, r, s, 3)
    out = gates[..., 0:1] * o_cmp + gates[..., 1:2] * o_sel + gates[..., 2:3] * o_win
    return out.reshape(b, NSA_HEADS, s, hd).transpose(0, 2, 1, 3).reshape(b, s, NSA_HEADS * hd)

def causal_depthwise_conv(x, w, bias):
    ch = x.shape[-1]
    y = lax.conv_general_dilated(x, w[:, None, :].astype(x.dtype), window_strides=(1,),
                                 padding=[(SSM_CONV - 1, 0)], dimension_numbers=('NWC', 'WIO', 'NWC'),
                                 feature_group_count=ch)
    return y + bias.astype(x.dtype)

def ssd_chunked(x, a, bm, cm):
    b, s, h, p = x.shape
    g, n = bm.shape[2], bm.shape[3]
    r = h // g
    c, l = s // SSM_CHUNK, SSM_CHUNK
    x = x.reshape(b, c, l, g, r, p)
    bm = bm.reshape(b, c, l, g, n)
    cm = cm.reshape(b, c, l, g, n)
    a_cs = jnp.cumsum(a.reshape(b, c, l, g, r).transpose(0, 3, 4, 1, 2), axis=-1)
    causal = np.tril(np.ones((l, l), dtype=bool))
    decay_in = jnp.exp(jnp.where(causal, a_cs[..., :, None] - a_cs[..., None, :], -jnp.inf))
    cb = jnp.einsum('bclgn,bcsgn->bgcls', cm, bm)
    y_diag = jnp.einsum('bgrcls,bcsgrp->bclgrp', cb[:, :, None] * decay_in, x)
    decay_states = jnp.exp(a_cs[..., -1:] - a_cs)
    states = jnp.einsum('bcsgn,bgrcs,bcsgrp->bcgrpn', bm, decay_states, x)
    chunk_decay = jnp.exp(a_cs[..., -1])

    def step(carry, inp):
        st, dec = inp
        return carry * dec[..., None, None] + st, carry

    init = jnp.zeros((b, g, r, p, n), jnp.float32)
    _, prev = lax.scan(step, init, (states.transpose(1, 0, 2, 3, 4, 5), chunk_decay.transpose(3, 0, 1, 2)))
    prev = prev.transpose(1, 0, 2, 3, 4, 5)
    y_off = jnp.einsum('bclgn,bcgrpn,bgrcl->bclgrp', cm, prev, jnp.exp(a_cs))
    return (y_diag + y_off).reshape(b, s, h, p)

def mamba2_mixer(z, xbc, dt, conv_w, conv_b, dt_bias, a_log, d_skip, norm_w):
    b, s = z.shape[0], z.shape[1]
    dtype = z.dtype
    f32 = jnp.float32
    xbc = jax.nn.silu(causal_depthwise_conv(xbc, conv_w, conv_b))
    xs, bm, cm = jnp.split(xbc, [SSM_D_INNER, SSM_D_INNER + SSM_BC_DIM], axis=-1)
    xs = xs.reshape(b, s, SSM_HEADS, SSM_HEAD_DIM).astype(f32)
    bm = bm.reshape(b, s, SSM_GROUPS, SSM_STATE).astype(f32)
    cm = cm.reshape(b, s, SSM_GROUPS, SSM_STATE).astype(f32)
    dt = jax.nn.softplus(dt.astype(f32) + dt_bias.astype(f32))
    a = -jnp.exp(a_log.astype(f32))
    y = ssd_chunked(xs * dt[..., None], dt * a, bm, cm)
    y = y + xs * d_skip.astype(f32)[:, None]
    gsz = SSM_D_INNER // SSM_GROUPS
    y = y.reshape(b, s, SSM_GROUPS, gsz) * jax.nn.silu(z.astype(f32)).reshape(b, s, SSM_GROUPS, gsz)
    y = rms_norm(y, norm_w.reshape(SSM_GROUPS, gsz))
    return y.reshape(b, s, SSM_D_INNER).astype(dtype)

def attn_ssm_mixer(h, w_in, w_out, cmp_pe, cmp_w1, cmp_w2, conv_w, conv_b, dt_bias, a_log, d_skip, norm_w):
    b, s = h.shape[0], h.shape[1]
    q, kc, vc, ks, vs, kw, vw, gl, z, xbc, dt = jnp.split(h @ w_in, EVEN_SPLIT_POINTS, axis=-1)
    kv = [t.reshape(b, s, NSA_KV_HEADS, HEAD_DIM) for t in (kc, vc, ks, vs, kw, vw)]
    o_attn = nsa_attention(q.reshape(b, s, NSA_HEADS, HEAD_DIM), kv[0], kv[1], kv[2], kv[3], kv[4], kv[5],
                           gl.reshape(b, s, NSA_HEADS, 3), cmp_pe, cmp_w1, cmp_w2)
    o_ssm = mamba2_mixer(z, xbc, dt, conv_w, conv_b, dt_bias, a_log, d_skip, norm_w)
    return jnp.concatenate([o_attn, o_ssm], axis=-1) @ w_out

def chunked_gmlp(h, w_in, ln_w, ln_b, w_s, b_s, w_out):
    b, s = h.shape[0], h.shape[1]
    u, v = jnp.split(jax.nn.gelu(h @ w_in, approximate=False), 2, axis=-1)
    v = layer_norm(v, ln_w, ln_b).reshape(b, s // GMLP_CHUNK, GMLP_CHUNK, GMLP_GROUPS, GMLP_GROUP_DIM)
    causal = np.tril(np.ones((GMLP_CHUNK, GMLP_CHUNK), dtype=bool))
    ws = jnp.where(causal, w_s, jnp.zeros_like(w_s))
    mixed = jnp.einsum('gts,bcsgd->bctgd', ws, v) + b_s.T[:, :, None]
    return (u * mixed.reshape(b, s, GMLP_WIDTH)) @ w_out

def swiglu_ffn(h, w_gate, w_up, w_down):
    return (jax.nn.silu(h @ w_gate) * (h @ w_up)) @ w_down

def setup_inputs(seed: int = 0) -> dict:
    key = jax.random.key(seed)
    k = jax.random.split(key, 24)
    ne, no = (DEPTH + 1) // 2, DEPTH // 2
    f32 = jnp.float32

    def normal(kk, shape, scale):
        return scale * jax.random.normal(kk, shape, f32)

    dt0 = jnp.exp(jax.random.uniform(k[12], (ne, SSM_HEADS), f32, math.log(1e-3), math.log(1e-1)))
    return {
        'x': normal(k[0], (BATCH, SEQ, D_MODEL), 1.0),
        'norm_gains': 1.0 + normal(k[1], (DEPTH, 4, D_MODEL), 0.05),
        'ffn_w_gate': normal(k[2], (DEPTH, D_MODEL, FFN_HIDDEN), D_MODEL ** -0.5),
        'ffn_w_up': normal(k[3], (DEPTH, D_MODEL, FFN_HIDDEN), D_MODEL ** -0.5),
        'ffn_w_down': normal(k[4], (DEPTH, FFN_HIDDEN, D_MODEL), FFN_HIDDEN ** -0.5),
        'ev_w_in': normal(k[5], (ne, D_MODEL, EVEN_IN_DIM), D_MODEL ** -0.5),
        'ev_w_out': normal(k[6], (ne, EVEN_MIX_DIM, D_MODEL), EVEN_MIX_DIM ** -0.5),
        'nsa_cmp_pe': normal(k[7], (ne, 2, CMP_BLOCK, HEAD_DIM), 0.1),
        'nsa_cmp_w1': normal(k[8], (ne, 2, CMP_BLOCK * HEAD_DIM, CMP_HIDDEN), (CMP_BLOCK * HEAD_DIM) ** -0.5),
        'nsa_cmp_w2': normal(k[9], (ne, 2, CMP_HIDDEN, HEAD_DIM), CMP_HIDDEN ** -0.5),
        'ssm_conv_w': normal(k[10], (ne, SSM_CONV, SSM_CONV_DIM), SSM_CONV ** -0.5),
        'ssm_conv_b': normal(k[11], (ne, SSM_CONV_DIM), 0.02),
        'ssm_dt_bias': dt0 + jnp.log(-jnp.expm1(-dt0)),
        'ssm_a_log': jnp.log(jax.random.uniform(k[13], (ne, SSM_HEADS), f32, 1.0, 16.0)),
        'ssm_d': 1.0 + normal(k[14], (ne, SSM_HEADS), 0.1),
        'ssm_norm_w': 1.0 + normal(k[15], (ne, SSM_D_INNER), 0.05),
        'od_w_in': normal(k[16], (no, D_MODEL, 2 * GMLP_WIDTH), D_MODEL ** -0.5),
        'od_ln_w': 1.0 + normal(k[17], (no, GMLP_WIDTH), 0.05),
        'od_ln_b': normal(k[18], (no, GMLP_WIDTH), 0.02),
        'od_w_s': normal(k[19], (no, GMLP_GROUPS, GMLP_CHUNK, GMLP_CHUNK), GMLP_CHUNK ** -0.5),
        'od_b_s': 1.0 + normal(k[20], (no, GMLP_GROUPS, GMLP_CHUNK), 0.05),
        'od_w_out': normal(k[21], (no, GMLP_WIDTH, D_MODEL), GMLP_WIDTH ** -0.5),
    }

def reference(x, norm_gains, ffn_w_gate, ffn_w_up, ffn_w_down, ev_w_in, ev_w_out, nsa_cmp_pe, nsa_cmp_w1,
              nsa_cmp_w2, ssm_conv_w, ssm_conv_b, ssm_dt_bias, ssm_a_log, ssm_d, ssm_norm_w, od_w_in, od_ln_w,
              od_ln_b, od_w_s, od_b_s, od_w_out):
    h = x
    for layer in range(DEPTH):
        gains = norm_gains[layer]
        i = layer // 2
        y = rms_norm(h, gains[0])
        if layer % 2 == 0:
            y = attn_ssm_mixer(y, ev_w_in[i], ev_w_out[i], nsa_cmp_pe[i], nsa_cmp_w1[i], nsa_cmp_w2[i],
                               ssm_conv_w[i], ssm_conv_b[i], ssm_dt_bias[i], ssm_a_log[i], ssm_d[i], ssm_norm_w[i])
        else:
            y = chunked_gmlp(y, od_w_in[i], od_ln_w[i], od_ln_b[i], od_w_s[i], od_b_s[i], od_w_out[i])
        h = h + rms_norm(y, gains[1])
        y = swiglu_ffn(rms_norm(h, gains[2]), ffn_w_gate[layer], ffn_w_up[layer], ffn_w_down[layer])
        h = h + rms_norm(y, gains[3])
    return h


_drawn_inputs = setup_inputs


def setup_inputs(seed=0):
    import zlib

    import numpy as np

    out = dict(_drawn_inputs(seed))
    spreads = {}
    factors = {}
    for name, (base, spread) in spreads.items():
        noise = np.random.default_rng([zlib.crc32(name.encode()), seed]).standard_normal(out[name].shape)
        drawn = base * np.exp(spread * noise) if base else spread * noise
        out[name] = jnp.asarray(drawn.astype(out[name].dtype))
    for name, factor in factors.items():
        out[name] = (out[name] * factor).astype(out[name].dtype)
    return out
```

```python
import numpy as np

D_MODEL = 1024
SEQ = 512
RMS_EPS, LN_EPS = 1e-6, 1e-5
HEADS, GROUPS, HEAD_DIM = 8, 2, 64
CMP_BLOCK, CMP_STRIDE, CMP_HIDDEN = 32, 16, 256
N_CMP = (SEQ - CMP_BLOCK) // CMP_STRIDE + 1
SSM_INNER, SSM_STATE, CONV_TAPS = 512, 128, 4
WIDTH = 2 * D_MODEL
FFN = 2816

P = 128
KT = D_MODEL // P
TT = SEQ // P
FT = FFN // P
WT = WIDTH // P
SLOTS = 4
UNIT = 1024
TAIL = 4

U_IN0 = 0
U_OUT0 = U_IN0 + 22
U_GU0 = U_OUT0 + KT
U_DN0 = U_GU0 + 2 * FT
U_V = U_DN0 + FT
U_U = U_V + WT
U_OUT1 = U_U + WT
U_GU1 = U_OUT1 + WT
U_DN1 = U_GU1 + 2 * FT
U_END = U_DN1 + FT
ROWS_END = (U_GU0, U_V, U_GU1, U_END)

C_Q, C_KC, C_VC, C_KS, C_VS, C_KW, C_VW, C_GATE, C_Z, C_XBC, C_DT = (
    0, 512, 640, 768, 896, 1024, 1152, 1280, 1304, 1816, 2840)
N_GATE = 3 * HEADS
COLS0 = 32 + 8 + 4 + 64
MASKED = 1e33
FLOOR = 1e29


def build(nc, x, gains, stream, w_small, cols, w1, w2, dt_bias, a_log, d_skip, w_s, b_s, out, stop=99):
    from contextlib import ExitStack

    import concourse.bass as bass
    from concourse import mybir

    f32, f32r, bf16 = mybir.dt.float32, mybir.dt.float32r, mybir.dt.bfloat16
    ALU = mybir.AluOpType
    ACT = mybir.ActivationFunctionType
    AX = mybir.AxisListType
    ds = bass.ds

    base = [16512 // 4]

    def at(name, shape, dt=f32, where=None):
        size = int(np.prod(shape[1:])) * (2 if dt is bf16 else 4)
        if where is None:
            where = base[0]
            base[0] += -(-size // 32) * 8
            assert base[0] * 4 <= 229344, (name, base[0] * 4)
        return nc.alloc_sbuf_tensor_at(name, list(shape), dt, offset=where * 4)

    h = at("h", [P, TT, D_MODEL])
    yhi = at("yhi", [P, KT, SEQ], f32r)
    ylo = at("ylo", [P, KT, SEQ], f32r)
    raw = at("raw", [P, SLOTS, UNIT])
    whi = at("whi", [P, SLOTS, UNIT], f32r)
    wlo = at("wlo", [P, SLOTS, UNIT], f32r)
    tmp_at = base[0]
    tmp = at("tmp", [P, 4, SEQ])
    tmp_a = at("tmp_a", [P, D_MODEL], where=tmp_at)
    tmp_b = at("tmp_b", [P, D_MODEL], where=tmp_at + D_MODEL)
    gain_pre = at("gain_pre", [P, D_MODEL])
    post_at = base[0]
    gain_post = at("gain_post", [P, D_MODEL])
    wsmhi = at("wsmhi", [P, 8, 32], f32r, where=post_at)
    wsmlo = at("wsmlo", [P, 8, 32], f32r, where=post_at + 256)
    w2s = at("w2s", [P, 2, 2, HEAD_DIM], where=post_at + 512)
    hidc = at("hidc", [P, 2, 2, 2 * N_CMP], where=post_at + 768)
    junk = at("junk", [P, D_MODEL], bf16)
    ident = at("ident", [P, P])
    stat = at("stat", [P, 4, 16])
    rst_t = at("rst_t", [P, 4, 16])
    half = at("half", [P, 8])
    arena = base[0]
    ARENA = FT * SEQ * 2
    hidhi = at("hidhi", [P, FT, SEQ], f32r)
    hidlo = at("hidlo", [P, FT, SEQ], f32r)

    a = [arena]

    def inner(name, shape, dt=f32, where=None):
        w = a[0] if where is None else where
        t = at(name, shape, dt, where=w)
        if where is None:
            a[0] += -(-int(np.prod(shape[1:])) // 8) * 8
            assert a[0] <= arena + ARENA, (name, a[0] - arena - ARENA)
        return t

    qT = inner("qT", [P, 4, SEQ])
    ksD = inner("ksD", [P, 2, GROUPS, SEQ])
    vN = inner("vN", [P, TT, 256])
    bias_at = a[0]
    bias = inner("bias", [P, HEADS, SEQ])
    w1v = inner("w1v", [P, 16, CMP_HIDDEN], where=bias_at)
    xbcT = inner("xbcT", [P, 8, SEQ])
    zN = inner("zN", [P, TT, SSM_INNER])
    early_at = a[0]
    w1k = inner("w1k", [P, 16, CMP_HIDDEN])
    blk = inner("blk", [P, 2, 16, 2 * N_CMP])
    cT = inner("cT", [P, 2, SEQ])
    late = early_at
    xN = inner("xN", [P, TT, SSM_INNER], where=late); late += 2048
    BN = inner("BN", [P, TT, 256], where=late); late += 1024
    dec = inner("dec", [P, HEADS, P], where=late); late += 1024
    Mt = inner("Mt", [P, HEADS, P], where=late); late += 1024
    xdt = inner("xdt", [P, SSM_INNER], where=late); late += 512
    xdd = inner("xdd", [P, SSM_INNER], where=late); late += 512
    prev = inner("prev", [P, SSM_INNER], where=late); late += 512
    assert late <= a[0]
    small = {"wsm": inner("wsm", [P, 256], where=bias_at + 4096 + 7 * SEQ)}
    for nm, n in (("cols", COLS0), ("dtb", 8), ("alog", 8),
                  ("dsk", 8), ("U", 128), ("mneg", 128)):
        small[nm] = at("c_" + nm, [P, n])
    small["cw"], small["cb"] = small["cols"][:, 0:32], small["cols"][:, 32:40]
    small["nw"], small["pe2"] = small["cols"][:, 40:44], small["cols"][:, 44:108]
    kcb = inner("kcb", [P, GROUPS, N_CMP], where=late)
    vcb = inner("vcb", [P, GROUPS, HEAD_DIM], where=late + 64)
    dcmp = inner("dcmp", [P, TT, N_CMP], where=late + 192)
    assert late + 320 <= arena + ARENA
    sm = at("sm", [P, 16, 32])
    gates = at("gates", [P, TT, N_GATE])
    ones = at("ones", [P, P])
    pr_at = early_at
    prob = inner("prob", [P, 2, 1280], where=pr_at)
    probT = inner("probT", [P, 2, 1280], where=pr_at + 2560)
    pc = inner("pc", [P, TT, N_CMP], where=pr_at + 5120)
    pcT = inner("pcT", [P, SEQ], where=pr_at + 5120 + 128)
    att = inner("att", [P, 8, 8], where=pr_at + 5120 + 128 + 512)
    assert pr_at + 5120 + 128 + 512 + 64 <= arena + ARENA
    vG = at("vG", [P, TT, WIDTH], where=arena)
    glo = at("glo", [P, WT, SEQ], f32r, where=arena)
    mixed = at("mixed", [P, WT, SEQ], where=arena + 8192)
    ghi = at("ghi", [P, WT, SEQ], f32r, where=arena + 8192)
    Rt = at("Rt", [P, WT, P], where=arena + 16384)
    ws = at("ws", [P, 8, P], where=arena + 18432)
    wsT = at("wsT", [P, 8, P], where=arena + 19456)
    bsbc = at("bsbc", [P, 8, P], where=arena + 20480)
    lncols = at("lncols", [P, 2 * WT], where=arena + 21504)
    lnw, lnb = lncols[:, 0:WT], lncols[:, WT:2 * WT]
    vstat = at("vstat", [P, TT, 4, 6], where=arena + 21504 + 32)
    vmv = at("vmv", [P, TT, 8], where=arena + 21504 + 32 + 96)

    ctx = ExitStack()
    with ctx:
        ps = ctx.enter_context(nc.psum_tensor("ps", [P, 8, 512], f32))

        def sem(name):
            return ctx.enter_context(nc.semaphore(name))

        raw_loaded = [sem(f"raw_loaded{i}") for i in range(SLOTS)]
        hi_done, lo_done, unit_used = sem("hi_done"), sem("lo_done"), sem("unit_used")
        x_loaded = [sem(f"x_loaded{i}") for i in range(TT)]
        gain_pre_loaded, gain_post_loaded = sem("gain_pre_loaded"), sem("gain_post_loaded")
        consts_loaded, cmp_loaded, gmlp_loaded = sem("consts_loaded"), sem("cmp_loaded"), sem("gmlp_loaded")
        act_step, dve_step, pool_step = sem("act_step"), sem("dve_step"), sem("pool_step")
        consts_made = sem("consts_made")
        presq_done, prerstd_done, hn_done, transposed = (
            sem("presq_done"), sem("prerstd_done"), sem("hn_done"), sem("transposed"))
        yhi_done, ylo_done = sem("yhi_done"), sem("ylo_done")
        rows_done, postsq_done, postrstd_done, scaled_done, h_ready = (
            sem("rows_done"), sem("postsq_done"), sem("postrstd_done"), sem("scaled_done"), sem("h_ready"))
        silu_done, mult_done, hidhi_done, hidlo_done = (
            sem("silu_done"), sem("mult_done"), sem("hidhi_done"), sem("hidlo_done"))
        staged = sem("staged")
        q_out, ka_out, kd_out, c_out, v_out = sem("q_out"), sem("ka_out"), sem("kd_out"), sem("c_out"), sem("v_out")
        conv_done, xbc_ready, z_ready = sem("conv_done"), sem("xbc_ready"), sem("z_ready")
        wsm_hi, wsm_lo, small_done = sem("wsm_hi"), sem("wsm_lo"), sem("small_done")
        blk_done, cmp_hid, cmp_silu, cmp_kv, cmp_out, bias_done = (
            sem("blk_done"), sem("cmp_hid"), sem("cmp_silu"), sem("cmp_kv"), sem("cmp_out"), sem("bias_done"))
        gate_exp, sp_exp, sp_ln, a_exp, dt_in, dt_w, da_done = (
            sem("gate_exp"), sem("sp_exp"), sem("sp_ln"), sem("a_exp"), sem("dt_in"), sem("dt_w"), sem("da_done"))
        cums_done, nacs_done, dst_in, ssm_exp = sem("cums_done"), sem("nacs_done"), sem("dst_in"), sem("ssm_exp")
        xb_tr, xn_out, bn_out = sem("xb_tr"), sem("xn_out"), sem("bn_out")
        ssm_seg, dec_done, m_done, xd_done, ssm_mm, prev_done, y_gated = (
            sem("ssm_seg"), sem("dec_done"), sem("m_done"), sem("xd_done"), sem("ssm_mm"), sem("prev_done"),
            sem("y_gated"))
        ysq_done, yr_done, yn_done, y_tr, mixs_hi, mixs_lo = (
            sem("ysq_done"), sem("yr_done"), sem("yn_done"), sem("y_tr"), sem("mixs_hi"), sem("mixs_lo"))
        qk_done, biased, cbiased, exp_done, cexp_done, scaled, p_tr, pt_act, pt_dve, pv_done, mixa_hi, mixa_lo = (
            sem("qk_done"), sem("biased"), sem("cbiased"), sem("exp_done"), sem("cexp_done"), sem("scaled"),
            sem("p_tr"), sem("pt_act"), sem("pt_dve"), sem("pv_done"), sem("mixa_hi"), sem("mixa_lo"))
        ws_masked, ws_tr, ws_out, rowsum_done, r_done = (
            sem("ws_masked"), sem("ws_tr"), sem("ws_out"), sem("rowsum_done"), sem("r_done"))
        v_done, vgelu_done, vmv_done, vrstd_done, vnorm_done = (
            sem("v_done"), sem("vgelu_done"), sem("vmv_done"), sem("vrstd_done"), sem("vnorm_done"))
        mix_mm, mixed_done, ugelu_done, g_done, ghi_done, glo_done = (
            sem("mix_mm"), sem("mixed_done"), sem("ugelu_done"), sem("g_done"), sem("ghi_done"), sem("glo_done"))
        out_written = sem("out_written")
        block = ctx.enter_context(nc.Block())

        n_small = 9

        in_cols = [C_Q + P * j for j in range(4)] + [C_KS, C_KW, C_KC, C_VC]
        PAIRS = HEADS // 2

        @block.sync
        def _(sp):
            def load(u, i=0):
                s = u % SLOTS
                if u >= SLOTS:
                    sp.wait_ge(lo_done, 4 * (u // 4 + i) + s - 3)
                src = stream[ds(4 * i + u, 1), :, :].rearrange("a p n -> (a p) n")
                sp.dma_start(raw[:, s, :], src).then_inc(raw_loaded[s], 16)

            def loads(u0, u1):
                turns = (u1 - u0) // 4
                if turns > 1:
                    with sp.Fori(0, turns) as i:
                        for j in range(4):
                            load(u0 + j, i)
                    u0 += 4 * turns
                for u in range(u0, u1):
                    load(u)

            def gain(dst, layer, k, signal):
                sp.dma_start(dst[:], gains[layer, k:k + 1, :].broadcast_to([P, D_MODEL])).then_inc(signal, 16)

            for t in range(TT):
                sp.dma_start(h[:, t, :], x[0].rearrange("(t p) d -> p t d", p=P)[:, t, :]).then_inc(x_loaded[t], 16)
            gain(gain_pre, 0, 0, gain_pre_loaded)
            for u in range(4):
                load(u)
            c = small
            sp.dma_start(c["wsm"][:], w_small).then_inc(consts_loaded, 16)
            sp.dma_start(c["cols"][:], cols[:, 0:COLS0]).then_inc(consts_loaded, 16)
            sp.dma_start(c["dtb"][:], dt_bias[0:1, :].broadcast_to([P, HEADS])).then_inc(consts_loaded, 16)
            sp.dma_start(c["alog"][:], a_log[0:1, :].broadcast_to([P, HEADS])).then_inc(consts_loaded, 16)
            sp.dma_start(c["dsk"][:], d_skip[0:1, :].broadcast_to([P, HEADS])).then_inc(consts_loaded, 16)
            for u in range(4, 8):
                load(u)
            sp.dma_start(w1k[:], w1[0, 0].rearrange("(t p) n -> p t n", p=P)).then_inc(cmp_loaded, 16)
            sp.dma_start(w1v[:], w1[0, 1].rearrange("(t p) n -> p t n", p=P)).then_inc(cmp_loaded, 16)
            sp.dma_start(w2s[:].rearrange("p y k d -> p (y k) d"),
                         w2[0].rearrange("y (k p) d -> p (y k) d", p=P)).then_inc(cmp_loaded, 16)
            loads(8, U_GU0)
            sp.wait_ge(cmp_kv, 1)
            gain(gain_post, 0, 1, gain_post_loaded)
            sp.wait_ge(ylo_done, 4)
            gain(gain_pre, 0, 2, gain_pre_loaded)
            if stop > 1:
                loads(U_GU0, U_GU0 + 4)
                sp.wait_ge(h_ready, 4)
                gain(gain_post, 0, 3, gain_post_loaded)
                sp.wait_ge(hn_done, 8)
                gain(gain_pre, 1, 0, gain_pre_loaded)
                loads(U_GU0 + 4, U_V)
            if stop > 2:
                loads(U_V, U_V + 4)
                sp.wait_ge(h_ready, 8)
                gain(gain_post, 1, 1, gain_post_loaded)
                sp.wait_ge(hn_done, 12)
                gain(gain_pre, 1, 2, gain_pre_loaded)
                sp.dma_start(ws[:], w_s[0].rearrange("g t s -> t g s")).then_inc(gmlp_loaded, 16)
                for g in range(8):
                    sp.dma_start(bsbc[:, g, :], b_s[0, g:g + 1, :].broadcast_to([P, P])).then_inc(gmlp_loaded, 16)
                sp.dma_start(lncols[:], cols[:, COLS0:COLS0 + 2 * WT]).then_inc(gmlp_loaded, 16)
                loads(U_V + 4, U_GU1)
            if stop > 3:
                loads(U_GU1, U_GU1 + 4)
                sp.wait_ge(h_ready, 12)
                gain(gain_post, 1, 3, gain_post_loaded)
                loads(U_GU1 + 4, U_END)
            n_ready = {1: 4, 2: 8, 3: 12}.get(stop, 16)
            o3 = out[0].rearrange("(t p) d -> p t d", p=P)
            for t in range(TT):
                sp.wait_ge(h_ready, n_ready - TT + t + 1)
                sp.dma_start(o3[:, t, :], h[:, t, :]).then_inc(out_written, 16)
            sp.wait_ge(out_written, 16 * TT)

        last_unit = {1: U_GU0, 2: U_V, 3: U_GU1}.get(stop, U_END)

        @block.scalar
        def _(act):
            steps = [0]

            def step(ins):
                steps[0] += 1
                ins.then_inc(act_step, 1)
                act.wait_ge(act_step, steps[0])

            def split_hi(u, i=0):
                s = u % SLOTS
                n = 4 * (u // 4 + i) + s
                if u >= last_unit:
                    return
                act.wait_ge(raw_loaded[s], 16 * (u // 4 + i) + 16)
                if u >= SLOTS:
                    act.wait_ge(unit_used, n - 3)
                nc.scalar.activation(whi[:, s, :], raw[:, s, :], ACT.Copy).then_inc(hi_done, 1)

            junk_writer = []

            def junk_free(sem_, count):
                if junk_writer:
                    act.wait_ge(*junk_writer.pop())
                junk_writer.append((sem_, count))

            def post_square(m, t):
                n = 4 * m + t
                if t < TT - 1:
                    act.wait_ge(rows_done, 3 * m + t + 1)
                else:
                    act.wait_ge(unit_used, ROWS_END[m])
                junk_free(postsq_done, n + 1)
                nc.scalar.activation(junk[:], ps[:, 2 * t:2 * t + 2, :].rearrange("p b n -> p (b n)"), ACT.Square,
                                     accum_out=stat[:, 0, n:n + 1]).then_inc(postsq_done, 1)

            def pre_square(k, t):
                n = 4 * k + t
                if k == 0:
                    act.wait_ge(x_loaded[t], 16)
                else:
                    act.wait_ge(h_ready, n - 3)
                junk_free(presq_done, n + 1)
                nc.scalar.activation(junk[:], h[:, t, :], ACT.Square,
                                     accum_out=stat[:, 1, n:n + 1]).then_inc(presq_done, 1)

            def pre_hi(k, t):
                n = 4 * k + t
                act.wait_ge(transposed, n + 1)
                nc.scalar.activation(yhi[:, :, t * P:t * P + P],
                                     ps[:, 2 * t:2 * t + 2, :].rearrange("p b (k n) -> p (b k) n", n=P),
                                     ACT.Copy).then_inc(yhi_done, 1)

            def boundary(m, u_next):
                last = m == 3 or m == stop - 1
                for t in range(TT):
                    post_square(m, t)
                    if t == TT - 1 and not last:
                        split_hi(u_next)
                    if not last:
                        pre_square(m + 1, t)
                        if t == TT - 1:
                            split_hi(u_next + 1)
                        pre_hi(m + 1, t)
                if not last:
                    split_hi(u_next + 2)
                    split_hi(u_next + 3)

            for t in range(TT):
                pre_square(0, t)
                if t:
                    pre_hi(0, t - 1)
            split_hi(0)
            pre_hi(0, 3)
            for u in range(1, 4):
                split_hi(u)
            for j in range(4):
                act.wait_ge(unit_used, j + 1)
                nc.scalar.mul(qT[:, j, :], ps[:, j, :], -HEAD_DIM ** -0.5).then_inc(q_out, 1)
                split_hi(j + 4)
            for j in range(2):
                act.wait_ge(unit_used, 4 + j + 1)
                for e in range(2):
                    nc.scalar.copy(ksD[64 * e:64 * e + 64, j, 0, :], ps[0:64, j, :]).then_inc(ka_out, 1)
                split_hi(8 + j)
            act.wait_ge(consts_loaded, 16 * 5)
            nc.scalar.activation(wsmhi[:].rearrange("p k n -> p (k n)"), small["wsm"][:], ACT.Copy).then_inc(wsm_hi, 1)
            for j in range(2):
                act.wait_ge(unit_used, 6 + j + 1)
                nc.scalar.copy(cT[:, j, :], ps[:, 2 + j, :]).then_inc(c_out, 1)
                split_hi(10 + j)
            split_hi(12)
            split_hi(13)
            for j in range(8):
                act.wait_ge(conv_done, j + 1)
                nc.scalar.activation(xbcT[:, j, :], tmp[:, j % 2, :], ACT.Silu).then_inc(xbc_ready, 1)
                split_hi(14 + j)
            for t in range(TT):
                if t == 0:
                    act.wait_ge(unit_used, 22)
                nc.scalar.activation(zN[:, t, :], ps[:, 4 + t, :], ACT.Silu).then_inc(z_ready, 1)
                split_hi(22 + t)
            act.wait_ge(cmp_hid, 1)
            nc.scalar.activation(hidc[:].rearrange("p a b n -> p (a b n)"), ps[:, 1, 0:8 * N_CMP],
                                 ACT.Silu).then_inc(cmp_silu, 1)
            glv = ps[:, 0, 0:128].rearrange("p (t n) -> p t n", t=TT)
            act.wait_ge(small_done, 1)
            nc.scalar.activation(gates[:], glv[:, :, 0:N_GATE], ACT.Exp, scale=-1.0).then_inc(gate_exp, 1)
            act.wait_ge(dt_in, 1)
            nc.scalar.activation(sm[:, 2, :], sm[:, 1, :], ACT.Exp).then_inc(sp_exp, 1)
            nc.scalar.activation(sm[:, 3, 0:8], small["alog"][:], ACT.Exp).then_inc(a_exp, 1)
            act.wait_ge(dt_w, 1)
            nc.scalar.activation(sm[:, 5, :], sm[:, 4, :], ACT.Ln).then_inc(sp_ln, 1)
            act.wait_ge(cums_done, 2)
            nc.scalar.activation(sm[:, 9, :], ps[:, 2, 0:32], ACT.Exp).then_inc(ssm_exp, 1)
            nc.scalar.activation(sm[:, 10, :], ps[:, 2, 32:64], ACT.Exp).then_inc(ssm_exp, 1)
            act.wait_ge(dst_in, 1)
            nc.scalar.activation(sm[:, 11, :], sm[:, 12, :], ACT.Exp).then_inc(ssm_exp, 1)
            for c in range(TT):
                act.wait_ge(xb_tr, c + 1)
                nc.scalar.copy(xN[:, c, :], ps[:, 4 + c % 2, :]).then_inc(xn_out, 1)
            for c in range(TT):
                act.wait_ge(ssm_seg, c + 1)
                act.wait_ge(nacs_done, 1)
                if c:
                    act.wait_ge(m_done, 2 * c)
                for hd in range(HEADS):
                    nc.scalar.activation(dec[:, hd, :], ps[:, hd // 4, (hd % 4) * P:(hd % 4) * P + P], ACT.Exp,
                                         bias=sm[:, 8, 8 * c + hd:8 * c + hd + 1]).then_inc(dec_done, 1)
            for c in range(TT):
                for g in range(2):
                    act.wait_ge(y_gated, 2 * (c + 1))
                    junk_free(ysq_done, 2 * c + g + 1)
                    nc.scalar.activation(junk[:, 0:256], zN[:, c, 256 * g:256 * g + 256], ACT.Square,
                                         accum_out=stat[:, 2, 2 * c + g:2 * c + g + 1]).then_inc(ysq_done, 1)
            for j in range(4):
                act.wait_ge(y_tr, 1)
                nc.scalar.activation(yhi[:, 4 + j, :], ps[:, j, :], ACT.Identity,
                                     scale=small["nw"][:, j:j + 1]).then_inc(mixs_hi, 1)

            widths = [(3, 0), (2, 512), (0, 896), (1, 1024)]

            def exps(j):
                b = j % 2
                for idx, (qt, off) in enumerate(widths):
                    act.wait_ge(biased, 4 * j + idx + 1)
                    w = (qt + 1) * P
                    nc.scalar.activation(prob[:, b, off:off + w], prob[:, b, off:off + w], ACT.Exp,
                                         bias=att[:, b, qt:qt + 1], scale=-1.0,
                                         accum_out=att[:, 2 + b, qt:qt + 1]).then_inc(exp_done, 1)
                if j % 2 == 0:
                    act.wait_ge(cbiased, j // 2 + 1)
                    for qt in range(TT):
                        nc.scalar.activation(pc[:, qt, :], pc[:, qt, :], ACT.Exp, bias=att[:, 4, qt:qt + 1],
                                             scale=-1.0, accum_out=att[:, 5, qt:qt + 1]).then_inc(cexp_done, 1)

            exps(0)
            for j in range(2 * HEADS):
                act.wait_ge(p_tr, j + 1)
                if j >= 2:
                    act.wait_ge(pv_done, j - 1)
                nc.scalar.copy(probT[:, j % 2, 0:512], ps[:, 3, :]).then_inc(pt_act, 1)
                nc.scalar.copy(probT[:, j % 2, 1024:1280], ps[:, 5, 0:256]).then_inc(pt_act, 1)
                if j + 1 < 2 * HEADS:
                    exps(j + 1)
                if j % 4 == 3:
                    act.wait_ge(pv_done, j + 1)
                    nc.scalar.copy(yhi[:, j // 4, :], ps[:, 7, :]).then_inc(mixa_hi, 1)
            for r in range(4):
                split_hi(U_OUT0 + 4 + r)
            boundary(0, U_GU0)

            def ffn(layer, u_gu, u_dn):
                f_base = FT * layer

                def tile(i, e, first):
                    f = 2 * i + e
                    u = u_gu + 2 * e
                    n = 4 * (u // 4) + u % 4
                    act.wait_ge(unit_used, n + 4 * i + 1)
                    if not first:
                        act.wait_ge(mult_done, f_base + f - 1)
                    nc.scalar.activation(tmp[:, e, :], ps[:, 2 * e, :], ACT.Silu).then_inc(silu_done, 1)
                    split_hi(u + 4, i)
                    act.wait_ge(mult_done, f_base + f + 1)
                    nc.scalar.copy(hidhi[:, f, :] if first else hidhi[:, ds(f, 1), :].rearrange("p a n -> p (a n)"),
                                   tmp[:, 2 + e, :]).then_inc(hidhi_done, 1)
                    split_hi(u + 5, i)

                for e in range(2):
                    tile(0, e, True)
                with act.Fori(1, FT // 2) as i:
                    for e in range(2):
                        tile(i, e, False)
                for r in range(2):
                    split_hi(u_dn + 4 + r)
                with act.Fori(0, 3) as i:
                    for j in range(4):
                        split_hi(u_dn + 6 + j, i)
                for r in range(18, FT):
                    split_hi(u_dn + r)

            if stop > 1:
                ffn(0, U_GU0, U_DN0)
                boundary(1, U_V)
            if stop > 2:
                act.wait_ge(ws_tr, 1)
                nc.scalar.copy(wsT[:].rearrange("p g t -> p (g t)"),
                               ps[:, 4:6, :].rearrange("p b n -> p (b n)")).then_inc(ws_out, 1)
                for qr in range(4):
                    for t in range(TT):
                        if t < TT - 1:
                            act.wait_ge(v_done, 3 * qr + t + 1)
                        else:
                            act.wait_ge(unit_used, U_V + 4 * qr + 4)
                        nc.scalar.activation(vG[:, t, 512 * qr:512 * qr + 512], ps[:, 4 * (qr % 2) + t, :],
                                             ACT.Gelu).then_inc(vgelu_done, 1)
                        if t == 3:
                            for j in range(4):
                                split_hi(U_V + 4 * qr + 4 + j)
                for j in range(WT):
                    act.wait_ge(unit_used, U_U + j + 1)
                    if j >= 2:
                        act.wait_ge(g_done, j - 1)
                    nc.scalar.activation(tmp[:, j % 2, :], ps[:, j % 2, :], ACT.Gelu).then_inc(ugelu_done, 1)
                    split_hi(U_U + j + 4)
                    act.wait_ge(g_done, j + 1)
                    nc.scalar.copy(ghi[:, j, :], tmp[:, 2 + j % 2, :]).then_inc(ghi_done, 1)
                for r in range(4, WT):
                    split_hi(U_OUT1 + r)
                boundary(2, U_GU1)
            if stop > 3:
                ffn(1, U_GU1, U_DN1)
                boundary(3, None)

        @block.gpsimd
        def _(pool):
            steps = [0]

            def step(ins):
                steps[0] += 1
                ins.then_inc(pool_step, 1)
                pool.wait_ge(pool_step, steps[0])

            def rstd(dst, src, scale, eps, done):
                step(nc.gpsimd.tensor_scalar(src, src, scale, eps, ALU.mult, ALU.add))
                n = src.shape[-1]
                nc.gpsimd.tensor_tensor(dst, src, half[:, 0:n], ALU.pow).then_inc(done, 1)

            def norms(k, done_sem, row, signal, t):
                n = 4 * k + t
                pool.wait_ge(done_sem, n + 1)
                c = slice(n % 16, n % 16 + 1)
                rstd(rst_t[:, row, c], stat[:, row, c], 1.0 / D_MODEL, RMS_EPS, signal)

            nc.gpsimd.memset(half[:], -0.5)
            nc.gpsimd.memset(ones[:], 1.0)
            step(nc.gpsimd.memset(ident[:], 0.0))
            nc.gpsimd.affine_select(out=ident[:], in_=ident[:], compare_op=ALU.not_equal, fill=1.0, base=0,
                                    pattern=[[-1, P]], channel_multiplier=1).then_inc(consts_made, 1)
            for t in range(TT):
                norms(0, presq_done, 1, prerstd_done, t)
            step(nc.gpsimd.memset(small["mneg"][:], 0.0))
            nc.gpsimd.affine_select(out=small["U"][:], in_=ones[:], compare_op=ALU.is_ge, fill=0.0, base=0,
                                    pattern=[[1, P]], channel_multiplier=-1).then_inc(consts_made, 1)
            nc.gpsimd.affine_select(out=small["mneg"][:], in_=small["mneg"][:], compare_op=ALU.is_ge, fill=-1e30,
                                    base=0, pattern=[[1, P]], channel_multiplier=-1).then_inc(consts_made, 1)
            pool.wait_ge(cmp_hid, 1)
            d0 = bias[:, HEADS - 1, :]
            step(nc.gpsimd.iota(d0, pattern=[[-1, SEQ]], base=SEQ - P, channel_multiplier=1,
                                allow_small_or_imprecise_dtypes=True))
            step(nc.gpsimd.affine_select(out=d0, in_=d0, compare_op=ALU.is_ge, fill=MASKED, base=SEQ - P,
                                         pattern=[[-1, SEQ]], channel_multiplier=1))
            for hd in range(HEADS):
                nc.gpsimd.tensor_scalar(bias[:, hd, :], d0, 2.0 ** -(hd + 1), None, ALU.mult).then_inc(bias_done, 1)
            step(nc.gpsimd.iota(dcmp[:], pattern=[[P, TT], [-CMP_STRIDE, N_CMP]], base=-(CMP_BLOCK - 1),
                                channel_multiplier=1, allow_small_or_imprecise_dtypes=True))
            nc.gpsimd.affine_select(out=dcmp[:], in_=dcmp[:], compare_op=ALU.is_ge, fill=MASKED,
                                    base=-(CMP_BLOCK - 1), pattern=[[P, TT], [-CMP_STRIDE, N_CMP]],
                                    channel_multiplier=1).then_inc(bias_done, 1)
            for c in range(TT):
                for g in range(2):
                    n = 2 * c + g
                    pool.wait_ge(ysq_done, n + 1)
                    rstd(rst_t[:, 2, n:n + 1], stat[:, 2, n:n + 1], 1.0 / 256, RMS_EPS, yr_done)

            def boundary(m):
                for t in range(TT):
                    norms(m, postsq_done, 0, postrstd_done, t)
                    if m < 3 and m != stop - 1:
                        norms(m + 1, presq_done, 1, prerstd_done, t)

            def stage(kt, slot, hi, lo, done_need, u_prev, i, n_staged):
                pool.wait_ge(unit_used, 4 * (u_prev // 4 + i) + u_prev % 4 + 1)
                nc.gpsimd.tensor_copy(yhi[:, slot, :], hi[:, ds(kt, 1), :].rearrange("p a n -> p (a n)")).then_inc(staged, 1)
                nc.gpsimd.tensor_copy(ylo[:, slot, :], lo[:, ds(kt, 1), :].rearrange("p a n -> p (a n)")).then_inc(staged, 1)

            def ffn_stage(layer, u_dn):
                pool.wait_ge(hidlo_done, FT * (layer + 1))
                with pool.Fori(0, 4) as i:
                    for j in range(4):
                        stage(4 * i + 2 + j, j % 2, hidhi, hidlo, None, u_dn + j, i, None)

            boundary(0)
            if stop > 1:
                ffn_stage(0, U_DN0)
                boundary(1)
            if stop > 2:
                pool.wait_ge(gmlp_loaded, 16 * 10)
                nc.gpsimd.affine_select(out=ws[:], in_=ws[:], compare_op=ALU.is_ge, fill=0.0, base=0,
                                        pattern=[[0, 8], [-1, P]], channel_multiplier=1).then_inc(ws_masked, 1)
                for t in range(TT):
                    pool.wait_ge(vmv_done, t + 1)
                    rstd(vmv[:, t, 2:3], vmv[:, t, 1:2], 1.0, LN_EPS, vrstd_done)
                pool.wait_ge(glo_done, WT)
                with pool.Fori(0, 2) as i:
                    for j in range(4):
                        stage(4 * i + 4 + j, j % 2, ghi, glo, None, U_OUT1 + 2 + j, i, None)
                boundary(2)
            if stop > 3:
                ffn_stage(1, U_DN1)
                boundary(3)

        @block.vector
        def _(dve):
            V = nc.vector
            steps = [0]

            def step(ins):
                steps[0] += 1
                ins.then_inc(dve_step, 1)
                dve.wait_ge(dve_step, steps[0])

            def split_lo(u, i=0):
                s = u % SLOTS
                if u >= last_unit:
                    return
                dve.wait_ge(hi_done, 4 * (u // 4 + i) + s + 1)
                V.tensor_tensor(wlo[:, s, :], raw[:, s, :], whi[:, s, :].bitcast(f32), ALU.subtract).then_inc(lo_done, 1)

            def post_residual(m, t):
                n = 4 * m + t
                dve.wait_ge(postrstd_done, n + 1)
                if t == 0:
                    dve.wait_ge(gain_post_loaded, 16 * (m + 1))
                if n:
                    dve.wait_ge(h_ready, n)
                y = ps[:, 2 * t:2 * t + 2, :].rearrange("p b n -> p (b n)")
                V.scalar_tensor_tensor(tmp_a[:], y, rst_t[:, 0, n:n + 1], gain_post[:], ALU.mult,
                                       ALU.mult).then_inc(scaled_done, 1)
                dve.wait_ge(scaled_done, n + 1)
                V.tensor_tensor(h[:, t, :], h[:, t, :], tmp_a[:], ALU.add).then_inc(h_ready, 1)

            def pre_scale(k, t):
                n = 4 * k + t
                dve.wait_ge(prerstd_done, n + 1)
                if t == 0:
                    dve.wait_ge(gain_pre_loaded, 16 * (k + 1))
                if n:
                    dve.wait_ge(transposed, n)
                V.scalar_tensor_tensor(tmp_b[:], h[:, t, :], rst_t[:, 1, n:n + 1], gain_pre[:], ALU.mult,
                                       ALU.mult).then_inc(hn_done, 1)

            def pre_lo(k, t):
                n = 4 * k + t
                dve.wait_ge(yhi_done, n + 1)
                sl = slice(t * P, t * P + P)
                V.tensor_tensor(ylo[:, :, sl], ps[:, 2 * t:2 * t + 2, :].rearrange("p b (k n) -> p (b k) n", n=P),
                                yhi[:, :, sl].bitcast(f32), ALU.subtract).then_inc(ylo_done, 1)

            def boundary(m, u_next):
                last = m == 3 or m == stop - 1
                for t in range(TT):
                    post_residual(m, t)
                    if last:
                        continue
                    if t == TT - 1:
                        split_lo(u_next)
                    pre_scale(m + 1, t)
                    if t == TT - 1:
                        split_lo(u_next + 1)
                    pre_lo(m + 1, t)
                if not last:
                    split_lo(u_next + 2)
                    split_lo(u_next + 3)

            for t in range(TT):
                pre_scale(0, t)
                if t == 3:
                    split_lo(0)
                pre_lo(0, t)
            for u in range(1, 4):
                split_lo(u)
            for u in range(4, 8):
                split_lo(u)
            for j in range(2):
                dve.wait_ge(unit_used, 4 + j + 1)
                for e in range(2):
                    V.tensor_copy(ksD[64 * e:64 * e + 64, j, 1, :], ps[64:128, j, :]).then_inc(kd_out, 1)
                split_lo(8 + j)
            dve.wait_ge(wsm_hi, 1)
            V.tensor_tensor(wsmlo[:].rearrange("p k n -> p (k n)"), small["wsm"][:],
                            wsmhi[:].rearrange("p k n -> p (k n)").bitcast(f32), ALU.subtract).then_inc(wsm_lo, 1)
            split_lo(10)
            split_lo(11)
            dve.wait_ge(unit_used, 10)
            for t in range(TT):
                V.tensor_copy(vN[:, t, :], ps[:, 4 + t, 0:256]).then_inc(v_out, 1)
            split_lo(12)
            split_lo(13)
            cwv = small["cw"].rearrange("p (k c) -> p k c", k=CONV_TAPS)
            for j in range(8):
                dve.wait_ge(unit_used, 10 + j + 1)
                if j >= 2:
                    dve.wait_ge(xbc_ready, j - 1)
                src, acc = ps[:, j % 4, :], tmp[:, j % 2, :]
                step(V.tensor_scalar(acc, src, cwv[:, 3, j:j + 1], small["cb"][:, j:j + 1], ALU.mult, ALU.add))
                for lag in (1, 2, 3):
                    ins = V.scalar_tensor_tensor(acc[:, lag:], src[:, 0:SEQ - lag], cwv[:, 3 - lag, j:j + 1],
                                                 acc[:, lag:], ALU.mult, ALU.add)
                    if lag < 3:
                        step(ins)
                    else:
                        ins.then_inc(conv_done, 1)
                split_lo(14 + j)
            dve.wait_ge(c_out, 2)
            dve.wait_ge(cmp_loaded, 16 * 3)
            for y in range(2):
                for g in range(2):
                    src = cT[64 * g:64 * g + 64, y, :].rearrange("p (b r) -> p r b", r=16)
                    pe3 = small["pe2"][64 * g:64 * g + 64, 32 * y:32 * y + 32]
                    for par in range(2):
                        for w in range(2):
                            pv = pe3[:, 16 * w + par:16 * w + 16:2].unsqueeze(2).broadcast_to([64, 8, N_CMP])
                            V.tensor_tensor(
                                blk[64 * par:64 * par + 64, y, 8 * w:8 * w + 8, N_CMP * g:N_CMP * g + N_CMP],
                                src[:, par::2, w:w + N_CMP], pv, ALU.add).then_inc(blk_done, 1)
            for t in range(4):
                split_lo(22 + t)
            dve.wait_ge(cmp_kv, 1)
            V.tensor_copy(kcb[:].rearrange("p g c -> p (g c)"), ps[:, 2, 0:2 * N_CMP])
            V.tensor_copy(vcb[0:N_CMP].rearrange("p g d -> p (g d)"), ps[0:N_CMP, 2, 128:256]).then_inc(cmp_out, 1)

            dve.wait_ge(small_done, 1)
            dve.wait_ge(consts_loaded, 16 * 5)
            dtp = ps[:, 0, 0:128].rearrange("p (t n) -> p t n", t=TT)[:, :, N_GATE:32]

            def smv(k):
                return sm[:, k, :].rearrange("p (t n) -> p t n", t=TT)

            def rowbc(ap):
                return ap.unsqueeze(1).broadcast_to([P, TT, HEADS])

            dve.wait_ge(gate_exp, 1)
            step(V.tensor_tensor(smv(0), dtp, rowbc(small["dtb"][:]), ALU.add))
            step(V.tensor_scalar(sm[:, 1, :], sm[:, 0, :], -1.0, None, ALU.mult))
            V.tensor_tensor(sm[:, 1, :], sm[:, 1, :], sm[:, 0, :], ALU.min).then_inc(dt_in, 1)
            dve.wait_ge(gate_exp, 1)
            gflat = gates[:].rearrange("p t n -> p (t n)")
            step(V.tensor_scalar(gflat, gflat, 1.0, None, ALU.add))
            V.reciprocal(gflat, gflat)
            dve.wait_ge(sp_exp, 1)
            V.tensor_scalar(sm[:, 4, :], sm[:, 2, :], 1.0, None, ALU.add).then_inc(dt_w, 1)
            dve.wait_ge(dt_w, 1)
            step(V.tensor_scalar(sm[:, 6, :], sm[:, 4, :], -1.0, 1e-30, ALU.add, ALU.add))
            step(V.reciprocal(sm[:, 6, :], sm[:, 6, :]))
            step(V.tensor_tensor(sm[:, 6, :], sm[:, 6, :], sm[:, 2, :], ALU.mult))
            dve.wait_ge(sp_ln, 1)
            step(V.scalar_tensor_tensor(sm[:, 6, :], sm[:, 5, :], 1e-30, sm[:, 6, :], ALU.add, ALU.mult))
            step(V.scalar_tensor_tensor(sm[:, 7, :], sm[:, 0, :], 0.0, sm[:, 6, :], ALU.max, ALU.add))
            dve.wait_ge(a_exp, 1)
            step(V.tensor_scalar(sm[:, 3, 0:8], sm[:, 3, 0:8], -1.0, None, ALU.mult))
            V.tensor_tensor(smv(13), smv(7), rowbc(sm[:, 3, 0:8]), ALU.mult).then_inc(da_done, 1)
            dve.wait_ge(cums_done, 2)
            dve.wait_ge(ssm_exp, 2)
            step(V.tensor_scalar(sm[:, 8, :], ps[:, 2, 0:32], -1.0, None, ALU.mult))
            V.tensor_copy(sm[:, 14, :], sm[:, 8, :]).then_inc(nacs_done, 1)
            V.tensor_tensor(sm[:, 12, :], sm[:, 8, :], ps[:, 2, 32:64], ALU.add).then_inc(dst_in, 1)
            for c in range(TT):
                dve.wait_ge(xb_tr, c + 1)
                V.tensor_copy(BN[:, c, :], ps[:, 6 + c % 2, 0:256]).then_inc(bn_out, 1)
            dve.wait_ge(ssm_exp, 3)
            step(V.memset(prev[:], 0.0))

            def heads3(ap):
                return ap.rearrange("p (h d) -> p h d", h=HEADS)

            def colbc(k, c):
                return sm[:, k, 8 * c:8 * c + 8].unsqueeze(2).broadcast_to([P, HEADS, HEAD_DIM])

            for c in range(TT):
                if c == 0:
                    dve.wait_ge(xn_out, TT)
                if c:
                    dve.wait_ge(ssm_mm, c)
                step(V.tensor_tensor(heads3(xdt[:]), heads3(xN[:, c, :]), colbc(7, c), ALU.mult))
                V.tensor_tensor(heads3(xdd[:]), heads3(xdt[:]), colbc(11, c), ALU.mult).then_inc(xd_done, 1)
                dve.wait_ge(dec_done, 8 * (c + 1))
                for g in range(2):
                    cb = ps[:, 2, 256 + P * g:256 + P * g + P].unsqueeze(1).broadcast_to([P, 4, P])
                    V.tensor_tensor(Mt[:, 4 * g:4 * g + 4, :], dec[:, 4 * g:4 * g + 4, :], cb,
                                    ALU.mult).then_inc(m_done, 1)
                dve.wait_ge(ssm_mm, c + 1)
                t1, t2 = tmp[:, 0, :], tmp[:, 1, :]
                step(V.tensor_tensor(heads3(t1), heads3(ps[:, 4, :]), colbc(9, c), ALU.mult))
                step(V.tensor_tensor(t1, t1, ps[:, 3, :], ALU.add))
                step(V.tensor_tensor(heads3(t2), heads3(xN[:, c, :]),
                                     small["dsk"][:].unsqueeze(2).broadcast_to([P, HEADS, HEAD_DIM]), ALU.mult))
                step(V.tensor_tensor(t1, t1, t2, ALU.add))
                if c == 0:
                    dve.wait_ge(z_ready, TT)
                V.tensor_tensor(zN[:, c, :], zN[:, c, :], t1, ALU.mult).then_inc(y_gated, 1)
                step(V.tensor_tensor(heads3(prev[:]), heads3(prev[:]), colbc(10, c), ALU.mult))
                V.tensor_tensor(prev[:], prev[:], ps[:, 5, :], ALU.add).then_inc(y_gated, 1)
                dve.wait_ge(y_gated, 2 * (c + 1))
            for c in range(TT):
                for g in range(2):
                    dve.wait_ge(yr_done, 2 * c + g + 1)
                    seg = zN[:, c, 256 * g:256 * g + 256]
                    V.tensor_scalar(seg, seg, rst_t[:, 2, 2 * c + g:2 * c + g + 1], None, ALU.mult).then_inc(yn_done, 1)
            for j in range(4):
                dve.wait_ge(mixs_hi, j + 1)
                V.scalar_tensor_tensor(ylo[:, 4 + j, :], ps[:, j, :], small["nw"][:, j:j + 1],
                                       yhi[:, 4 + j, :].bitcast(f32), ALU.mult, ALU.subtract).then_inc(mixs_lo, 1)

            widths = [(3, 0), (2, 512), (0, 896), (1, 1024)]
            where = {3: (0, 0), 2: (1, 0), 0: (1, 384), 1: (2, 0)}

            def add_bias(j):
                hd, b = j // 2, j % 2
                dve.wait_ge(qk_done, j + 1)
                if j == 0:
                    dve.wait_ge(bias_done, HEADS + 1)
                if j >= 2:
                    dve.wait_ge(p_tr, j - 1)
                for qt, off in widths:
                    bk, c0 = where[qt]
                    w = (qt + 1) * P
                    V.tensor_tensor_reduce(out=prob[:, b, off:off + w], in0=ps[:, bk, c0:c0 + w],
                                           in1=bias[:, hd, SEQ - w:SEQ], scale=1.0, scalar=3e38, op0=ALU.add,
                                           op1=ALU.min, accum_out=att[:, b, qt:qt + 1]).then_inc(biased, 1)
                if b == 0:
                    sc = ps[:, 2, 256:256 + TT * N_CMP].rearrange("p (t c) -> p t c", t=TT)
                    step(V.scalar_tensor_tensor(pc[:].rearrange("p t c -> p (t c)"),
                                                dcmp[:].rearrange("p t c -> p (t c)"), 2.0 ** -(hd + 1),
                                                sc.rearrange("p t c -> p (t c)"), ALU.mult, ALU.add))
                    step(V.tensor_reduce(out=att[:, 4, 0:4], in_=pc[:], op=ALU.min, axis=AX.X))
                    V.tensor_scalar(att[:, 4, 0:4], att[:, 4, 0:4], FLOOR, None, ALU.min).then_inc(cbiased, 1)

            gT = gates[:].rearrange("p t n -> p n t")
            add_bias(0)
            for j in range(2 * HEADS):
                hd, b = j // 2, j % 2
                dve.wait_ge(exp_done, 4 * (j + 1))
                step(V.reciprocal(att[:, 6, 0:4], att[:, 2 + b, 0:4]))
                step(V.tensor_tensor(att[:, 6, 0:4], att[:, 6, 0:4], gT[:, 3 * hd + 1 + b, :], ALU.mult))
                for qt, off in widths:
                    w = (qt + 1) * P
                    V.tensor_scalar(prob[:, b, off:off + w], prob[:, b, off:off + w], att[:, 6, qt:qt + 1], None,
                                    ALU.mult).then_inc(scaled, 1)
                if b == 0:
                    dve.wait_ge(cexp_done, 4 * (hd + 1))
                    step(V.tensor_scalar(att[:, 7, 0:4], att[:, 5, 0:4], 1e-30, None, ALU.max))
                    step(V.reciprocal(att[:, 7, 0:4], att[:, 7, 0:4]))
                    step(V.tensor_tensor(att[:, 7, 0:4], att[:, 7, 0:4], gT[:, 3 * hd, :], ALU.mult))
                    V.tensor_tensor(pc[:], pc[:], att[:, 7, 0:4].unsqueeze(2).broadcast_to([P, TT, N_CMP]),
                                    ALU.mult)
                    dve_last = None
                V.tensor_copy(att[:, 6, 4:5], att[:, 6, 0:1]).then_inc(scaled, 1)
                if j + 1 < 2 * HEADS and not (b == 1):
                    add_bias(j + 1)
                elif j + 1 < 2 * HEADS:
                    dve.wait_ge(p_tr, j)
                    add_bias(j + 1)
                dve.wait_ge(p_tr, j + 1)
                if j >= 2:
                    dve.wait_ge(pv_done, j - 1)
                V.tensor_copy(probT[:, b, 512:1024], ps[:, 4, :]).then_inc(pt_dve, 1)
                if b == 0:
                    V.tensor_copy(pcT[0:N_CMP, :], ps[0:N_CMP, 6, :]).then_inc(pt_dve, 1)
                if j % 4 == 3:
                    dve.wait_ge(mixa_hi, j // 4 + 1)
                    V.tensor_tensor(ylo[:, j // 4, :], ps[:, 7, :], yhi[:, j // 4, :].bitcast(f32),
                                    ALU.subtract).then_inc(mixa_lo, 1)
            for r in range(4):
                split_lo(U_OUT0 + 4 + r)
            boundary(0, U_GU0)

            def ffn(layer, u_gu, u_dn):
                f_base = FT * layer

                def tile(i, e, first):
                    f = 2 * i + e
                    u = u_gu + 2 * e
                    dve.wait_ge(unit_used, 4 * ((u + 1) // 4) + (u + 1) % 4 + 4 * i + 1)
                    dve.wait_ge(silu_done, f_base + f + 1)
                    if not first:
                        dve.wait_ge(hidlo_done, f_base + f - 1)
                    V.tensor_tensor(tmp[:, 2 + e, :], tmp[:, e, :], ps[:, 2 * e + 1, :], ALU.mult).then_inc(mult_done, 1)
                    split_lo(u + 4, i)
                    dve.wait_ge(hidhi_done, f_base + f + 1)
                    row = lambda tl: tl[:, f, :] if first else tl[:, ds(f, 1), :].rearrange("p a n -> p (a n)")
                    V.tensor_tensor(row(hidlo), tmp[:, 2 + e, :], row(hidhi).bitcast(f32),
                                    ALU.subtract).then_inc(hidlo_done, 1)
                    split_lo(u + 5, i)

                for e in range(2):
                    tile(0, e, True)
                with dve.Fori(1, FT // 2) as i:
                    for e in range(2):
                        tile(i, e, False)
                for r in range(2):
                    split_lo(u_dn + 4 + r)
                with dve.Fori(0, 3) as i:
                    for j in range(4):
                        split_lo(u_dn + 6 + j, i)
                for r in range(18, FT):
                    split_lo(u_dn + r)

            if stop > 1:
                ffn(0, U_GU0, U_DN0)
                boundary(1, U_V)
            if stop > 2:
                for j in range(WT):
                    g = j // 2
                    if j == 0:
                        dve.wait_ge(rowsum_done, 1)
                    V.scalar_tensor_tensor(Rt[:, j, :], ps[:, 6 + g // 4, (g % 4) * P:(g % 4) * P + P],
                                           lnb[:, j:j + 1], bsbc[:, g, :], ALU.mult, ALU.add).then_inc(r_done, 1)
                for qr in range(4):
                    for t in range(TT):
                        dve.wait_ge(vgelu_done, 4 * qr + t + 1)
                        V.bn_stats(vstat[:, t, qr, :], vG[:, t, 512 * qr:512 * qr + 512]).then_inc(dve_step, 1)
                        steps[0] += 1
                    for j in range(4):
                        if qr < 3:
                            split_lo(U_V + 4 * qr + 4 + j)
                for t in range(TT):
                    if t == 0:
                        dve.wait_ge(dve_step, steps[0])
                    V.bn_aggr(vmv[:, t, 0:2], vstat[:, t].rearrange("p a b -> p (a b)")).then_inc(vmv_done, 1)
                split_lo(U_U)
                for t in range(TT):
                    dve.wait_ge(vrstd_done, t + 1)
                    V.tensor_scalar(vG[:, t, :], vG[:, t, :], vmv[:, t, 0:1], vmv[:, t, 2:3], ALU.subtract,
                                    ALU.mult).then_inc(vnorm_done, 1)
                for j in range(1, 4):
                    split_lo(U_U + j)
                for j in range(WT):
                    dve.wait_ge(mix_mm, j + 1)
                    if j == 0:
                        dve.wait_ge(r_done, WT)
                    V.scalar_tensor_tensor(mixed[:, j, :].rearrange("p (c n) -> p c n", c=TT),
                                           ps[:, 2 + j % 4, :].rearrange("p (c n) -> p c n", c=TT), lnw[:, j:j + 1],
                                           Rt[:, j, :].unsqueeze(1).broadcast_to([P, TT, P]), ALU.mult,
                                           ALU.add).then_inc(mixed_done, 1)
                dve.wait_ge(mixed_done, WT)
                for j in range(WT):
                    dve.wait_ge(ugelu_done, j + 1)
                    if j >= 2:
                        dve.wait_ge(glo_done, j - 1)
                    V.tensor_tensor(tmp[:, 2 + j % 2, :], tmp[:, j % 2, :], mixed[:, j, :], ALU.mult).then_inc(g_done, 1)
                    split_lo(U_U + j + 4)
                    dve.wait_ge(ghi_done, j + 1)
                    V.tensor_tensor(glo[:, j, :], tmp[:, 2 + j % 2, :], ghi[:, j, :].bitcast(f32),
                                    ALU.subtract).then_inc(glo_done, 1)
                for r in range(4, WT):
                    split_lo(U_OUT1 + r)
                boundary(2, U_GU1)
            if stop > 3:
                ffn(1, U_GU1, U_DN1)
                boundary(3, None)

        @block.tensor
        def _(pe):
            T = nc.tensor

            def ready(u, i=0):
                pe.wait_ge(lo_done, 4 * (u // 4 + i) + u % 4 + 1)

            def col_unit(u, bank, i=0):
                s = u % SLOTS
                ready(u, i)
                for k in range(KT):
                    hi, lo = whi[:, s, k * P:k * P + P], wlo[:, s, k * P:k * P + P]
                    T.matmul(ps[:, bank, :], hi, yhi[:, k, :], start=(k == 0), stop=False)
                    T.matmul(ps[:, bank, :], hi, ylo[:, k, :], start=False, stop=False)
                    last = T.matmul(ps[:, bank, :], lo, yhi[:, k, :], start=False, stop=(k == KT - 1))
                return last

            def row_products(s, t, hi, lo, first, last_k):
                for hf in range(2):
                    o = ps[:, 2 * t + hf, :]
                    c = slice(512 * hf, 512 * hf + 512)
                    T.matmul(o, hi[:, t * P:t * P + P], whi[:, s, c], start=first, stop=False)
                    T.matmul(o, hi[:, t * P:t * P + P], wlo[:, s, c], start=False, stop=False)
                    last = T.matmul(o, lo[:, t * P:t * P + P], whi[:, s, c], start=False, stop=last_k)
                return last

            def rows(m, u0, n, hi, lo, peel, free=None, staged_base=0):
                for r in range(peel):
                    ready(u0 + r)
                    for q, t in enumerate((2, 3, 0, 1)):
                        if r == 0 and free and q in free:
                            free[q]()
                        last = row_products((u0 + r) % SLOTS, t, hi[:, r, :], lo[:, r, :], r == 0, False)
                    last.then_inc(unit_used, 1)
                loops = (n - peel - TAIL) // 4
                if loops:
                    with pe.Fori(0, loops) as i:
                        for j in range(4):
                            u = u0 + peel + j
                            pe.wait_ge(staged, staged_base + 8 * i + 2 * (j + 1))
                            ready(u, i)
                            for t in range(TT):
                                last = row_products(u % SLOTS, t, yhi[:, j % 2, :], ylo[:, j % 2, :], False, False)
                            last.then_inc(unit_used, 1)
                for r in range(n - TAIL, n):
                    ready(u0 + r)
                for t in range(TT):
                    for r in range(n - TAIL, n):
                        last = row_products((u0 + r) % SLOTS, t, hi[:, r, :], lo[:, r, :], peel == 0 and r == n - TAIL,
                                            r == n - 1)
                        if r == n - 1 and t < TT - 1:
                            last.then_inc(rows_done, 1)
                        if t == TT - 1:
                            last.then_inc(unit_used, 1)

            def pre_transposes(k):
                for t in range(TT):
                    n = 4 * k + t
                    pe.wait_ge(hn_done, n + 1)
                    for kk in range(KT):
                        last = T.transpose(ps[:, 2 * t + kk // 4, (kk % 4) * P:(kk % 4) * P + P],
                                           tmp_b[:, kk * P:kk * P + P], ident[:])
                    last.then_inc(transposed, 1)
                pe.wait_ge(ylo_done, 4 * (k + 1))

            pe.wait_ge(consts_made, 1)
            pre_transposes(0)
            for u in range(8):
                if u == 4:
                    pe.wait_ge(q_out, 1)
                if u >= 5:
                    pe.wait_ge(q_out, u - 3)
                col_unit(u, u % 4).then_inc(unit_used, 1)
            for u in (8, 9):
                ready(u)
                s = u % SLOTS
                for t in range(TT):
                    for k in range(4):
                        kk = 4 * (u - 8) + k
                        c = slice(256 * k, 256 * k + 256)
                        yh, yl = yhi[:, kk, t * P:t * P + P], ylo[:, kk, t * P:t * P + P]
                        o = ps[:, 4 + t, 0:256]
                        T.matmul(o, yh, whi[:, s, c], start=(kk == 0), stop=False)
                        T.matmul(o, yh, wlo[:, s, c], start=False, stop=False)
                        last = T.matmul(o, yl, whi[:, s, c], start=False, stop=(kk == KT - 1))
                last.then_inc(unit_used, 1)
            for j in range(8):
                if j < 2:
                    pe.wait_ge(ka_out, 2 * (j + 1))
                    pe.wait_ge(kd_out, 2 * (j + 1))
                elif j < 4:
                    pe.wait_ge(c_out, j - 1)
                else:
                    pe.wait_ge(conv_done, j - 3)
                col_unit(10 + j, j % 4).then_inc(unit_used, 1)
            for u in range(18, 22):
                ready(u)
                s = u % SLOTS
                for t in range(TT):
                    if u == 18:
                        pe.wait_ge(v_out, t + 1)
                    for b in range(2):
                        kk = 2 * (u - 18) + b
                        c = slice(512 * b, 512 * b + 512)
                        yh, yl = yhi[:, kk, t * P:t * P + P], ylo[:, kk, t * P:t * P + P]
                        T.matmul(ps[:, 4 + t, :], yh, whi[:, s, c], start=(kk == 0), stop=False)
                        T.matmul(ps[:, 4 + t, :], yh, wlo[:, s, c], start=False, stop=False)
                        last = T.matmul(ps[:, 4 + t, :], yl, whi[:, s, c], start=False, stop=(kk == KT - 1))
                last.then_inc(unit_used, 1)
            pe.wait_ge(wsm_lo, 1)
            pe.wait_ge(conv_done, 5)
            for t in range(TT):
                o = ps[:, 0, 32 * t:32 * t + 32]
                for kk in range(KT):
                    yh, yl = yhi[:, kk, t * P:t * P + P], ylo[:, kk, t * P:t * P + P]
                    T.matmul(o, yh, wsmhi[:, kk, :], start=(kk == 0), stop=False)
                    T.matmul(o, yh, wsmlo[:, kk, :], start=False, stop=False)
                    last = T.matmul(o, yl, wsmhi[:, kk, :], start=False, stop=(kk == KT - 1))
            last.then_inc(small_done, 1)
            pe.wait_ge(blk_done, 16)
            pe.wait_ge(conv_done, 6)
            for y, w1t in ((0, w1k), (1, w1v)):
                for ht in range(2):
                    c0 = (2 * y + ht) * 2 * N_CMP
                    for pr in range(16):
                        last = T.matmul(ps[:, 1, c0:c0 + 2 * N_CMP], w1t[:, pr, ht * P:ht * P + P], blk[:, y, pr, :],
                                        start=(pr == 0), stop=(pr == 15))
            last.then_inc(cmp_hid, 1)
            pe.wait_ge(conv_done, 7)
            pe.wait_ge(cmp_silu, 1)
            for e in range(2):
                for ht in range(2):
                    T.matmul(ps[64 * e:64 * e + 64, 2, 0:2 * N_CMP], w2s[:, 0, ht, :], hidc[:, 0, ht, :],
                             start=(ht == 0), stop=(ht == 1))
            for g in range(2):
                for ht in range(2):
                    last = T.matmul(ps[0:N_CMP, 2, 128 + 64 * g:192 + 64 * g],
                                    hidc[:, 1, ht, N_CMP * g:N_CMP * g + N_CMP], w2s[:, 1, ht, :],
                                    start=(ht == 0), stop=(ht == 1))
            last.then_inc(cmp_kv, 1)
            pe.wait_ge(cmp_out, 1)
            pe.wait_ge(da_done, 1)
            pe.wait_ge(consts_made, 3)
            T.matmul(ps[:, 2, 0:32], small["U"][:], sm[:, 13, :], start=True, stop=True).then_inc(cums_done, 1)
            T.matmul(ps[:, 2, 32:64], ones[:], sm[:, 13, :], start=True, stop=True).then_inc(cums_done, 1)
            pe.wait_ge(z_ready, 4)
            pe.wait_ge(xbc_ready, 8)
            for c in range(TT):
                if c >= 2:
                    pe.wait_ge(xn_out, c - 1)
                    pe.wait_ge(bn_out, c - 1)
                for j in range(4):
                    T.transpose(ps[:, 4 + c % 2, j * P:j * P + P], xbcT[:, j, c * P:c * P + P], ident[:])
                for g in range(2):
                    last = T.transpose(ps[:, 6 + c % 2, g * P:g * P + P], xbcT[:, 4 + g, c * P:c * P + P], ident[:])
                last.then_inc(xb_tr, 1)
            av = sm[:, 13, :]
            pe.wait_ge(dst_in, 1)
            pe.wait_ge(ssm_exp, 2)
            pe.wait_ge(gate_exp, 1)
            for c in range(TT):
                tok = slice(c * P, c * P + P)
                if c:
                    pe.wait_ge(dec_done, 8 * c)
                    pe.wait_ge(m_done, 2 * c)
                for g in range(2):
                    for q in range(4):
                        o = ps[:, g, q * P:q * P + P]
                        T.matmul(o, ident[:], small["mneg"][:], start=True, stop=False)
                        last = T.matmul(o, av[:, 8 * c + 4 * g + q:8 * c + 4 * g + q + 1].broadcast_to([P, P]),
                                        small["U"][:], start=False, stop=True)
                for g in range(2):
                    last = T.matmul(ps[:, 2, 256 + P * g:256 + P * g + P], xbcT[:, 4 + g, tok], xbcT[:, 6 + g, tok],
                                    start=True, stop=True)
                last.then_inc(ssm_seg, 1)
                if c == 0:
                    pe.wait_ge(xn_out, TT)
                    pe.wait_ge(bn_out, TT)
                pe.wait_ge(xd_done, c + 1)
                if c:
                    pe.wait_ge(y_gated, 2 * c)
                for g in range(2):
                    T.matmul(ps[:, 4, 256 * g:256 * g + 256], xbcT[:, 6 + g, tok], prev[:, 256 * g:256 * g + 256],
                             start=True, stop=True)
                    T.matmul(ps[:, 5, 256 * g:256 * g + 256], BN[:, c, P * g:P * g + P],
                             xdd[:, 256 * g:256 * g + 256], start=True, stop=True)
                pe.wait_ge(m_done, 2 * (c + 1))
                for hd in range(HEADS):
                    last = T.matmul(ps[:, 3, 64 * hd:64 * hd + 64], Mt[:, hd, :], xdt[:, 64 * hd:64 * hd + 64],
                                    start=True, stop=True)
                last.then_inc(ssm_mm, 1)
            pe.wait_ge(yn_done, 8)
            for j in range(4):
                for c in range(TT):
                    last = T.transpose(ps[:, j, c * P:c * P + P], zN[:, c, j * P:j * P + P], ident[:])
            last.then_inc(y_tr, 1)
            pe.wait_ge(mixs_lo, 4)

            widths = [(3, 0), (2, 512), (0, 896), (1, 1024)]
            where = {3: (0, 0), 2: (1, 0), 0: (1, 384), 1: (2, 0)}
            p_off = dict(widths)
            tr = {0: (3, 0, 0), 1: (4, 0, 512), 3: (4, 384, 896), 2: (5, 0, 1024)}

            def scores(j):
                hd, kind = j // 2, j % 2
                e, g = hd % 2, hd // 4
                rws = slice(64 * e, 64 * e + 64)
                if j:
                    pe.wait_ge(biased, 4 * j)
                    pe.wait_ge(cbiased, (j + 1) // 2)
                for qt, _ in widths:
                    bk, c0 = where[qt]
                    w = (qt + 1) * P
                    last = T.matmul(ps[:, bk, c0:c0 + w], qT[rws, hd // 2, qt * P:qt * P + P],
                                    ksD[rws, kind, g, 0:w], start=True, stop=True)
                if kind == 0:
                    for qt in range(TT):
                        last = T.matmul(ps[:, 2, 256 + N_CMP * qt:256 + N_CMP * (qt + 1)],
                                        qT[rws, hd // 2, qt * P:qt * P + P], kcb[rws, g, :], start=True, stop=True)
                last.then_inc(qk_done, 1)

            scores(0)
            for j in range(2 * HEADS):
                hd, b = j // 2, j % 2
                e, g = hd % 2, hd // 4
                if j + 1 < 2 * HEADS:
                    scores(j + 1)
                pe.wait_ge(scaled, 5 * (j + 1))
                if j:
                    pe.wait_ge(pt_act, 2 * j)
                    pe.wait_ge(pt_dve, (3 * j + 1) // 2)
                for kt in range(TT):
                    bk, c0, _ = tr[kt]
                    for qt in range(kt, TT):
                        last = T.transpose(ps[:, bk, c0 + (qt - kt) * P:c0 + (qt - kt) * P + P],
                                           prob[:, b, p_off[qt] + kt * P:p_off[qt] + kt * P + P], ident[:])
                if b == 0:
                    for qt in range(TT):
                        last = T.transpose(ps[0:N_CMP, 6, qt * P:qt * P + P], pc[:, qt, :], ident[:])
                last.then_inc(p_tr, 1)
                pe.wait_ge(pt_act, 2 * (j + 1))
                pe.wait_ge(pt_dve, (3 * (j + 1) + 1) // 2)
                if j % 4 == 0 and j:
                    pe.wait_ge(mixa_lo, j // 4)
                o = slice(64 * e, 64 * e + 64)
                for kt in (range(TT) if b == 0 else reversed(range(TT))):
                    c0 = tr[kt][2]
                    w = SEQ - kt * P
                    last = T.matmul(ps[o, 7, kt * P:SEQ], vN[:, kt, P * b + 64 * g:P * b + 64 * g + 64],
                                    probT[:, b, c0:c0 + w], start=(kt == 0 and b == 0), stop=(kt == 0 and b == 1))
                if b == 0:
                    last = T.matmul(ps[o, 7, :], vcb[0:N_CMP, g, :], pcT[0:N_CMP, :], start=False, stop=False)
                last.then_inc(pv_done, 1)
            pe.wait_ge(mixa_lo, PAIRS)
            rows(0, U_OUT0, KT, yhi, ylo, 4)
            if stop == 1:
                return

            def ffn(layer, k, m, u_gu, u_dn):
                f_base = FT * layer
                pre_transposes(k)

                def tile(i, e, first):
                    u = u_gu + 2 * e
                    if not first:
                        pe.wait_ge(mult_done, f_base + 2 * i + e - 1)
                    col_unit(u, 2 * e, i).then_inc(unit_used, 1)
                    col_unit(u + 1, 2 * e + 1, i).then_inc(unit_used, 1)

                for e in range(2):
                    tile(0, e, True)
                with pe.Fori(1, FT // 2) as i:
                    for e in range(2):
                        tile(i, e, False)
                pe.wait_ge(hidlo_done, f_base + 2)
                rows(m, u_dn, FT, hidhi, hidlo, 2,
                     free={2: lambda: pe.wait_ge(mult_done, f_base + FT)}, staged_base=48 * 0 + (0 if layer == 0 else 32 + 16))
                return

            ffn(0, 1, 1, U_GU0, U_DN0)
            if stop == 2:
                return
            pre_transposes(2)
            pe.wait_ge(ws_masked, 1)
            for g in range(8):
                last = T.transpose(ps[:, 4 + g // 4, (g % 4) * P:(g % 4) * P + P], ws[:, g, :], ident[:])
            last.then_inc(ws_tr, 1)
            pe.wait_ge(ws_out, 1)
            for b in range(2):
                last = T.matmul(ps[:, 6 + b, :], ones[:], wsT[:, 4 * b:4 * b + 4, :].rearrange("p g t -> p (g t)"),
                                start=True, stop=True)
            last.then_inc(rowsum_done, 1)
            for qr in range(4):
                if qr == 1:
                    pe.wait_ge(r_done, WT)
                for j in range(4):
                    u = U_V + 4 * qr + j
                    ready(u)
                    s = u % SLOTS
                    for t in range(TT):
                        if qr >= 2 and j == 0:
                            pe.wait_ge(vgelu_done, 4 * (qr - 2) + t + 1)
                        bank = 4 * (qr % 2) + t
                        for b in range(2):
                            kk = 2 * j + b
                            c = slice(512 * b, 512 * b + 512)
                            yh, yl = yhi[:, kk, t * P:t * P + P], ylo[:, kk, t * P:t * P + P]
                            T.matmul(ps[:, bank, :], yh, whi[:, s, c], start=(kk == 0), stop=False)
                            T.matmul(ps[:, bank, :], yh, wlo[:, s, c], start=False, stop=False)
                            last = T.matmul(ps[:, bank, :], yl, whi[:, s, c], start=False, stop=(kk == KT - 1))
                        if j == 3 and t < TT - 1:
                            last.then_inc(v_done, 1)
                    last.then_inc(unit_used, 1)
            pe.wait_ge(vgelu_done, 16)
            col_unit(U_U, 0).then_inc(unit_used, 1)
            pe.wait_ge(vnorm_done, 4)
            for j in range(WT):
                if j >= 4:
                    pe.wait_ge(mixed_done, j - 3)
                for c in range(TT):
                    last = T.matmul(ps[:, 2 + j % 4, c * P:c * P + P], vG[:, c, j * P:j * P + P], wsT[:, j // 2, :],
                                    start=True, stop=True)
                last.then_inc(mix_mm, 1)
            for j in range(1, WT):
                if j >= 2:
                    pe.wait_ge(ugelu_done, j - 1)
                col_unit(U_U + j, j % 2).then_inc(unit_used, 1)
            pe.wait_ge(mixed_done, WT)
            pe.wait_ge(glo_done, 4)
            rows(2, U_OUT1, WT, ghi, glo, 4, free={2: lambda: pe.wait_ge(ugelu_done, WT)}, staged_base=32)
            if stop == 3:
                return
            ffn(1, 3, 3, U_GU1, U_DN1)
    return nc


def column_units(w):
    n = w.shape[1] // P
    return w.reshape(KT, P, n, P).transpose(2, 1, 0, 3).reshape(n, P, UNIT)


def row_units(w):
    return w.reshape(-1, P, UNIT)


def wide_units(w, c0, width):
    k = UNIT // width
    return w[:, c0:c0 + width].reshape(KT // k, k, P, width).transpose(0, 2, 1, 3).reshape(KT // k, P, UNIT)


def kernel(x, norm_gains, ffn_w_gate, ffn_w_up, ffn_w_down, ev_w_in, ev_w_out, nsa_cmp_pe, nsa_cmp_w1, nsa_cmp_w2,
           ssm_conv_w, ssm_conv_b, ssm_dt_bias, ssm_a_log, ssm_d, ssm_norm_w, od_w_in, od_ln_w, od_ln_b, od_w_s,
           od_b_s, od_w_out):
    import concourse.bacc as bacc
    from concourse import mybir
    from concourse.bass_utils import run_bass_kernel_spmd

    def ffn_units(layer):
        gu = np.stack([column_units(ffn_w_gate[layer]), column_units(ffn_w_up[layer])], axis=1)
        return [gu.reshape(2 * FT, P, UNIT), row_units(ffn_w_down[layer])]

    w_in, g_in = ev_w_in[0], od_w_in[0]
    v2 = np.concatenate([w_in[:, C_VS:C_VS + P], w_in[:, C_VW:C_VW + P]], axis=1)
    front = np.concatenate([w_in[:, c:c + n] for c, n in ((C_Q, 512), (C_KS, P), (C_KW, P), (C_KC, P), (C_VC, P))],
                           axis=1)
    stream = np.concatenate(
        [column_units(front), wide_units(v2, 0, 256), column_units(w_in[:, C_XBC:C_XBC + 1024]),
         wide_units(w_in, C_Z, 512), row_units(ev_w_out[0])]
        + ffn_units(0)
        + [wide_units(g_in, WIDTH + 512 * q, 512) for q in range(4)]
        + [column_units(g_in[:, 0:WIDTH]), row_units(od_w_out[0])]
        + ffn_units(1), axis=0)
    w_small = np.concatenate([w_in[:, C_GATE:C_GATE + N_GATE], w_in[:, C_DT:C_DT + HEADS]], axis=1)
    w_small = w_small.reshape(KT, P, 32).transpose(1, 0, 2).reshape(P, 256)
    pe = nsa_cmp_pe[0].transpose(2, 0, 1).reshape(HEAD_DIM, 2 * CMP_BLOCK)
    cols = np.concatenate(
        [ssm_conv_w[0].reshape(CONV_TAPS, 8, P).transpose(2, 0, 1).reshape(P, 32), ssm_conv_b[0].reshape(8, P).T,
         ssm_norm_w[0].reshape(4, P).T, np.concatenate([pe, pe], axis=0), od_ln_w[0].reshape(WT, P).T,
         od_ln_b[0].reshape(WT, P).T], axis=1)

    nc = bacc.Bacc("TRN2", target_bir_lowering=False, num_devices=1)
    arrays, args = {}, []
    for name, v in (("x", x), ("gains", norm_gains), ("stream", stream), ("w_small", w_small), ("cols", cols),
                    ("w1", nsa_cmp_w1), ("w2", nsa_cmp_w2), ("dt_bias", ssm_dt_bias), ("a_log", ssm_a_log),
                    ("d_skip", ssm_d), ("w_s", od_w_s), ("b_s", od_b_s)):
        arrays["in_" + name] = np.ascontiguousarray(v)
        args.append(nc.dram_tensor("in_" + name, v.shape, mybir.dt.float32, kind="ExternalInput").ap())
    out = nc.dram_tensor("out_h", (1, SEQ, D_MODEL), mybir.dt.float32, kind="ExternalOutput").ap()
    build(nc, *args, out)
    r = run_bass_kernel_spmd(nc, [arrays], core_ids=[0])
    return r.results[0]["out_h"]
```

```python
import numpy as np

D_MODEL = 1024
SEQ = 512
RMS_EPS, LN_EPS = 1e-6, 1e-5
HEADS, GROUPS, HEAD_DIM = 8, 2, 64
CMP_BLOCK, CMP_STRIDE, CMP_HIDDEN = 32, 16, 256
N_CMP = (SEQ - CMP_BLOCK) // CMP_STRIDE + 1
SSM_INNER, SSM_STATE, CONV_TAPS = 512, 128, 4
WIDTH = 2 * D_MODEL
FFN = 2816

P = 128
KT = D_MODEL // P
TT = SEQ // P
FT = FFN // P
WT = WIDTH // P
SLOTS = 4
UNIT = 1024
TAIL = 4

U_VV = 0
U_XBC = U_VV + 3
U_C = U_XBC + 8
U_Z = U_C + 2
U_KS = U_Z + 4
U_Q = U_KS + 2
U_OUT0 = U_Q + 4
U_GU0 = U_OUT0 + KT
U_DN0 = U_GU0 + 2 * FT
U_V = U_DN0 + FT
U_U = U_V + WT
U_OUT1 = U_U + WT
U_GU1 = U_OUT1 + WT
U_DN1 = U_GU1 + 2 * FT
U_END = U_DN1 + FT
ROWS_END = (U_GU0, U_V, U_GU1, U_END)

C_Q, C_KC, C_VC, C_KS, C_VS, C_KW, C_VW, C_GATE, C_Z, C_XBC, C_DT = (
    0, 512, 640, 768, 896, 1024, 1152, 1280, 1304, 1816, 2840)
N_GATE = 3 * HEADS
VV = 256 + N_GATE + HEADS
COLS0 = 32 + 8 + 4 + 64
MASKED = 1e33
FLOOR = 1e29


def build(nc, x, gains, stream, cols, w1, w2, dt_bias, a_log, d_skip, w_s, b_s, out, stop=99):
    from contextlib import ExitStack

    import concourse.bass as bass
    from concourse import mybir

    f32, f32r, bf16 = mybir.dt.float32, mybir.dt.float32r, mybir.dt.bfloat16
    ALU = mybir.AluOpType
    ACT = mybir.ActivationFunctionType
    AX = mybir.AxisListType
    ds = bass.ds

    base = [16512 // 4]

    def at(name, shape, dt=f32, where=None):
        size = int(np.prod(shape[1:])) * (2 if dt is bf16 else 4)
        if where is None:
            where = base[0]
            base[0] += -(-size // 32) * 8
            assert base[0] * 4 <= 229344, (name, base[0] * 4)
        return nc.alloc_sbuf_tensor_at(name, list(shape), dt, offset=where * 4)

    h = at("h", [P, TT, D_MODEL])
    yhi = at("yhi", [P, KT, SEQ], f32r)
    ylo = at("ylo", [P, KT, SEQ], f32r)
    raw = at("raw", [P, SLOTS, UNIT])
    whi = at("whi", [P, SLOTS, UNIT], f32r)
    wlo = at("wlo", [P, SLOTS, UNIT], f32r)
    tmp_at = base[0]
    tmp = at("tmp", [P, 4, SEQ])
    hn = at("hn", [P, 2, D_MODEL], where=tmp_at)
    gain_pre = at("gain_pre", [P, D_MODEL])
    post_at = base[0]
    gain_post = at("gain_post", [P, D_MODEL])
    w2s = at("w2s", [P, 2, 2, HEAD_DIM], where=post_at + 512)
    hidc = at("hidc", [P, 2, 2, 2 * N_CMP], where=post_at + 768)
    junk = at("junk", [P, D_MODEL], bf16)
    ident = at("ident", [P, P])
    stat = at("stat", [P, 4, 16])
    rst_t = at("rst_t", [P, 4, 16])
    half = at("half", [P, 8])
    arena = base[0]
    ARENA = FT * SEQ * 2
    hidhi = at("hidhi", [P, FT, SEQ], f32r)
    hidlo = at("hidlo", [P, FT, SEQ], f32r)

    a = [arena]

    def inner(name, shape, dt=f32, where=None):
        w = a[0] if where is None else where
        t = at(name, shape, dt, where=w)
        if where is None:
            a[0] += -(-int(np.prod(shape[1:])) // 8) * 8
            assert a[0] <= arena + ARENA, (name, a[0] - arena - ARENA)
        return t

    qT = inner("qT", [P, 4, SEQ])
    ksD = inner("ksD", [P, 2, GROUPS, SEQ])
    vN = inner("vN", [P, TT, 256])
    bias_at = a[0]
    bias = inner("bias", [P, HEADS, SEQ])
    w1v = inner("w1v", [P, 16, CMP_HIDDEN], where=bias_at)
    xbcT = inner("xbcT", [P, 8, SEQ])
    zN = inner("zN", [P, TT, SSM_INNER])
    early_at = a[0]
    w1k = inner("w1k", [P, 16, CMP_HIDDEN])
    blk = inner("blk", [P, 2, 16, 2 * N_CMP])
    cT = inner("cT", [P, 2, SEQ])
    late = early_at
    xN = inner("xN", [P, TT, SSM_INNER], where=late); late += 2048
    BN = inner("BN", [P, TT, 256], where=late); late += 1024
    dec = inner("dec", [P, HEADS, P], where=late); late += 1024
    Mt = inner("Mt", [P, HEADS, P], where=late); late += 1024
    xdt = inner("xdt", [P, SSM_INNER], where=late); late += 512
    xdd = inner("xdd", [P, SSM_INNER], where=late); late += 512
    prev = inner("prev", [P, SSM_INNER], where=late); late += 512
    assert late <= a[0]
    small = {}
    for nm, n in (("cols", COLS0), ("dtb", 8), ("alog", 8),
                  ("dsk", 8), ("U", 128)):
        small[nm] = at("c_" + nm, [P, n])
    mneg = at("mneg", [P, P], bf16)
    ident_bf = at("ident_bf", [P, P], bf16)
    small["cw"], small["cb"] = small["cols"][:, 0:32], small["cols"][:, 32:40]
    small["nw"], small["pe2"] = small["cols"][:, 40:44], small["cols"][:, 44:108]
    kcb = inner("kcb", [P, GROUPS, N_CMP], where=late)
    vcb = inner("vcb", [P, GROUPS, HEAD_DIM], where=late + 64)
    dcmp = inner("dcmp", [P, TT, N_CMP], where=late + 192)
    assert late + 320 <= arena + ARENA
    sm = at("sm", [P, 16, 32])
    gates = at("gates", [P, TT, N_GATE])
    ones = at("ones", [P, P])
    pr_at = early_at
    prob = inner("prob", [P, 2, 1280], where=pr_at)
    probT = inner("probT", [P, 2, 1280], where=pr_at + 2560)
    pc = inner("pc", [P, TT, N_CMP], where=pr_at + 5120)
    pcT = inner("pcT", [P, SEQ], where=pr_at + 5120 + 128)
    att = inner("att", [P, 8, 8], where=pr_at + 5120 + 128 + 512)
    assert pr_at + 5120 + 128 + 512 + 64 <= arena + ARENA
    vG = at("vG", [P, TT, WIDTH], where=arena)
    glo = at("glo", [P, WT, SEQ], f32r, where=arena)
    mixed = at("mixed", [P, WT, SEQ], where=arena + 8192)
    ghi = at("ghi", [P, WT, SEQ], f32r, where=arena + 8192)
    Rt = at("Rt", [P, WT, P], where=arena + 16384)
    ws = at("ws", [P, 8, P], where=arena + 18432)
    wsT = at("wsT", [P, 8, P], where=arena + 19456)
    bsbc = at("bsbc", [P, 8, P], where=arena + 20480)
    lncols = at("lncols", [P, 2 * WT], where=arena + 21504)
    lnw, lnb = lncols[:, 0:WT], lncols[:, WT:2 * WT]
    vstat = at("vstat", [P, TT, 4, 6], where=arena + 21504 + 32)
    vmv = at("vmv", [P, TT, 8], where=arena + 21504 + 32 + 96)

    ctx = ExitStack()
    with ctx:
        ps = ctx.enter_context(nc.psum_tensor("ps", [P, 8, 512], f32))

        def sem(name):
            return ctx.enter_context(nc.semaphore(name))

        raw_loaded = [sem(f"raw_loaded{i}") for i in range(SLOTS)]
        hi_done, lo_done, unit_used = sem("hi_done"), sem("lo_done"), sem("unit_used")
        x_loaded = [sem(f"x_loaded{i}") for i in range(TT)]
        gain_pre_loaded, gain_post_loaded = sem("gain_pre_loaded"), sem("gain_post_loaded")
        consts_loaded, cmp_loaded, gmlp_loaded = sem("consts_loaded"), sem("cmp_loaded"), sem("gmlp_loaded")
        act_step, dve_step, pool_step = sem("act_step"), sem("dve_step"), sem("pool_step")
        consts_made = sem("consts_made")
        presq_done, prerstd_done, hn_done, transposed = (
            sem("presq_done"), sem("prerstd_done"), sem("hn_done"), sem("transposed"))
        yhi_done, ylo_done = sem("yhi_done"), sem("ylo_done")
        rows_done, postsq_done, postrstd_done, scaled_done, h_ready = (
            sem("rows_done"), sem("postsq_done"), sem("postrstd_done"), sem("scaled_done"), sem("h_ready"))
        silu_done, mult_done, hidhi_done, hidlo_done = (
            sem("silu_done"), sem("mult_done"), sem("hidhi_done"), sem("hidlo_done"))
        staged = sem("staged")
        q_out, ka_out, kd_out, c_out, v_out = sem("q_out"), sem("ka_out"), sem("kd_out"), sem("c_out"), sem("v_out")
        conv_done, xbc_ready, z_ready = sem("conv_done"), sem("xbc_ready"), sem("z_ready")
        yf_done, ytot = sem("yf_done"), 0
        blk_done, cmp_hid, cmp_silu, cmp_kv, cmp_out, bias_done = (
            sem("blk_done"), sem("cmp_hid"), sem("cmp_silu"), sem("cmp_kv"), sem("cmp_out"), sem("bias_done"))
        gate_exp, sp_exp, sp_ln, a_exp, dt_in, dt_w, da_done = (
            sem("gate_exp"), sem("sp_exp"), sem("sp_ln"), sem("a_exp"), sem("dt_in"), sem("dt_w"), sem("da_done"))
        cums_done, nacs_done, dst_in, ssm_exp = sem("cums_done"), sem("nacs_done"), sem("dst_in"), sem("ssm_exp")
        xb_tr, xn_out, bn_out = sem("xb_tr"), sem("xn_out"), sem("bn_out")
        ssm_seg, dec_done, m_done, xd_done, ssm_mm, prev_done, y_gated = (
            sem("ssm_seg"), sem("dec_done"), sem("m_done"), sem("xd_done"), sem("ssm_mm"), sem("prev_done"),
            sem("y_gated"))
        ysq_done, yr_done, yn_done, y_tr, mixs_hi, mixs_lo = (
            sem("ysq_done"), sem("yr_done"), sem("yn_done"), sem("y_tr"), sem("mixs_hi"), sem("mixs_lo"))
        qk_done, biased, cbiased, exp_done, cexp_done, scaled, p_tr, pt_act, pt_dve, pv_done, mixa_hi, mixa_lo = (
            sem("qk_done"), sem("biased"), sem("cbiased"), sem("exp_done"), sem("cexp_done"), sem("scaled"),
            sem("p_tr"), sem("pt_act"), sem("pt_dve"), sem("pv_done"), sem("mixa_hi"), sem("mixa_lo"))
        ws_masked, ws_tr, ws_out, rowsum_done, r_done = (
            sem("ws_masked"), sem("ws_tr"), sem("ws_out"), sem("rowsum_done"), sem("r_done"))
        v_done, vgelu_done, vmv_done, vrstd_done, vnorm_done = (
            sem("v_done"), sem("vgelu_done"), sem("vmv_done"), sem("vrstd_done"), sem("vnorm_done"))
        mix_mm, mixed_done, ugelu_done, g_done, ghi_done, glo_done = (
            sem("mix_mm"), sem("mixed_done"), sem("ugelu_done"), sem("g_done"), sem("ghi_done"), sem("glo_done"))
        out_written = sem("out_written")
        block = ctx.enter_context(nc.Block())

        n_small = 9

        in_cols = [C_Q + P * j for j in range(4)] + [C_KS, C_KW, C_KC, C_VC]
        PAIRS = HEADS // 2

        @block.sync
        def _(sp):
            def load(u, i=0):
                s = u % SLOTS
                if u >= SLOTS:
                    sp.wait_ge(lo_done, 4 * (u // 4 + i) + s - 3)
                src = stream[ds(4 * i + u, 1), :, :].rearrange("a p n -> (a p) n")
                sp.dma_start(raw[:, s, :], src).then_inc(raw_loaded[s], 16)

            def loads(u0, u1):
                turns = (u1 - u0) // 4
                if turns > 1:
                    with sp.Fori(0, turns) as i:
                        for j in range(4):
                            load(u0 + j, i)
                    u0 += 4 * turns
                for u in range(u0, u1):
                    load(u)

            def gain(dst, layer, k, signal):
                sp.dma_start(dst[:], gains[layer, k:k + 1, :].broadcast_to([P, D_MODEL])).then_inc(signal, 16)

            for t in range(TT):
                sp.dma_start(h[:, t, :], x[0].rearrange("(t p) d -> p t d", p=P)[:, t, :]).then_inc(x_loaded[t], 16)
            gain(gain_pre, 0, 0, gain_pre_loaded)
            for u in range(4):
                load(u)
            c = small
            sp.dma_start(c["cols"][:], cols[:, 0:COLS0]).then_inc(consts_loaded, 16)
            sp.dma_start(c["dtb"][:], dt_bias[0:1, :].broadcast_to([P, HEADS])).then_inc(consts_loaded, 16)
            sp.dma_start(c["alog"][:], a_log[0:1, :].broadcast_to([P, HEADS])).then_inc(consts_loaded, 16)
            sp.dma_start(c["dsk"][:], d_skip[0:1, :].broadcast_to([P, HEADS])).then_inc(consts_loaded, 16)
            for u in range(4, 8):
                load(u)
            sp.dma_start(w1k[:], w1[0, 0].rearrange("(t p) n -> p t n", p=P)).then_inc(cmp_loaded, 16)
            sp.dma_start(w1v[:], w1[0, 1].rearrange("(t p) n -> p t n", p=P)).then_inc(cmp_loaded, 16)
            sp.dma_start(w2s[:].rearrange("p y k d -> p (y k) d"),
                         w2[0].rearrange("y (k p) d -> p (y k) d", p=P)).then_inc(cmp_loaded, 16)
            loads(8, U_GU0)
            sp.wait_ge(cmp_kv, 1)
            gain(gain_post, 0, 1, gain_post_loaded)
            sp.wait_ge(ylo_done, 4)
            gain(gain_pre, 0, 2, gain_pre_loaded)
            if stop > 1:
                loads(U_GU0, U_GU0 + 4)
                sp.wait_ge(h_ready, 4)
                gain(gain_post, 0, 3, gain_post_loaded)
                sp.wait_ge(hn_done, 8)
                gain(gain_pre, 1, 0, gain_pre_loaded)
                loads(U_GU0 + 4, U_V)
            if stop > 2:
                loads(U_V, U_V + 4)
                sp.wait_ge(h_ready, 8)
                gain(gain_post, 1, 1, gain_post_loaded)
                sp.wait_ge(hn_done, 12)
                gain(gain_pre, 1, 2, gain_pre_loaded)
                sp.dma_start(ws[:], w_s[0].rearrange("g t s -> t g s")).then_inc(gmlp_loaded, 16)
                for g in range(8):
                    sp.dma_start(bsbc[:, g, :], b_s[0, g:g + 1, :].broadcast_to([P, P])).then_inc(gmlp_loaded, 16)
                sp.dma_start(lncols[:], cols[:, COLS0:COLS0 + 2 * WT]).then_inc(gmlp_loaded, 16)
                loads(U_V + 4, U_GU1)
            if stop > 3:
                loads(U_GU1, U_GU1 + 4)
                sp.wait_ge(h_ready, 12)
                gain(gain_post, 1, 3, gain_post_loaded)
                loads(U_GU1 + 4, U_END)
            n_ready = {1: 4, 2: 8, 3: 12}.get(stop, 16)
            o3 = out[0].rearrange("(t p) d -> p t d", p=P)
            for t in range(TT):
                sp.wait_ge(h_ready, n_ready - TT + t + 1)
                sp.dma_start(o3[:, t, :], h[:, t, :]).then_inc(out_written, 16)
            sp.wait_ge(out_written, 16 * TT)

        last_unit = {1: U_GU0, 2: U_V, 3: U_GU1}.get(stop, U_END)

        @block.scalar
        def _(act):
            steps = [0]

            def step(ins):
                steps[0] += 1
                ins.then_inc(act_step, 1)
                act.wait_ge(act_step, steps[0])

            def split_hi(u, i=0):
                s = u % SLOTS
                n = 4 * (u // 4 + i) + s
                if u >= last_unit:
                    return
                act.wait_ge(raw_loaded[s], 16 * (u // 4 + i) + 16)
                if u >= SLOTS:
                    act.wait_ge(unit_used, n - 3)
                nc.scalar.activation(whi[:, s, :], raw[:, s, :], ACT.Copy).then_inc(hi_done, 1)

            junk_writer = []

            def junk_free(sem_, count):
                if junk_writer:
                    act.wait_ge(*junk_writer.pop())
                junk_writer.append((sem_, count))

            def post_square(m, t):
                n = 4 * m + t
                if t < TT - 1:
                    act.wait_ge(rows_done, 3 * m + t + 1)
                else:
                    act.wait_ge(unit_used, ROWS_END[m])
                junk_free(postsq_done, n + 1)
                nc.scalar.activation(junk[:], ps[:, 2 * t:2 * t + 2, :].rearrange("p b n -> p (b n)"), ACT.Square,
                                     accum_out=stat[:, 0, n:n + 1]).then_inc(postsq_done, 1)

            def pre_square(k, t):
                n = 4 * k + t
                if k == 0:
                    act.wait_ge(x_loaded[t], 16)
                else:
                    act.wait_ge(h_ready, n - 3)
                junk_free(presq_done, n + 1)
                nc.scalar.activation(junk[:], h[:, t, :], ACT.Square,
                                     accum_out=stat[:, 1, n:n + 1]).then_inc(presq_done, 1)

            def pre_hi(k, t):
                n = 4 * k + t
                act.wait_ge(transposed, n + 1)
                nc.scalar.activation(yhi[:, :, t * P:t * P + P],
                                     ps[:, 2 * t:2 * t + 2, :].rearrange("p b (k n) -> p (b k) n", n=P),
                                     ACT.Copy).then_inc(yhi_done, 1)

            def boundary(m, u_next):
                last = m == 3 or m == stop - 1
                for t in range(TT):
                    post_square(m, t)
                    if last:
                        continue
                    if t == TT - 1:
                        split_hi(u_next)
                    pre_square(m + 1, t)
                    if t:
                        pre_hi(m + 1, t - 1)
                if not last:
                    split_hi(u_next + 1)
                    pre_hi(m + 1, TT - 1)
                    split_hi(u_next + 2)
                    split_hi(u_next + 3)

            for t in range(TT):
                pre_square(0, t)
                if t:
                    pre_hi(0, t - 1)
            split_hi(0)
            pre_hi(0, 3)
            for u in range(1, 4):
                split_hi(u)
            for u in range(4, 7):
                split_hi(u)
            act.wait_ge(unit_used, U_VV + 3)
            nc.scalar.activation(gates[:], ps[:, 4:8, 256:256 + N_GATE], ACT.Exp, scale=-1.0).then_inc(gate_exp, 1)
            act.wait_ge(dt_in, 1)
            nc.scalar.activation(sm[:, 2, :], sm[:, 1, :], ACT.Exp).then_inc(sp_exp, 1)
            nc.scalar.activation(sm[:, 3, 0:8], small["alog"][:], ACT.Exp).then_inc(a_exp, 1)
            act.wait_ge(dt_w, 1)
            nc.scalar.activation(sm[:, 5, :], sm[:, 4, :], ACT.Ln).then_inc(sp_ln, 1)
            split_hi(7)
            act.wait_ge(cums_done, 2)
            nc.scalar.activation(sm[:, 9, :], ps[:, 4, 0:32], ACT.Exp).then_inc(ssm_exp, 1)
            nc.scalar.activation(sm[:, 10, :], ps[:, 4, 32:64], ACT.Exp).then_inc(ssm_exp, 1)
            act.wait_ge(dst_in, 1)
            nc.scalar.activation(sm[:, 11, :], sm[:, 12, :], ACT.Exp).then_inc(ssm_exp, 1)
            split_hi(8)
            for j in range(8):
                act.wait_ge(conv_done, j + 1)
                nc.scalar.activation(xbcT[:, j, :], tmp[:, j % 2, :], ACT.Silu).then_inc(xbc_ready, 1)
                split_hi(9 + j)
            for j in range(2):
                act.wait_ge(unit_used, U_C + j + 1)
                nc.scalar.copy(cT[:, j, :], ps[:, j, :]).then_inc(c_out, 1)
            for u in range(17, 21):
                split_hi(u)
            for t in range(TT):
                if t == 0:
                    act.wait_ge(unit_used, U_Z + 4)
                nc.scalar.activation(zN[:, t, :], ps[:, 4 + t, :], ACT.Silu).then_inc(z_ready, 1)
            act.wait_ge(cmp_hid, 1)
            nc.scalar.activation(hidc[:].rearrange("p a b n -> p (a b n)"), ps[:, 0, 0:8 * N_CMP],
                                 ACT.Silu).then_inc(cmp_silu, 1)
            for j in range(2):
                act.wait_ge(unit_used, U_KS + j + 1)
                for e in range(2):
                    nc.scalar.copy(ksD[64 * e:64 * e + 64, j, 0, :], ps[0:64, 2 + j, :]).then_inc(ka_out, 1)
                split_hi(21 + j)
            for c in range(TT):
                act.wait_ge(xb_tr, c + 1)
                nc.scalar.copy(xN[:, c, :], ps[:, c % 2, :]).then_inc(xn_out, 1)

            def y_square(c):
                for g in range(2):
                    act.wait_ge(y_gated, 2 * (c + 1))
                    junk_free(ysq_done, 2 * c + g + 1)
                    nc.scalar.activation(junk[:, 0:256], zN[:, c, 256 * g:256 * g + 256], ACT.Square,
                                         accum_out=stat[:, 2, 2 * c + g:2 * c + g + 1]).then_inc(ysq_done, 1)

            for c in range(TT):
                act.wait_ge(ssm_seg, c + 1)
                if c:
                    act.wait_ge(m_done, 2 * c)
                for hd in range(HEADS):
                    nc.scalar.activation(dec[:, hd, :], ps[:, hd // 4, (hd % 4) * P:(hd % 4) * P + P], ACT.Exp,
                                         bias=sm[:, 8, 8 * c + hd:8 * c + hd + 1]).then_inc(dec_done, 1)
                act.wait_ge(unit_used, U_Q + c + 1)
                nc.scalar.mul(qT[:, c, :], ps[:, 6 + c % 2, :], -HEAD_DIM ** -0.5).then_inc(q_out, 1)
                split_hi(23 + c)
                if c:
                    y_square(c - 1)
            y_square(3)

            widths = [(3, 0), (2, 512), (0, 896), (1, 1024)]

            def exps(j):
                b = j % 2
                for idx, (qt, off) in enumerate(widths):
                    act.wait_ge(biased, 4 * j + idx + 1)
                    w = (qt + 1) * P
                    nc.scalar.activation(prob[:, b, off:off + w], prob[:, b, off:off + w], ACT.Exp,
                                         bias=att[:, b, qt:qt + 1], scale=-1.0,
                                         accum_out=att[:, 2 + b, qt:qt + 1]).then_inc(exp_done, 1)
                if j % 2 == 0:
                    act.wait_ge(cbiased, j // 2 + 1)
                    for qt in range(TT):
                        nc.scalar.activation(pc[:, qt, :], pc[:, qt, :], ACT.Exp, bias=att[:, 4, qt:qt + 1],
                                             scale=-1.0, accum_out=att[:, 5, qt:qt + 1]).then_inc(cexp_done, 1)

            exps(0)
            for j in range(4):
                act.wait_ge(y_tr, 1)
                nc.scalar.activation(yhi[:, 4 + j, :], ps[:, 3 + j, :], ACT.Identity,
                                     scale=small["nw"][:, j:j + 1]).then_inc(mixs_hi, 1)
            for j in range(2 * HEADS):
                if j + 1 < 2 * HEADS:
                    exps(j + 1)
                act.wait_ge(p_tr, j + 1)
                if j >= 2:
                    act.wait_ge(pv_done, j - 1)
                nc.scalar.copy(probT[:, j % 2, 0:512], ps[:, 3, :]).then_inc(pt_act, 1)
                nc.scalar.copy(probT[:, j % 2, 1024:1280], ps[:, 5, 0:256]).then_inc(pt_act, 1)
                if j % 4 == 0 and j:
                    act.wait_ge(pv_done, j)
                    nc.scalar.copy(yhi[:, j // 4 - 1, :], ps[:, 7, :]).then_inc(mixa_hi, 1)
            act.wait_ge(pv_done, 2 * HEADS)
            nc.scalar.copy(yhi[:, PAIRS - 1, :], ps[:, 7, :]).then_inc(mixa_hi, 1)
            for r in range(4):
                split_hi(U_OUT0 + 4 + r)
            boundary(0, U_GU0)

            def ffn(layer, u_gu, u_dn):
                f_base = FT * layer

                def tile(i, e, first):
                    f = 2 * i + e
                    u = u_gu + 2 * e
                    n = 4 * (u // 4) + u % 4
                    act.wait_ge(unit_used, n + 4 * i + 1)
                    if not first:
                        act.wait_ge(mult_done, f_base + f - 1)
                    nc.scalar.activation(tmp[:, e, :], ps[:, 2 * e, :], ACT.Silu).then_inc(silu_done, 1)
                    split_hi(u + 4, i)
                    act.wait_ge(mult_done, f_base + f + 1)
                    nc.scalar.copy(hidhi[:, f, :] if first else hidhi[:, ds(f, 1), :].rearrange("p a n -> p (a n)"),
                                   tmp[:, 2 + e, :]).then_inc(hidhi_done, 1)
                    split_hi(u + 5, i)

                for e in range(2):
                    tile(0, e, True)
                with act.Fori(1, FT // 2) as i:
                    for e in range(2):
                        tile(i, e, False)
                for r in range(2):
                    split_hi(u_dn + 4 + r)
                with act.Fori(0, 3) as i:
                    for j in range(4):
                        split_hi(u_dn + 6 + j, i)
                for r in range(18, FT):
                    split_hi(u_dn + r)

            if stop > 1:
                ffn(0, U_GU0, U_DN0)
                boundary(1, U_V)
            if stop > 2:
                act.wait_ge(ws_tr, 1)
                nc.scalar.copy(wsT[:].rearrange("p g t -> p (g t)"),
                               ps[:, 4:6, :].rearrange("p b n -> p (b n)")).then_inc(ws_out, 1)
                for qr in range(4):
                    for t in range(TT):
                        if t < TT - 1:
                            act.wait_ge(v_done, 3 * qr + t + 1)
                        else:
                            act.wait_ge(unit_used, U_V + 4 * qr + 4)
                        nc.scalar.activation(vG[:, t, 512 * qr:512 * qr + 512], ps[:, 4 * (qr % 2) + t, :],
                                             ACT.Gelu).then_inc(vgelu_done, 1)
                        if t == 3:
                            for j in range(4):
                                split_hi(U_V + 4 * qr + 4 + j)
                for j in range(WT):
                    act.wait_ge(unit_used, U_U + j + 1)
                    if j >= 2:
                        act.wait_ge(g_done, j - 1)
                    nc.scalar.activation(tmp[:, j % 2, :], ps[:, j % 2, :], ACT.Gelu).then_inc(ugelu_done, 1)
                    split_hi(U_U + j + 4)
                    act.wait_ge(g_done, j + 1)
                    nc.scalar.copy(ghi[:, j, :], tmp[:, 2 + j % 2, :]).then_inc(ghi_done, 1)
                for r in range(4, WT):
                    split_hi(U_OUT1 + r)
                boundary(2, U_GU1)
            if stop > 3:
                ffn(1, U_GU1, U_DN1)
                boundary(3, None)

        @block.gpsimd
        def _(pool):
            steps = [0]

            def step(ins):
                steps[0] += 1
                ins.then_inc(pool_step, 1)
                pool.wait_ge(pool_step, steps[0])

            def rstd(dst, src, scale, eps, done):
                step(nc.gpsimd.tensor_scalar(src, src, scale, eps, ALU.mult, ALU.add))
                n = src.shape[-1]
                nc.gpsimd.tensor_tensor(dst, src, half[:, 0:n], ALU.pow).then_inc(done, 1)

            def norms(k, done_sem, row, signal, t):
                n = 4 * k + t
                pool.wait_ge(done_sem, n + 1)
                c = slice(n % 16, n % 16 + 1)
                rstd(rst_t[:, row, c], stat[:, row, c], 1.0 / D_MODEL, RMS_EPS, signal)

            nc.gpsimd.memset(half[:], -0.5)
            nc.gpsimd.memset(ones[:], 1.0)
            step(nc.gpsimd.memset(ident[:], 0.0))
            nc.gpsimd.affine_select(out=ident[:], in_=ident[:], compare_op=ALU.not_equal, fill=1.0, base=0,
                                    pattern=[[-1, P]], channel_multiplier=1).then_inc(consts_made, 1)
            for t in range(TT):
                norms(0, presq_done, 1, prerstd_done, t)
            step(nc.gpsimd.memset(mneg[:], 0.0))
            nc.gpsimd.affine_select(out=small["U"][:], in_=ones[:], compare_op=ALU.is_ge, fill=0.0, base=0,
                                    pattern=[[1, P]], channel_multiplier=-1).then_inc(consts_made, 1)
            nc.gpsimd.affine_select(out=mneg[:], in_=mneg[:], compare_op=ALU.is_ge, fill=-1e30,
                                    base=0, pattern=[[1, P]], channel_multiplier=-1).then_inc(consts_made, 1)
            nc.gpsimd.tensor_copy(ident_bf[:], ident[:]).then_inc(consts_made, 1)
            pool.wait_ge(cmp_hid, 1)
            d0 = bias[:, HEADS - 1, :]
            step(nc.gpsimd.iota(d0, pattern=[[-1, SEQ]], base=SEQ - P, channel_multiplier=1,
                                allow_small_or_imprecise_dtypes=True))
            step(nc.gpsimd.affine_select(out=d0, in_=d0, compare_op=ALU.is_ge, fill=MASKED, base=SEQ - P,
                                         pattern=[[-1, SEQ]], channel_multiplier=1))
            for hd in range(HEADS):
                nc.gpsimd.tensor_scalar(bias[:, hd, :], d0, 2.0 ** -(hd + 1), None, ALU.mult).then_inc(bias_done, 1)
            step(nc.gpsimd.iota(dcmp[:], pattern=[[P, TT], [-CMP_STRIDE, N_CMP]], base=-(CMP_BLOCK - 1),
                                channel_multiplier=1, allow_small_or_imprecise_dtypes=True))
            nc.gpsimd.affine_select(out=dcmp[:], in_=dcmp[:], compare_op=ALU.is_ge, fill=MASKED,
                                    base=-(CMP_BLOCK - 1), pattern=[[P, TT], [-CMP_STRIDE, N_CMP]],
                                    channel_multiplier=1).then_inc(bias_done, 1)
            for c in range(TT):
                for g in range(2):
                    n = 2 * c + g
                    pool.wait_ge(ysq_done, n + 1)
                    rstd(rst_t[:, 2, n:n + 1], stat[:, 2, n:n + 1], 1.0 / 256, RMS_EPS, yr_done)

            def boundary(m):
                for t in range(TT):
                    norms(m, postsq_done, 0, postrstd_done, t)
                    if m < 3 and m != stop - 1:
                        norms(m + 1, presq_done, 1, prerstd_done, t)

            def stage(kt, slot, hi, lo, done_need, u_prev, i, n_staged):
                pool.wait_ge(unit_used, 4 * (u_prev // 4 + i) + u_prev % 4 + 1)
                nc.gpsimd.tensor_copy(yhi[:, slot, :], hi[:, ds(kt, 1), :].rearrange("p a n -> p (a n)")).then_inc(staged, 1)
                nc.gpsimd.tensor_copy(ylo[:, slot, :], lo[:, ds(kt, 1), :].rearrange("p a n -> p (a n)")).then_inc(staged, 1)

            def ffn_stage(layer, u_dn):
                pool.wait_ge(hidlo_done, FT * (layer + 1))
                with pool.Fori(0, 4) as i:
                    for j in range(4):
                        stage(4 * i + 2 + j, j % 2, hidhi, hidlo, None, u_dn + j, i, None)

            boundary(0)
            if stop > 1:
                ffn_stage(0, U_DN0)
                boundary(1)
            if stop > 2:
                pool.wait_ge(gmlp_loaded, 16 * 10)
                nc.gpsimd.affine_select(out=ws[:], in_=ws[:], compare_op=ALU.is_ge, fill=0.0, base=0,
                                        pattern=[[0, 8], [-1, P]], channel_multiplier=1).then_inc(ws_masked, 1)
                for t in range(TT):
                    pool.wait_ge(vmv_done, t + 1)
                    rstd(vmv[:, t, 2:3], vmv[:, t, 1:2], 1.0, LN_EPS, vrstd_done)
                pool.wait_ge(glo_done, WT)
                with pool.Fori(0, 2) as i:
                    for j in range(4):
                        stage(4 * i + 4 + j, j % 2, ghi, glo, None, U_OUT1 + 2 + j, i, None)
                boundary(2)
            if stop > 3:
                ffn_stage(1, U_DN1)
                boundary(3)

        @block.vector
        def _(dve):
            V = nc.vector
            steps = [0]

            def step(ins):
                steps[0] += 1
                ins.then_inc(dve_step, 1)
                dve.wait_ge(dve_step, steps[0])

            def split_lo(u, i=0):
                s = u % SLOTS
                if u >= last_unit:
                    return
                dve.wait_ge(hi_done, 4 * (u // 4 + i) + s + 1)
                V.tensor_tensor(wlo[:, s, :], raw[:, s, :], whi[:, s, :].bitcast(f32), ALU.subtract).then_inc(lo_done, 1)

            def post_residual(m, t):
                n = 4 * m + t
                dve.wait_ge(postrstd_done, n + 1)
                if t == 0:
                    dve.wait_ge(gain_post_loaded, 16 * (m + 1))
                y = ps[:, 2 * t:2 * t + 2, :].rearrange("p b n -> p (b n)")
                V.scalar_tensor_tensor(y, y, rst_t[:, 0, n:n + 1], gain_post[:], ALU.mult,
                                       ALU.mult).then_inc(scaled_done, 1)
                dve.wait_ge(scaled_done, n + 1)
                V.tensor_tensor(h[:, t, :], h[:, t, :], y, ALU.add).then_inc(h_ready, 1)

            def pre_scale(k, t):
                n = 4 * k + t
                dve.wait_ge(prerstd_done, n + 1)
                if t == 0:
                    dve.wait_ge(gain_pre_loaded, 16 * (k + 1))
                if n >= 2:
                    dve.wait_ge(transposed, n - 1)
                V.scalar_tensor_tensor(hn[:, n % 2, :], h[:, t, :], rst_t[:, 1, n:n + 1], gain_pre[:], ALU.mult,
                                       ALU.mult).then_inc(hn_done, 1)

            def pre_lo(k, t):
                n = 4 * k + t
                dve.wait_ge(yhi_done, n + 1)
                sl = slice(t * P, t * P + P)
                V.tensor_tensor(ylo[:, :, sl], ps[:, 2 * t:2 * t + 2, :].rearrange("p b (k n) -> p (b k) n", n=P),
                                yhi[:, :, sl].bitcast(f32), ALU.subtract).then_inc(ylo_done, 1)

            def boundary(m, u_next):
                last = m == 3 or m == stop - 1
                for t in range(TT):
                    post_residual(m, t)
                    if last:
                        continue
                    if t == TT - 1:
                        split_lo(u_next)
                    pre_scale(m + 1, t)
                    if t:
                        pre_lo(m + 1, t - 1)
                if not last:
                    split_lo(u_next + 1)
                    pre_lo(m + 1, TT - 1)
                    split_lo(u_next + 2)
                    split_lo(u_next + 3)

            for t in range(TT):
                pre_scale(0, t)
                if t == 3:
                    split_lo(0)
                if t:
                    pre_lo(0, t - 1)
            pre_lo(0, 3)
            for u in range(1, 4):
                split_lo(u)
            for u in range(4, 7):
                split_lo(u)
            dve.wait_ge(unit_used, U_VV + 3)
            dve.wait_ge(consts_loaded, 16 * 4)
            dtp = ps[:, 4:8, 256 + N_GATE:VV]

            def smv(k):
                return sm[:, k, :].rearrange("p (t n) -> p t n", t=TT)

            def rowbc(ap):
                return ap.unsqueeze(1).broadcast_to([P, TT, HEADS])

            dve.wait_ge(gate_exp, 1)
            step(V.tensor_tensor(smv(0), dtp, rowbc(small["dtb"][:]), ALU.add))
            step(V.tensor_scalar(sm[:, 1, :], sm[:, 0, :], -1.0, None, ALU.mult))
            V.tensor_tensor(sm[:, 1, :], sm[:, 1, :], sm[:, 0, :], ALU.min).then_inc(dt_in, 1)
            for t in range(TT):
                V.tensor_copy(vN[:, t, :], ps[:, 4 + t, 0:256]).then_inc(v_out, 1)
            gflat = gates[:].rearrange("p t n -> p (t n)")
            step(V.tensor_scalar(gflat, gflat, 1.0, None, ALU.add))
            V.reciprocal(gflat, gflat)
            dve.wait_ge(sp_exp, 1)
            V.tensor_scalar(sm[:, 4, :], sm[:, 2, :], 1.0, None, ALU.add).then_inc(dt_w, 1)
            dve.wait_ge(dt_w, 1)
            step(V.tensor_scalar(sm[:, 6, :], sm[:, 4, :], -1.0, 1e-30, ALU.add, ALU.add))
            step(V.reciprocal(sm[:, 6, :], sm[:, 6, :]))
            step(V.tensor_tensor(sm[:, 6, :], sm[:, 6, :], sm[:, 2, :], ALU.mult))
            dve.wait_ge(sp_ln, 1)
            step(V.scalar_tensor_tensor(sm[:, 6, :], sm[:, 5, :], 1e-30, sm[:, 6, :], ALU.add, ALU.mult))
            step(V.scalar_tensor_tensor(sm[:, 7, :], sm[:, 0, :], 0.0, sm[:, 6, :], ALU.max, ALU.add))
            dve.wait_ge(a_exp, 1)
            step(V.tensor_scalar(sm[:, 3, 0:8], sm[:, 3, 0:8], -1.0, None, ALU.mult))
            V.tensor_tensor(smv(13), smv(7), rowbc(sm[:, 3, 0:8]), ALU.mult).then_inc(da_done, 1)
            split_lo(7)
            dve.wait_ge(cums_done, 2)
            dve.wait_ge(ssm_exp, 2)
            step(V.tensor_scalar(sm[:, 8, :], ps[:, 4, 0:32], -1.0, None, ALU.mult))
            V.tensor_copy(sm[:, 14, :], sm[:, 8, :]).then_inc(nacs_done, 1)
            V.tensor_tensor(sm[:, 12, :], sm[:, 8, :], ps[:, 4, 32:64], ALU.add).then_inc(dst_in, 1)
            split_lo(8)
            cwv = small["cw"].rearrange("p (k c) -> p k c", k=CONV_TAPS)
            for j in range(8):
                dve.wait_ge(unit_used, U_XBC + j + 1)
                if j >= 2:
                    dve.wait_ge(xbc_ready, j - 1)
                src, acc = ps[:, j % 4, :], tmp[:, j % 2, :]
                step(V.tensor_scalar(acc, src, cwv[:, 3, j:j + 1], small["cb"][:, j:j + 1], ALU.mult, ALU.add))
                for lag in (1, 2, 3):
                    ins = V.scalar_tensor_tensor(acc[:, lag:], src[:, 0:SEQ - lag], cwv[:, 3 - lag, j:j + 1],
                                                 acc[:, lag:], ALU.mult, ALU.add)
                    if lag < 3:
                        step(ins)
                    else:
                        ins.then_inc(conv_done, 1)
                split_lo(9 + j)
            dve.wait_ge(c_out, 2)
            dve.wait_ge(cmp_loaded, 16 * 3)
            for y in range(2):
                for g in range(2):
                    src = cT[64 * g:64 * g + 64, y, :].rearrange("p (b r) -> p r b", r=16)
                    pe3 = small["pe2"][64 * g:64 * g + 64, 32 * y:32 * y + 32]
                    for par in range(2):
                        for w in range(2):
                            pv = pe3[:, 16 * w + par:16 * w + 16:2].unsqueeze(2).broadcast_to([64, 8, N_CMP])
                            V.tensor_tensor(
                                blk[64 * par:64 * par + 64, y, 8 * w:8 * w + 8, N_CMP * g:N_CMP * g + N_CMP],
                                src[:, par::2, w:w + N_CMP], pv, ALU.add).then_inc(blk_done, 1)
            for u in range(17, 21):
                split_lo(u)
            dve.wait_ge(unit_used, U_KS + 1)
            for e in range(2):
                V.tensor_copy(ksD[64 * e:64 * e + 64, 0, 1, :], ps[64:128, 2, :]).then_inc(kd_out, 1)
            split_lo(21)
            dve.wait_ge(cmp_kv, 1)
            V.tensor_copy(kcb[:].rearrange("p g c -> p (g c)"), ps[:, 1, 0:2 * N_CMP])
            V.tensor_copy(vcb[0:N_CMP].rearrange("p g d -> p (g d)"), ps[0:N_CMP, 1, 128:256]).then_inc(cmp_out, 1)

            dve.wait_ge(unit_used, U_KS + 2)
            for e in range(2):
                V.tensor_copy(ksD[64 * e:64 * e + 64, 1, 1, :], ps[64:128, 3, :]).then_inc(kd_out, 1)
            split_lo(22)
            for c in range(TT):
                dve.wait_ge(xb_tr, c + 1)
                V.tensor_copy(BN[:, c, :], ps[:, 2 + c % 2, 0:256]).then_inc(bn_out, 1)
            dve.wait_ge(ssm_exp, 3)
            step(V.memset(prev[:], 0.0))

            def heads3(ap):
                return ap.rearrange("p (h d) -> p h d", h=HEADS)

            def colbc(k, c):
                return sm[:, k, 8 * c:8 * c + 8].unsqueeze(2).broadcast_to([P, HEADS, HEAD_DIM])

            for c in range(TT):
                if c == 0:
                    dve.wait_ge(xn_out, TT)
                if c:
                    dve.wait_ge(ssm_mm, c)
                step(V.tensor_tensor(heads3(xdt[:]), heads3(xN[:, c, :]), colbc(7, c), ALU.mult))
                V.tensor_tensor(heads3(xdd[:]), heads3(xdt[:]), colbc(11, c), ALU.mult).then_inc(xd_done, 1)
                dve.wait_ge(dec_done, 8 * (c + 1))
                for g in range(2):
                    cb = ps[:, 2, P * g:P * g + P].unsqueeze(1).broadcast_to([P, 4, P])
                    V.tensor_tensor(Mt[:, 4 * g:4 * g + 4, :], dec[:, 4 * g:4 * g + 4, :], cb,
                                    ALU.mult).then_inc(m_done, 1)
                split_lo(23 + c)
                dve.wait_ge(ssm_mm, c + 1)
                t1, t2 = tmp[:, 0, :], tmp[:, 1, :]
                step(V.tensor_tensor(heads3(t1), heads3(ps[:, 4, :]), colbc(9, c), ALU.mult))
                step(V.tensor_tensor(t1, t1, ps[:, 3, :], ALU.add))
                step(V.tensor_tensor(heads3(t2), heads3(xN[:, c, :]),
                                     small["dsk"][:].unsqueeze(2).broadcast_to([P, HEADS, HEAD_DIM]), ALU.mult))
                step(V.tensor_tensor(t1, t1, t2, ALU.add))
                if c == 0:
                    dve.wait_ge(z_ready, TT)
                V.tensor_tensor(zN[:, c, :], zN[:, c, :], t1, ALU.mult).then_inc(y_gated, 1)
                step(V.tensor_tensor(heads3(prev[:]), heads3(prev[:]), colbc(10, c), ALU.mult))
                V.tensor_tensor(prev[:], prev[:], ps[:, 5, :], ALU.add).then_inc(y_gated, 1)
                dve.wait_ge(y_gated, 2 * (c + 1))
            widths = [(3, 0), (2, 512), (0, 896), (1, 1024)]
            where = {3: (0, 0), 2: (1, 0), 0: (1, 384), 1: (2, 0)}

            def add_bias(j):
                hd, b = j // 2, j % 2
                dve.wait_ge(qk_done, j + 1)
                if j == 0:
                    dve.wait_ge(bias_done, HEADS + 1)
                if j >= 2:
                    dve.wait_ge(p_tr, j - 1)
                for qt, off in widths:
                    bk, c0 = where[qt]
                    w = (qt + 1) * P
                    V.tensor_tensor_reduce(out=prob[:, b, off:off + w], in0=ps[:, bk, c0:c0 + w],
                                           in1=bias[:, hd, SEQ - w:SEQ], scale=1.0, scalar=3e38, op0=ALU.add,
                                           op1=ALU.min, accum_out=att[:, b, qt:qt + 1]).then_inc(biased, 1)
                if b == 0:
                    sc = ps[:, 2, 256:256 + TT * N_CMP].rearrange("p (t c) -> p t c", t=TT)
                    step(V.scalar_tensor_tensor(pc[:].rearrange("p t c -> p (t c)"),
                                                dcmp[:].rearrange("p t c -> p (t c)"), 2.0 ** -(hd + 1),
                                                sc.rearrange("p t c -> p (t c)"), ALU.mult, ALU.add))
                    step(V.tensor_reduce(out=att[:, 4, 0:4], in_=pc[:], op=ALU.min, axis=AX.X))
                    V.tensor_scalar(att[:, 4, 0:4], att[:, 4, 0:4], FLOOR, None, ALU.min).then_inc(cbiased, 1)

            gT = gates[:].rearrange("p t n -> p n t")
            for c in range(TT):
                for g in range(2):
                    dve.wait_ge(yr_done, 2 * c + g + 1)
                    seg = zN[:, c, 256 * g:256 * g + 256]
                    V.tensor_scalar(seg, seg, rst_t[:, 2, 2 * c + g:2 * c + g + 1], None, ALU.mult).then_inc(yn_done, 1)
            add_bias(0)
            for j in range(4):
                dve.wait_ge(mixs_hi, j + 1)
                V.scalar_tensor_tensor(ylo[:, 4 + j, :], ps[:, 3 + j, :], small["nw"][:, j:j + 1],
                                       yhi[:, 4 + j, :].bitcast(f32), ALU.mult, ALU.subtract).then_inc(mixs_lo, 1)
            for j in range(2 * HEADS):
                hd, b = j // 2, j % 2
                dve.wait_ge(exp_done, 4 * (j + 1))
                step(V.reciprocal(att[:, 6, 0:4], att[:, 2 + b, 0:4]))
                step(V.tensor_tensor(att[:, 6, 0:4], att[:, 6, 0:4], gT[:, 3 * hd + 1 + b, :], ALU.mult))
                for qt, off in widths:
                    w = (qt + 1) * P
                    V.tensor_scalar(prob[:, b, off:off + w], prob[:, b, off:off + w], att[:, 6, qt:qt + 1], None,
                                    ALU.mult).then_inc(scaled, 1)
                if b == 0:
                    dve.wait_ge(cexp_done, 4 * (hd + 1))
                    step(V.tensor_scalar(att[:, 7, 0:4], att[:, 5, 0:4], 1e-30, None, ALU.max))
                    step(V.reciprocal(att[:, 7, 0:4], att[:, 7, 0:4]))
                    step(V.tensor_tensor(att[:, 7, 0:4], att[:, 7, 0:4], gT[:, 3 * hd, :], ALU.mult))
                    V.tensor_tensor(pc[:], pc[:], att[:, 7, 0:4].unsqueeze(2).broadcast_to([P, TT, N_CMP]),
                                    ALU.mult)
                    dve_last = None
                V.tensor_copy(att[:, 6, 4:5], att[:, 6, 0:1]).then_inc(scaled, 1)
                if j + 1 < 2 * HEADS and not (b == 1):
                    add_bias(j + 1)
                elif j + 1 < 2 * HEADS:
                    dve.wait_ge(p_tr, j)
                    add_bias(j + 1)
                dve.wait_ge(p_tr, j + 1)
                if j >= 2:
                    dve.wait_ge(pv_done, j - 1)
                V.tensor_copy(probT[:, b, 512:1024], ps[:, 4, :]).then_inc(pt_dve, 1)
                if b == 0:
                    V.tensor_copy(pcT[0:N_CMP, :], ps[0:N_CMP, 6, :]).then_inc(pt_dve, 1)
                if (j % 4 == 0 and j) or j == 2 * HEADS - 1:
                    pr = (j - 1) // 4
                    dve.wait_ge(mixa_hi, pr + 1)
                    V.tensor_tensor(ylo[:, pr, :], ps[:, 7, :], yhi[:, pr, :].bitcast(f32),
                                    ALU.subtract).then_inc(mixa_lo, 1)
            for r in range(4):
                split_lo(U_OUT0 + 4 + r)
            boundary(0, U_GU0)

            def ffn(layer, u_gu, u_dn):
                f_base = FT * layer

                def tile(i, e, first):
                    f = 2 * i + e
                    u = u_gu + 2 * e
                    dve.wait_ge(unit_used, 4 * ((u + 1) // 4) + (u + 1) % 4 + 4 * i + 1)
                    dve.wait_ge(silu_done, f_base + f + 1)
                    if not first:
                        dve.wait_ge(hidlo_done, f_base + f - 1)
                    V.tensor_tensor(tmp[:, 2 + e, :], tmp[:, e, :], ps[:, 2 * e + 1, :], ALU.mult).then_inc(mult_done, 1)
                    split_lo(u + 4, i)
                    dve.wait_ge(hidhi_done, f_base + f + 1)
                    row = lambda tl: tl[:, f, :] if first else tl[:, ds(f, 1), :].rearrange("p a n -> p (a n)")
                    V.tensor_tensor(row(hidlo), tmp[:, 2 + e, :], row(hidhi).bitcast(f32),
                                    ALU.subtract).then_inc(hidlo_done, 1)
                    split_lo(u + 5, i)

                for e in range(2):
                    tile(0, e, True)
                with dve.Fori(1, FT // 2) as i:
                    for e in range(2):
                        tile(i, e, False)
                for r in range(2):
                    split_lo(u_dn + 4 + r)
                with dve.Fori(0, 3) as i:
                    for j in range(4):
                        split_lo(u_dn + 6 + j, i)
                for r in range(18, FT):
                    split_lo(u_dn + r)

            if stop > 1:
                ffn(0, U_GU0, U_DN0)
                boundary(1, U_V)
            if stop > 2:
                for j in range(WT):
                    g = j // 2
                    if j == 0:
                        dve.wait_ge(rowsum_done, 1)
                    V.scalar_tensor_tensor(Rt[:, j, :], ps[:, 6 + g // 4, (g % 4) * P:(g % 4) * P + P],
                                           lnb[:, j:j + 1], bsbc[:, g, :], ALU.mult, ALU.add).then_inc(r_done, 1)
                for qr in range(4):
                    for t in range(TT):
                        dve.wait_ge(vgelu_done, 4 * qr + t + 1)
                        V.bn_stats(vstat[:, t, qr, :], vG[:, t, 512 * qr:512 * qr + 512]).then_inc(dve_step, 1)
                        steps[0] += 1
                    for j in range(4):
                        if qr < 3:
                            split_lo(U_V + 4 * qr + 4 + j)
                for t in range(TT):
                    if t == 0:
                        dve.wait_ge(dve_step, steps[0])
                    V.bn_aggr(vmv[:, t, 0:2], vstat[:, t].rearrange("p a b -> p (a b)")).then_inc(vmv_done, 1)
                split_lo(U_U)
                for t in range(TT):
                    dve.wait_ge(vrstd_done, t + 1)
                    V.tensor_scalar(vG[:, t, :], vG[:, t, :], vmv[:, t, 0:1], vmv[:, t, 2:3], ALU.subtract,
                                    ALU.mult).then_inc(vnorm_done, 1)
                for j in range(1, 4):
                    split_lo(U_U + j)
                for j in range(WT):
                    dve.wait_ge(mix_mm, j + 1)
                    if j == 0:
                        dve.wait_ge(r_done, WT)
                    V.scalar_tensor_tensor(mixed[:, j, :].rearrange("p (c n) -> p c n", c=TT),
                                           ps[:, 2 + j % 4, :].rearrange("p (c n) -> p c n", c=TT), lnw[:, j:j + 1],
                                           Rt[:, j, :].unsqueeze(1).broadcast_to([P, TT, P]), ALU.mult,
                                           ALU.add).then_inc(mixed_done, 1)
                dve.wait_ge(mixed_done, WT)
                for j in range(WT):
                    dve.wait_ge(ugelu_done, j + 1)
                    if j >= 2:
                        dve.wait_ge(glo_done, j - 1)
                    V.tensor_tensor(tmp[:, 2 + j % 2, :], tmp[:, j % 2, :], mixed[:, j, :], ALU.mult).then_inc(g_done, 1)
                    split_lo(U_U + j + 4)
                    dve.wait_ge(ghi_done, j + 1)
                    V.tensor_tensor(glo[:, j, :], tmp[:, 2 + j % 2, :], ghi[:, j, :].bitcast(f32),
                                    ALU.subtract).then_inc(glo_done, 1)
                for r in range(4, WT):
                    split_lo(U_OUT1 + r)
                boundary(2, U_GU1)
            if stop > 3:
                ffn(1, U_GU1, U_DN1)
                boundary(3, None)

        @block.tensor
        def _(pe):
            T = nc.tensor

            def ready(u, i=0):
                pe.wait_ge(lo_done, 4 * (u // 4 + i) + u % 4 + 1)

            def col_unit(u, bank, i=0):
                s = u % SLOTS
                ready(u, i)
                for k in range(KT):
                    hi, lo = whi[:, s, k * P:k * P + P], wlo[:, s, k * P:k * P + P]
                    T.matmul(ps[:, bank, :], hi, yhi[:, k, :], start=(k == 0), stop=False)
                    T.matmul(ps[:, bank, :], hi, ylo[:, k, :], start=False, stop=False)
                    last = T.matmul(ps[:, bank, :], lo, yhi[:, k, :], start=False, stop=(k == KT - 1))
                return last

            def row_products(s, t, hi, lo, first, last_k):
                for hf in range(2):
                    o = ps[:, 2 * t + hf, :]
                    c = slice(512 * hf, 512 * hf + 512)
                    T.matmul(o, hi[:, t * P:t * P + P], whi[:, s, c], start=first, stop=False)
                    T.matmul(o, hi[:, t * P:t * P + P], wlo[:, s, c], start=False, stop=False)
                    last = T.matmul(o, lo[:, t * P:t * P + P], whi[:, s, c], start=False, stop=last_k)
                return last

            def rows(m, u0, n, hi, lo, peel, free=None, staged_base=0):
                for r in range(peel):
                    ready(u0 + r)
                    for q, t in enumerate((2, 3, 0, 1)):
                        if r == 0 and free and q in free:
                            free[q]()
                        last = row_products((u0 + r) % SLOTS, t, hi[:, r, :], lo[:, r, :], r == 0, False)
                    last.then_inc(unit_used, 1)
                loops = (n - peel - TAIL) // 4
                if loops:
                    with pe.Fori(0, loops) as i:
                        for j in range(4):
                            u = u0 + peel + j
                            pe.wait_ge(staged, staged_base + 8 * i + 2 * (j + 1))
                            ready(u, i)
                            for t in range(TT):
                                last = row_products(u % SLOTS, t, yhi[:, j % 2, :], ylo[:, j % 2, :], False, False)
                            last.then_inc(unit_used, 1)
                for r in range(n - TAIL, n):
                    ready(u0 + r)
                for t in range(TT):
                    for r in range(n - TAIL, n):
                        last = row_products((u0 + r) % SLOTS, t, hi[:, r, :], lo[:, r, :], peel == 0 and r == n - TAIL,
                                            r == n - 1)
                        if r == n - 1 and t < TT - 1:
                            last.then_inc(rows_done, 1)
                        if t == TT - 1:
                            last.then_inc(unit_used, 1)
                    if m < 3 and m != stop - 1 and t >= 2:
                        pre_transpose(m + 1, t - 2)
                if m < 3 and m != stop - 1:
                    for t in range(TT - 2, TT):
                        pre_transpose(m + 1, t)
                    pe.wait_ge(ylo_done, 4 * (m + 2))

            def pre_transpose(k, t):
                n = 4 * k + t
                pe.wait_ge(hn_done, n + 1)
                for kk in range(KT):
                    last = T.transpose(ps[:, 2 * t + kk // 4, (kk % 4) * P:(kk % 4) * P + P],
                                       hn[:, n % 2, kk * P:kk * P + P], ident[:])
                last.then_inc(transposed, 1)

            pe.wait_ge(consts_made, 1)
            for t in range(TT):
                pre_transpose(0, t)
            pe.wait_ge(ylo_done, 4)
            def wide(u, k0, k1, width, out, free=None):
                ready(u)
                s = u % SLOTS
                for t in range(TT):
                    if k0 == 0 and free:
                        free(t)
                    for kk in range(k0, k1):
                        c = slice((kk - k0) * width, (kk - k0 + 1) * width)
                        yh, yl = yhi[:, kk, t * P:t * P + P], ylo[:, kk, t * P:t * P + P]
                        T.matmul(out(t), yh, whi[:, s, c], start=(kk == 0), stop=False)
                        T.matmul(out(t), yh, wlo[:, s, c], start=False, stop=False)
                        last = T.matmul(out(t), yl, whi[:, s, c], start=False, stop=(kk == KT - 1))
                last.then_inc(unit_used, 1)

            for r in range(3):
                wide(U_VV + r, 3 * r, min(3 * r + 3, KT), VV, lambda t: ps[:, 4 + t, 0:VV])
            for j in range(8):
                if j >= 4:
                    pe.wait_ge(conv_done, j - 3)
                col_unit(U_XBC + j, j % 4).then_inc(unit_used, 1)
                if j == 1:
                    pe.wait_ge(da_done, 1)
                    pe.wait_ge(v_out, TT)
                    pe.wait_ge(consts_made, 2)
                    T.matmul(ps[:, 4, 0:32], small["U"][:], sm[:, 13, :], start=True, stop=True).then_inc(cums_done, 1)
                    T.matmul(ps[:, 4, 32:64], ones[:], sm[:, 13, :], start=True, stop=True).then_inc(cums_done, 1)
            for j in range(2):
                pe.wait_ge(conv_done, 5 + j)
                col_unit(U_C + j, j).then_inc(unit_used, 1)
            pe.wait_ge(dst_in, 1)
            pe.wait_ge(ssm_exp, 2)
            for r in range(4):
                wide(U_Z + r, 2 * r, 2 * r + 2, 512, lambda t: ps[:, 4 + t, :])
            pe.wait_ge(blk_done, 16)
            pe.wait_ge(c_out, 1)
            for y, w1t in ((0, w1k), (1, w1v)):
                for ht in range(2):
                    c0 = (2 * y + ht) * 2 * N_CMP
                    for pr in range(16):
                        last = T.matmul(ps[:, 0, c0:c0 + 2 * N_CMP], w1t[:, pr, ht * P:ht * P + P], blk[:, y, pr, :],
                                        start=(pr == 0), stop=(pr == 15))
            last.then_inc(cmp_hid, 1)
            pe.wait_ge(conv_done, 7)
            col_unit(U_KS, 2).then_inc(unit_used, 1)
            pe.wait_ge(c_out, 2)
            pe.wait_ge(cmp_silu, 1)
            for e in range(2):
                for ht in range(2):
                    T.matmul(ps[64 * e:64 * e + 64, 1, 0:2 * N_CMP], w2s[:, 0, ht, :], hidc[:, 0, ht, :],
                             start=(ht == 0), stop=(ht == 1))
            for g in range(2):
                for ht in range(2):
                    last = T.matmul(ps[0:N_CMP, 1, 128 + 64 * g:192 + 64 * g],
                                    hidc[:, 1, ht, N_CMP * g:N_CMP * g + N_CMP], w2s[:, 1, ht, :],
                                    start=(ht == 0), stop=(ht == 1))
            last.then_inc(cmp_kv, 1)
            pe.wait_ge(conv_done, 8)
            col_unit(U_KS + 1, 3).then_inc(unit_used, 1)
            pe.wait_ge(xbc_ready, 8)
            pe.wait_ge(cmp_out, 1)
            for c in range(TT):
                if c < 2:
                    pe.wait_ge(ka_out, 2 * c + 2)
                    pe.wait_ge(kd_out, 2 * c + 2)
                else:
                    pe.wait_ge(xn_out, c - 1)
                    pe.wait_ge(bn_out, c - 1)
                for j in range(4):
                    T.transpose(ps[:, c % 2, j * P:j * P + P], xbcT[:, j, c * P:c * P + P], ident[:])
                for g in range(2):
                    last = T.transpose(ps[:, 2 + c % 2, g * P:g * P + P], xbcT[:, 4 + g, c * P:c * P + P], ident[:])
                last.then_inc(xb_tr, 1)
            av = sm[:, 13, :]

            def segments(c):
                tok = slice(c * P, c * P + P)
                if c:
                    pe.wait_ge(dec_done, 8 * c)
                    pe.wait_ge(m_done, 2 * c)
                for g in range(2):
                    T.matmul(ps[:, g, :].rearrange("p (q n) -> p q n", q=4), ident_bf[:],
                             mneg[:].unsqueeze(1).broadcast_to([P, 4, P]), start=True, stop=False)
                    for q in range(4):
                        col = 8 * c + 4 * g + q
                        last = T.matmul(ps[:, g, q * P:q * P + P], av[:, col:col + 1].broadcast_to([P, P]),
                                        small["U"][:], start=False, stop=(q == 3))
                for g in range(2):
                    last = T.matmul(ps[:, 2, P * g:P * g + P], xbcT[:, 4 + g, tok], xbcT[:, 6 + g, tok],
                                    start=True, stop=True)
                last.then_inc(ssm_seg, 1)

            pe.wait_ge(xn_out, TT)
            pe.wait_ge(bn_out, TT)
            pe.wait_ge(consts_made, 4)
            segments(0)
            for c in range(TT):
                tok = slice(c * P, c * P + P)
                if c == 0:
                    pe.wait_ge(z_ready, 4)
                elif c >= 2:
                    pe.wait_ge(q_out, c - 1)
                col_unit(U_Q + c, 6 + c % 2).then_inc(unit_used, 1)
                pe.wait_ge(xd_done, c + 1)
                if c:
                    pe.wait_ge(y_gated, 2 * c)
                for g in range(2):
                    T.matmul(ps[:, 4, 256 * g:256 * g + 256], xbcT[:, 6 + g, tok], prev[:, 256 * g:256 * g + 256],
                             start=True, stop=True)
                    T.matmul(ps[:, 5, 256 * g:256 * g + 256], BN[:, c, P * g:P * g + P],
                             xdd[:, 256 * g:256 * g + 256], start=True, stop=True)
                pe.wait_ge(m_done, 2 * (c + 1))
                for hd in range(HEADS):
                    last = T.matmul(ps[:, 3, 64 * hd:64 * hd + 64], Mt[:, hd, :], xdt[:, 64 * hd:64 * hd + 64],
                                    start=True, stop=True)
                last.then_inc(ssm_mm, 1)
                if c < TT - 1:
                    segments(c + 1)

            widths = [(3, 0), (2, 512), (0, 896), (1, 1024)]
            where = {3: (0, 0), 2: (1, 0), 0: (1, 384), 1: (2, 0)}
            p_off = dict(widths)
            tr = {0: (3, 0, 0), 1: (4, 0, 512), 3: (4, 384, 896), 2: (5, 0, 1024)}

            def scores(j):
                hd, kind = j // 2, j % 2
                e, g = hd % 2, hd // 4
                rws = slice(64 * e, 64 * e + 64)
                if j:
                    pe.wait_ge(biased, 4 * j)
                    pe.wait_ge(cbiased, (j + 1) // 2)
                for qt, _ in widths:
                    bk, c0 = where[qt]
                    w = (qt + 1) * P
                    last = T.matmul(ps[:, bk, c0:c0 + w], qT[rws, hd // 2, qt * P:qt * P + P],
                                    ksD[rws, kind, g, 0:w], start=True, stop=True)
                if kind == 0:
                    for qt in range(TT):
                        last = T.matmul(ps[:, 2, 256 + N_CMP * qt:256 + N_CMP * (qt + 1)],
                                        qT[rws, hd // 2, qt * P:qt * P + P], kcb[rws, g, :], start=True, stop=True)
                last.then_inc(qk_done, 1)

            def values(j):
                hd, b = j // 2, j % 2
                e, g = hd % 2, hd // 4
                pe.wait_ge(pt_act, 2 * (j + 1))
                pe.wait_ge(pt_dve, (3 * (j + 1) + 1) // 2)
                if j % 4 == 0 and j:
                    pe.wait_ge(mixa_lo, j // 4)
                o = slice(64 * e, 64 * e + 64)
                for kt in (range(TT) if b == 0 else reversed(range(TT))):
                    c0 = tr[kt][2]
                    w = SEQ - kt * P
                    last = T.matmul(ps[o, 7, kt * P:SEQ], vN[:, kt, P * b + 64 * g:P * b + 64 * g + 64],
                                    probT[:, b, c0:c0 + w], start=(kt == 0 and b == 0), stop=(kt == 0 and b == 1))
                if b == 0:
                    last = T.matmul(ps[o, 7, :], vcb[0:N_CMP, g, :], pcT[0:N_CMP, :], start=False, stop=False)
                last.then_inc(pv_done, 1)

            pe.wait_ge(cmp_out, 1)
            pe.wait_ge(dec_done, 8 * TT)
            pe.wait_ge(m_done, 2 * TT)
            pe.wait_ge(q_out, 4)
            scores(0)
            pe.wait_ge(yn_done, 8)
            for j in range(4):
                for c in range(TT):
                    last = T.transpose(ps[:, 3 + j, c * P:c * P + P], zN[:, c, j * P:j * P + P], ident[:])
            last.then_inc(y_tr, 1)
            for j in range(2 * HEADS):
                hd, b = j // 2, j % 2
                if j + 1 < 2 * HEADS:
                    scores(j + 1)
                if j == 0:
                    pe.wait_ge(mixs_lo, 4)
                pe.wait_ge(scaled, 5 * (j + 1))
                if j:
                    pe.wait_ge(pt_act, 2 * j)
                    pe.wait_ge(pt_dve, (3 * j + 1) // 2)
                for kt in range(TT):
                    bk, c0, _ = tr[kt]
                    for qt in range(kt, TT):
                        last = T.transpose(ps[:, bk, c0 + (qt - kt) * P:c0 + (qt - kt) * P + P],
                                           prob[:, b, p_off[qt] + kt * P:p_off[qt] + kt * P + P], ident[:])
                if b == 0:
                    for qt in range(TT):
                        last = T.transpose(ps[0:N_CMP, 6, qt * P:qt * P + P], pc[:, qt, :], ident[:])
                last.then_inc(p_tr, 1)
                if j:
                    values(j - 1)
            values(2 * HEADS - 1)
            pe.wait_ge(mixa_lo, PAIRS)
            rows(0, U_OUT0, KT, yhi, ylo, 4)
            if stop == 1:
                return

            def ffn(layer, k, m, u_gu, u_dn):
                f_base = FT * layer
                def tile(i, e, first):
                    u = u_gu + 2 * e
                    if not first:
                        pe.wait_ge(mult_done, f_base + 2 * i + e - 1)
                    col_unit(u, 2 * e, i).then_inc(unit_used, 1)
                    col_unit(u + 1, 2 * e + 1, i).then_inc(unit_used, 1)

                for e in range(2):
                    tile(0, e, True)
                with pe.Fori(1, FT // 2) as i:
                    for e in range(2):
                        tile(i, e, False)
                pe.wait_ge(hidlo_done, f_base + 2)
                rows(m, u_dn, FT, hidhi, hidlo, 2,
                     free={2: lambda: pe.wait_ge(mult_done, f_base + FT)}, staged_base=48 * 0 + (0 if layer == 0 else 32 + 16))
                return

            ffn(0, 1, 1, U_GU0, U_DN0)
            if stop == 2:
                return
            pe.wait_ge(ws_masked, 1)
            for g in range(8):
                last = T.transpose(ps[:, 4 + g // 4, (g % 4) * P:(g % 4) * P + P], ws[:, g, :], ident[:])
            last.then_inc(ws_tr, 1)
            pe.wait_ge(ws_out, 1)
            for b in range(2):
                last = T.matmul(ps[:, 6 + b, :], ones[:], wsT[:, 4 * b:4 * b + 4, :].rearrange("p g t -> p (g t)"),
                                start=True, stop=True)
            last.then_inc(rowsum_done, 1)
            for qr in range(4):
                if qr == 1:
                    pe.wait_ge(r_done, WT)
                for j in range(4):
                    u = U_V + 4 * qr + j
                    ready(u)
                    s = u % SLOTS
                    for t in range(TT):
                        if qr >= 2 and j == 0:
                            pe.wait_ge(vgelu_done, 4 * (qr - 2) + t + 1)
                        bank = 4 * (qr % 2) + t
                        for b in range(2):
                            kk = 2 * j + b
                            c = slice(512 * b, 512 * b + 512)
                            yh, yl = yhi[:, kk, t * P:t * P + P], ylo[:, kk, t * P:t * P + P]
                            T.matmul(ps[:, bank, :], yh, whi[:, s, c], start=(kk == 0), stop=False)
                            T.matmul(ps[:, bank, :], yh, wlo[:, s, c], start=False, stop=False)
                            last = T.matmul(ps[:, bank, :], yl, whi[:, s, c], start=False, stop=(kk == KT - 1))
                        if j == 3 and t < TT - 1:
                            last.then_inc(v_done, 1)
                    last.then_inc(unit_used, 1)
            pe.wait_ge(vgelu_done, 16)
            col_unit(U_U, 0).then_inc(unit_used, 1)
            pe.wait_ge(vnorm_done, 4)
            for j in range(WT):
                if j >= 4:
                    pe.wait_ge(mixed_done, j - 3)
                for c in range(TT):
                    last = T.matmul(ps[:, 2 + j % 4, c * P:c * P + P], vG[:, c, j * P:j * P + P], wsT[:, j // 2, :],
                                    start=True, stop=True)
                last.then_inc(mix_mm, 1)
            for j in range(1, WT):
                if j >= 2:
                    pe.wait_ge(ugelu_done, j - 1)
                col_unit(U_U + j, j % 2).then_inc(unit_used, 1)
            pe.wait_ge(mixed_done, WT)
            pe.wait_ge(glo_done, 4)
            rows(2, U_OUT1, WT, ghi, glo, 4, free={2: lambda: pe.wait_ge(ugelu_done, WT)}, staged_base=32)
            if stop == 3:
                return
            ffn(1, 3, 3, U_GU1, U_DN1)
    return nc


def column_units(w):
    n = w.shape[1] // P
    return w.reshape(KT, P, n, P).transpose(2, 1, 0, 3).reshape(n, P, UNIT)


def row_units(w):
    return w.reshape(-1, P, UNIT)


def wide_units(w, c0, width):
    k = UNIT // width
    return w[:, c0:c0 + width].reshape(KT // k, k, P, width).transpose(0, 2, 1, 3).reshape(KT // k, P, UNIT)


def kernel(x, norm_gains, ffn_w_gate, ffn_w_up, ffn_w_down, ev_w_in, ev_w_out, nsa_cmp_pe, nsa_cmp_w1, nsa_cmp_w2,
           ssm_conv_w, ssm_conv_b, ssm_dt_bias, ssm_a_log, ssm_d, ssm_norm_w, od_w_in, od_ln_w, od_ln_b, od_w_s,
           od_b_s, od_w_out):
    import concourse.bacc as bacc
    from concourse import mybir
    from concourse.bass_utils import run_bass_kernel_spmd

    def ffn_units(layer):
        gu = np.stack([column_units(ffn_w_gate[layer]), column_units(ffn_w_up[layer])], axis=1)
        return [gu.reshape(2 * FT, P, UNIT), row_units(ffn_w_down[layer])]

    w_in, g_in = ev_w_in[0], od_w_in[0]
    v2 = np.concatenate([w_in[:, c:c + n] for c, n in ((C_VS, P), (C_VW, P), (C_GATE, N_GATE), (C_DT, HEADS))], axis=1)
    v2 = np.concatenate([v2, np.zeros((P, VV), v2.dtype)], axis=0).reshape(3, 3, P, VV).transpose(0, 2, 1, 3)
    v2 = np.concatenate([v2.reshape(3, P, 3 * VV), np.zeros((3, P, UNIT - 3 * VV), v2.dtype)], axis=2)

    def columns(*firsts):
        return column_units(np.concatenate([w_in[:, c:c + P] for c in firsts], axis=1))

    stream = np.concatenate(
        [v2, columns(*range(C_XBC, C_XBC + 1024, P)), columns(C_KC, C_VC), wide_units(w_in, C_Z, 512),
         columns(C_KS, C_KW), columns(*range(C_Q, C_Q + 512, P)), row_units(ev_w_out[0])]
        + ffn_units(0)
        + [wide_units(g_in, WIDTH + 512 * q, 512) for q in range(4)]
        + [column_units(g_in[:, 0:WIDTH]), row_units(od_w_out[0])]
        + ffn_units(1), axis=0)
    pe = nsa_cmp_pe[0].transpose(2, 0, 1).reshape(HEAD_DIM, 2 * CMP_BLOCK)
    cols = np.concatenate(
        [ssm_conv_w[0].reshape(CONV_TAPS, 8, P).transpose(2, 0, 1).reshape(P, 32), ssm_conv_b[0].reshape(8, P).T,
         ssm_norm_w[0].reshape(4, P).T, np.concatenate([pe, pe], axis=0), od_ln_w[0].reshape(WT, P).T,
         od_ln_b[0].reshape(WT, P).T], axis=1)

    nc = bacc.Bacc("TRN2", target_bir_lowering=False, num_devices=1)
    arrays, args = {}, []
    for name, v in (("x", x), ("gains", norm_gains), ("stream", stream), ("cols", cols),
                    ("w1", nsa_cmp_w1), ("w2", nsa_cmp_w2), ("dt_bias", ssm_dt_bias), ("a_log", ssm_a_log),
                    ("d_skip", ssm_d), ("w_s", od_w_s), ("b_s", od_b_s)):
        arrays["in_" + name] = np.ascontiguousarray(v)
        args.append(nc.dram_tensor("in_" + name, v.shape, mybir.dt.float32, kind="ExternalInput").ap())
    out = nc.dram_tensor("out_h", (1, SEQ, D_MODEL), mybir.dt.float32, kind="ExternalOutput").ap()
    build(nc, *args, out)
    r = run_bass_kernel_spmd(nc, [arrays], core_ids=[0])
    return r.results[0]["out_h"]
```

```python
import numpy as np

D_MODEL = 1024
SEQ = 512
RMS_EPS, LN_EPS = 1e-6, 1e-5
HEADS, GROUPS, HEAD_DIM = 8, 2, 64
CMP_BLOCK, CMP_STRIDE, CMP_HIDDEN = 32, 16, 256
N_CMP = (SEQ - CMP_BLOCK) // CMP_STRIDE + 1
SSM_INNER, SSM_STATE, CONV_TAPS = 512, 128, 4
WIDTH = 2 * D_MODEL
FFN = 2816

P = 128
KT = D_MODEL // P
TT = SEQ // P
FT = FFN // P
WT = WIDTH // P
SLOTS = 4
UNIT = 1024
TAIL = 4

U_VV = 0
U_XBC = U_VV + 3
U_C = U_XBC + 8
U_Z = U_C + 2
U_KS = U_Z + 4
U_Q = U_KS + 2
U_OUT0 = U_Q + 4
U_GU0 = U_OUT0 + KT
U_DN0 = U_GU0 + 2 * FT
U_V = U_DN0 + FT
U_U = U_V + WT
U_OUT1 = U_U + WT
U_GU1 = U_OUT1 + WT
U_DN1 = U_GU1 + 2 * FT
U_END = U_DN1 + FT
ROWS_END = (U_GU0, U_V, U_GU1, U_END)

C_Q, C_KC, C_VC, C_KS, C_VS, C_KW, C_VW, C_GATE, C_Z, C_XBC, C_DT = (
    0, 512, 640, 768, 896, 1024, 1152, 1280, 1304, 1816, 2840)
N_GATE = 3 * HEADS
VV = 256 + N_GATE + HEADS
COLS0 = 32 + 8 + 4 + 64
MASKED = 1e33
C_PAD = N_CMP + N_CMP % 2
FLOOR = 1e29


def build(nc, x, gains, stream, cols, w1, w2, dt_bias, a_log, d_skip, w_s, b_s, out):
    from contextlib import ExitStack

    import concourse.bass as bass
    from concourse import mybir

    f32, f32r, bf16 = mybir.dt.float32, mybir.dt.float32r, mybir.dt.bfloat16
    ALU = mybir.AluOpType
    ACT = mybir.ActivationFunctionType
    AX = mybir.AxisListType
    ds = bass.ds

    base = [16512 // 4]

    def at(name, shape, dt=f32, where=None):
        size = int(np.prod(shape[1:])) * (2 if dt is bf16 else 4)
        if where is None:
            where = base[0]
            base[0] += -(-size // 32) * 8
            assert base[0] * 4 <= 229344, (name, base[0] * 4)
        return nc.alloc_sbuf_tensor_at(name, list(shape), dt, offset=where * 4)

    h = at("h", [P, TT, D_MODEL])
    yhi = at("yhi", [P, KT, SEQ], f32r)
    ylo = at("ylo", [P, KT, SEQ], f32r)
    raw = at("raw", [P, SLOTS, UNIT])
    whi = at("whi", [P, SLOTS, UNIT], f32r)
    wlo = at("wlo", [P, SLOTS, UNIT], f32r)
    tmp_at = base[0]
    tmp = at("tmp", [P, 4, SEQ])
    hn = at("hn", [P, 2, D_MODEL], where=tmp_at)
    gain_pre = at("gain_pre", [P, D_MODEL])
    post_at = base[0]
    gain_post = at("gain_post", [P, D_MODEL])
    w2s = at("w2s", [P, 2, 2, HEAD_DIM], where=post_at + 512)
    hidc = at("hidc", [P, 2, 2, 2 * N_CMP], where=post_at + 768)
    junk = at("junk", [P, D_MODEL], bf16)
    ident = at("ident", [P, P])
    stat = at("stat", [P, 4, 16])
    rst_t = at("rst_t", [P, 4, 16])
    half = at("half", [P, 8])
    arena = base[0]
    ARENA = FT * SEQ * 2
    hidhi = at("hidhi", [P, FT, SEQ], f32r)
    hidlo = at("hidlo", [P, FT, SEQ], f32r)

    a = [arena]

    def inner(name, shape, dt=f32, where=None):
        w = a[0] if where is None else where
        t = at(name, shape, dt, where=w)
        if where is None:
            a[0] += -(-int(np.prod(shape[1:])) // 8) * 8
            assert a[0] <= arena + ARENA, (name, a[0] - arena - ARENA)
        return t

    q_even = inner("q_even", [P, 4, SEQ], f32r)
    k_at = a[0]
    ksD = inner("ksD", [P, 2, GROUPS, SEQ])
    vN = inner("vN", [P, TT, 256])
    bias_at = a[0]
    bias = inner("bias", [P, HEADS, SEQ])
    w1v = inner("w1v", [P, 16, CMP_HIDDEN], where=bias_at)
    klo = inner("klo", [P, 2, GROUPS, SEQ], f32r, where=k_at)
    kh0 = at("kh0", [P, 2, SEQ], f32r, where=tmp_at + 2 * SEQ)
    xbc_at = a[0]
    xbcT = inner("xbcT", [P, 8, SEQ])
    q_odd = inner("q_odd", [P, 4, SEQ], f32r, where=xbc_at)
    kh1 = inner("kh1", [P, 2, SEQ], f32r, where=xbc_at + 4 * SEQ)
    zN = inner("zN", [P, TT, SSM_INNER])
    early_at = a[0]
    w1k = inner("w1k", [P, 16, CMP_HIDDEN])
    blk = inner("blk", [P, 2, 16, 2 * N_CMP])
    cT = inner("cT", [P, 2, SEQ])
    late = early_at
    xN = inner("xN", [P, TT, SSM_INNER], where=late); late += 2048
    BN = inner("BN", [P, TT, 256], where=late); late += 1024
    dec = inner("dec", [P, HEADS, P], where=late); late += 1024
    Mt = inner("Mt", [P, HEADS, P], where=late); late += 1024
    xdt = inner("xdt", [P, SSM_INNER], where=late); late += 512
    xdd = inner("xdd", [P, SSM_INNER], where=late); late += 512
    prev = inner("prev", [P, SSM_INNER], where=late); late += 512
    assert late <= a[0]
    small = {}
    for nm, n in (("cols", COLS0), ("dtb", 8), ("alog", 8),
                  ("dsk", 8), ("U", 128)):
        small[nm] = at("c_" + nm, [P, n])
    mneg = at("mneg", [P, P], bf16)
    ident_bf = at("ident_bf", [P, P], bf16)
    small["cw"], small["cb"] = small["cols"][:, 0:32], small["cols"][:, 32:40]
    small["nw"], small["pe2"] = small["cols"][:, 40:44], small["cols"][:, 44:108]
    kch = inner("kch", [P, GROUPS, C_PAD], f32r, where=late)
    kcl = inner("kcl", [P, GROUPS, C_PAD], f32r, where=late + 320)
    vcb = inner("vcb", [P, GROUPS, HEAD_DIM], where=late + 64)
    dcmp = inner("dcmp", [P, TT, N_CMP], where=late + 192)
    assert late + 384 <= arena + ARENA
    sm = at("sm", [P, 16, 32])
    gates = at("gates", [P, TT, N_GATE])
    ones = at("ones", [P, P])
    pr_at = early_at
    prob = inner("prob", [P, 2, 1280], where=pr_at)
    probT = inner("probT", [P, 2, 1280], where=pr_at + 2560)
    pc = inner("pc", [P, TT, N_CMP], where=pr_at + 5120)
    pcT = inner("pcT", [P, SEQ], where=pr_at + 5120 + 128)
    att = inner("att", [P, 8, 8], where=pr_at + 5120 + 128 + 512)
    assert pr_at + 5120 + 128 + 512 + 64 <= arena + ARENA
    vG = at("vG", [P, TT, WIDTH], where=arena)
    glo = at("glo", [P, WT, SEQ], f32r, where=arena)
    mixed = at("mixed", [P, WT, SEQ], where=arena + 8192)
    ghi = at("ghi", [P, WT, SEQ], f32r, where=arena + 8192)
    Rt = at("Rt", [P, WT, P], where=arena + 16384)
    ws = at("ws", [P, 8, P], where=arena + 18432)
    wsT = at("wsT", [P, 8, P], where=arena + 19456)
    bsbc = at("bsbc", [P, 8, P], where=arena + 20480)
    lncols = at("lncols", [P, 2 * WT], where=arena + 21504)
    lnw, lnb = lncols[:, 0:WT], lncols[:, WT:2 * WT]
    vstat = at("vstat", [P, TT, 4, 6], where=arena + 21504 + 32)
    vmv = at("vmv", [P, TT, 8], where=arena + 21504 + 32 + 96)

    ctx = ExitStack()
    with ctx:
        ps = ctx.enter_context(nc.psum_tensor("ps", [P, 8, 512], f32))

        def sem(name):
            return ctx.enter_context(nc.semaphore(name))

        raw_loaded = [sem(f"raw_loaded{i}") for i in range(SLOTS)]
        hi_done, lo_done, unit_used = sem("hi_done"), sem("lo_done"), sem("unit_used")
        x_loaded = [sem(f"x_loaded{i}") for i in range(TT)]
        gain_pre_loaded, gain_post_loaded = sem("gain_pre_loaded"), sem("gain_post_loaded")
        consts_loaded, cmp_loaded, gmlp_loaded = sem("consts_loaded"), sem("cmp_loaded"), sem("gmlp_loaded")
        dve_step, pool_step = sem("dve_step"), sem("pool_step")
        consts_made = sem("consts_made")
        presq_done, prerstd_done, hn_done, transposed = (
            sem("presq_done"), sem("prerstd_done"), sem("hn_done"), sem("transposed"))
        yhi_done, ylo_done = sem("yhi_done"), sem("ylo_done")
        rows_done, postsq_done, postrstd_done, scaled_done, h_ready = (
            sem("rows_done"), sem("postsq_done"), sem("postrstd_done"), sem("scaled_done"), sem("h_ready"))
        silu_done, mult_done, hidhi_done, hidlo_done = (
            sem("silu_done"), sem("mult_done"), sem("hidhi_done"), sem("hidlo_done"))
        staged = sem("staged")
        q_lo, k1_hi, k1_lo = sem("q_lo"), sem("k1_hi"), sem("k1_lo")
        q_out, ka_out, kd_out, c_out, v_out = sem("q_out"), sem("ka_out"), sem("kd_out"), sem("c_out"), sem("v_out")
        conv_done, xbc_ready, z_ready = sem("conv_done"), sem("xbc_ready"), sem("z_ready")
        blk_done, cmp_hid, cmp_silu, cmp_kv, cmp_out, bias_done = (
            sem("blk_done"), sem("cmp_hid"), sem("cmp_silu"), sem("cmp_kv"), sem("cmp_out"), sem("bias_done"))
        gate_exp, sp_exp, sp_ln, a_exp, dt_in, dt_w, da_done = (
            sem("gate_exp"), sem("sp_exp"), sem("sp_ln"), sem("a_exp"), sem("dt_in"), sem("dt_w"), sem("da_done"))
        cums_done, dst_in, ssm_exp = sem("cums_done"), sem("dst_in"), sem("ssm_exp")
        xb_tr, xn_out, bn_out = sem("xb_tr"), sem("xn_out"), sem("bn_out")
        ssm_seg, dec_done, m_done, xd_done, ssm_mm, y_gated = (
            sem("ssm_seg"), sem("dec_done"), sem("m_done"), sem("xd_done"), sem("ssm_mm"),
            sem("y_gated"))
        ysq_done, yr_done, yn_done, y_tr, mixs_hi, mixs_lo = (
            sem("ysq_done"), sem("yr_done"), sem("yn_done"), sem("y_tr"), sem("mixs_hi"), sem("mixs_lo"))
        qk_done, biased, cbiased, exp_done, cexp_done, scaled, p_tr, pt_act, pt_dve, pv_done, mixa_hi, mixa_lo = (
            sem("qk_done"), sem("biased"), sem("cbiased"), sem("exp_done"), sem("cexp_done"), sem("scaled"),
            sem("p_tr"), sem("pt_act"), sem("pt_dve"), sem("pv_done"), sem("mixa_hi"), sem("mixa_lo"))
        ws_masked, ws_tr, ws_out, rowsum_done, r_done = (
            sem("ws_masked"), sem("ws_tr"), sem("ws_out"), sem("rowsum_done"), sem("r_done"))
        v_done, vgelu_done, vmv_done, vrstd_done, vnorm_done = (
            sem("v_done"), sem("vgelu_done"), sem("vmv_done"), sem("vrstd_done"), sem("vnorm_done"))
        mix_mm, mixed_done, ugelu_done, g_done, ghi_done, glo_done = (
            sem("mix_mm"), sem("mixed_done"), sem("ugelu_done"), sem("g_done"), sem("ghi_done"), sem("glo_done"))
        out_written = sem("out_written")
        block = ctx.enter_context(nc.Block())

        PAIRS = HEADS // 2

        def transposed_bank(k, t):
            return 2 * (TT - 1 - t) if k == 0 else 2 * t

        @block.sync
        def _(sp):
            def load(u, i=0):
                s = u % SLOTS
                if u >= SLOTS:
                    sp.wait_ge(lo_done, 4 * (u // 4 + i) + s - 3)
                src = stream[ds(4 * i + u, 1), :, :].rearrange("a p n -> (a p) n")
                sp.dma_start(raw[:, s, :], src).then_inc(raw_loaded[s], 16)

            def loads(u0, u1):
                turns = (u1 - u0) // 4
                if turns > 1:
                    with sp.Fori(0, turns) as i:
                        for j in range(4):
                            load(u0 + j, i)
                    u0 += 4 * turns
                for u in range(u0, u1):
                    load(u)

            def gain(dst, layer, k, signal):
                sp.dma_start(dst[:], gains[layer, k:k + 1, :].broadcast_to([P, D_MODEL])).then_inc(signal, 16)

            for t in range(TT):
                sp.dma_start(h[:, t, :], x[0].rearrange("(t p) d -> p t d", p=P)[:, t, :]).then_inc(x_loaded[t], 16)
                if t == 0:
                    gain(gain_pre, 0, 0, gain_pre_loaded)
            for u in range(4):
                load(u)
            c = small
            sp.dma_start(c["cols"][:], cols[:, 0:COLS0]).then_inc(consts_loaded, 16)
            sp.dma_start(c["dtb"][:], dt_bias[0:1, :].broadcast_to([P, HEADS])).then_inc(consts_loaded, 16)
            sp.dma_start(c["alog"][:], a_log[0:1, :].broadcast_to([P, HEADS])).then_inc(consts_loaded, 16)
            sp.dma_start(c["dsk"][:], d_skip[0:1, :].broadcast_to([P, HEADS])).then_inc(consts_loaded, 16)
            for u in range(4, 8):
                load(u)
            sp.dma_start(w1k[:], w1[0, 0].rearrange("(t p) n -> p t n", p=P)).then_inc(cmp_loaded, 16)
            sp.dma_start(w1v[:], w1[0, 1].rearrange("(t p) n -> p t n", p=P)).then_inc(cmp_loaded, 16)
            sp.dma_start(w2s[:].rearrange("p y k d -> p (y k) d"),
                         w2[0].rearrange("y (k p) d -> p (y k) d", p=P)).then_inc(cmp_loaded, 16)
            loads(8, U_GU0)
            sp.wait_ge(cmp_kv, 1)
            gain(gain_post, 0, 1, gain_post_loaded)
            sp.wait_ge(ylo_done, 4)
            gain(gain_pre, 0, 2, gain_pre_loaded)
            loads(U_GU0, U_GU0 + 4)
            sp.wait_ge(h_ready, 4)
            gain(gain_post, 0, 3, gain_post_loaded)
            sp.wait_ge(hn_done, 8)
            gain(gain_pre, 1, 0, gain_pre_loaded)
            loads(U_GU0 + 4, U_V)
            loads(U_V, U_V + 4)
            sp.wait_ge(h_ready, 8)
            gain(gain_post, 1, 1, gain_post_loaded)
            sp.wait_ge(hn_done, 12)
            gain(gain_pre, 1, 2, gain_pre_loaded)
            sp.dma_start(ws[:], w_s[0].rearrange("g t s -> t g s")).then_inc(gmlp_loaded, 16)
            for g in range(8):
                sp.dma_start(bsbc[:, g, :], b_s[0, g:g + 1, :].broadcast_to([P, P])).then_inc(gmlp_loaded, 16)
            sp.dma_start(lncols[:], cols[:, COLS0:COLS0 + 2 * WT]).then_inc(gmlp_loaded, 16)
            loads(U_V + 4, U_GU1)
            loads(U_GU1, U_GU1 + 4)
            sp.wait_ge(h_ready, 12)
            gain(gain_post, 1, 3, gain_post_loaded)
            loads(U_GU1 + 4, U_END)
            o3 = out[0].rearrange("(t p) d -> p t d", p=P)
            for t in range(TT):
                sp.wait_ge(h_ready, 3 * TT + t + 1)
                sp.dma_start(o3[:, t, :], h[:, t, :]).then_inc(out_written, 16)
            sp.wait_ge(out_written, 16 * TT)

        @block.scalar
        def _(act):
            def split_hi(u, i=0):
                s = u % SLOTS
                n = 4 * (u // 4 + i) + s
                act.wait_ge(raw_loaded[s], 16 * (u // 4 + i) + 16)
                if u >= SLOTS:
                    act.wait_ge(unit_used, n - 3)
                nc.scalar.activation(whi[:, s, :], raw[:, s, :], ACT.Copy).then_inc(hi_done, 1)

            junk_writer = []

            def junk_free(sem_, count):
                if junk_writer:
                    act.wait_ge(*junk_writer.pop())
                junk_writer.append((sem_, count))

            def post_square(m, t):
                n = 4 * m + t
                if t < TT - 1:
                    act.wait_ge(rows_done, 3 * m + t + 1)
                else:
                    act.wait_ge(unit_used, ROWS_END[m])
                junk_free(postsq_done, n + 1)
                nc.scalar.activation(junk[:], ps[:, 2 * t:2 * t + 2, :].rearrange("p b n -> p (b n)"), ACT.Square,
                                     accum_out=stat[:, 0, n:n + 1]).then_inc(postsq_done, 1)

            def pre_square(k, t):
                n = 4 * k + t
                if k == 0:
                    act.wait_ge(x_loaded[t], 16)
                else:
                    act.wait_ge(h_ready, n - 3)
                junk_free(presq_done, n + 1)
                nc.scalar.activation(junk[:], h[:, t, :], ACT.Square,
                                     accum_out=stat[:, 1, n:n + 1]).then_inc(presq_done, 1)

            def pre_hi(k, t):
                n = 4 * k + t
                act.wait_ge(transposed, n + 1)
                b0 = transposed_bank(k, t)
                nc.scalar.activation(yhi[:, :, t * P:t * P + P],
                                     ps[:, b0:b0 + 2, :].rearrange("p b (k n) -> p (b k) n", n=P),
                                     ACT.Copy).then_inc(yhi_done, 1)

            def boundary(m, u_next):
                if m == 3:
                    for t in range(TT):
                        post_square(m, t)
                    return
                for t in range(3):
                    post_square(m, t)
                    if t == 2:
                        split_hi(u_next)
                        split_hi(u_next + 1)
                        pre_hi(m + 1, 1)
                    pre_square(m + 1, t)
                    if t == 1:
                        pre_hi(m + 1, 0)
                post_square(m, 3)
                pre_square(m + 1, 3)
                pre_hi(m + 1, 2)
                pre_hi(m + 1, 3)
                split_hi(u_next + 2)
                split_hi(u_next + 3)

            pre_square(0, 0)
            pre_square(0, 1)
            pre_square(0, 2)
            pre_hi(0, 0)
            pre_square(0, 3)
            pre_hi(0, 1)
            split_hi(0)
            pre_hi(0, 2)
            split_hi(1)
            pre_hi(0, 3)
            for u in range(2, 4):
                split_hi(u)
            for u in range(4, U_XBC + 4):
                split_hi(u)
            act.wait_ge(unit_used, U_VV + 3)
            nc.scalar.activation(gates[:], ps[:, 4:8, 256:256 + N_GATE], ACT.Exp, scale=-1.0).then_inc(gate_exp, 1)
            act.wait_ge(dt_in, 1)
            nc.scalar.activation(sm[:, 2, :], sm[:, 1, :], ACT.Exp).then_inc(sp_exp, 1)
            nc.scalar.activation(sm[:, 3, 0:8], small["alog"][:], ACT.Exp).then_inc(a_exp, 1)
            act.wait_ge(dt_w, 1)
            nc.scalar.activation(sm[:, 5, :], sm[:, 4, :], ACT.Ln).then_inc(sp_ln, 1)
            split_hi(U_XBC + 4)
            act.wait_ge(cums_done, 2)
            nc.scalar.activation(sm[:, 9, :], ps[:, 4, 0:32], ACT.Exp).then_inc(ssm_exp, 1)
            nc.scalar.activation(sm[:, 10, :], ps[:, 4, 32:64], ACT.Exp).then_inc(ssm_exp, 1)
            act.wait_ge(dst_in, 1)
            nc.scalar.activation(sm[:, 11, :], sm[:, 12, :], ACT.Exp).then_inc(ssm_exp, 1)
            split_hi(U_XBC + 5)
            for j in range(8):
                act.wait_ge(conv_done, j + 1)
                nc.scalar.activation(xbcT[:, j, :], tmp[:, j % 2, :], ACT.Silu).then_inc(xbc_ready, 1)
                split_hi(U_XBC + 6 + j)
            for j in range(2):
                act.wait_ge(unit_used, U_C + j + 1)
                nc.scalar.copy(cT[:, j, :], ps[:, j, :]).then_inc(c_out, 1)
            for u in range(U_KS, U_Q + 2):
                split_hi(u)
            for t in range(TT):
                if t == 0:
                    act.wait_ge(unit_used, U_Z + 4)
                nc.scalar.activation(zN[:, t, :], ps[:, 4 + t, :], ACT.Silu).then_inc(z_ready, 1)
            act.wait_ge(cmp_hid, 1)
            nc.scalar.activation(hidc[:].rearrange("p a b n -> p (a b n)"), ps[:, 0, 0:8 * N_CMP],
                                 ACT.Silu).then_inc(cmp_silu, 1)
            for j in range(2):
                act.wait_ge(unit_used, U_KS + j + 1)
                for e in range(2):
                    nc.scalar.copy(kh0[64 * e:64 * e + 64, j, :], ps[0:64, 2 + j, :]).then_inc(ka_out, 1)
                split_hi(U_Q + 2 + j)
            for c in range(TT):
                act.wait_ge(xb_tr, c + 1)
                nc.scalar.copy(xN[:, c, :], ps[:, c % 2, :]).then_inc(xn_out, 1)

            def y_square(c):
                for g in range(2):
                    act.wait_ge(y_gated, 2 * c + 1)
                    junk_free(ysq_done, 2 * c + g + 1)
                    nc.scalar.activation(junk[:, 0:256], zN[:, c, 256 * g:256 * g + 256], ACT.Square,
                                         accum_out=stat[:, 2, 2 * c + g:2 * c + g + 1]).then_inc(ysq_done, 1)

            def q_hi(c):
                act.wait_ge(unit_used, U_Q + c + 1)
                nc.scalar.mul(q_even[0:64, c, :], ps[0:64, 6 + c % 2, :], -HEAD_DIM ** -0.5).then_inc(q_out, 1)
                nc.scalar.mul(q_odd[64:128, c, :], ps[64:128, 6 + c % 2, :], -HEAD_DIM ** -0.5).then_inc(q_out, 1)

            for c in range(TT):
                act.wait_ge(ssm_seg, c + 1)
                if c:
                    act.wait_ge(m_done, 2 * c)
                for hd in range(HEADS):
                    nc.scalar.activation(dec[:, hd, :], ps[:, hd // 4, (hd % 4) * P:(hd % 4) * P + P], ACT.Exp,
                                         bias=sm[:, 8, 8 * c + hd:8 * c + hd + 1]).then_inc(dec_done, 1)
                if c < TT - 1:
                    q_hi(c)
                    split_hi(U_OUT0 + c)
                if c:
                    y_square(c - 1)
            y_square(3)

            widths = [(3, 0), (2, 512), (0, 896), (1, 1024)]

            def exps(j):
                b = j % 2
                for idx, (qt, off) in enumerate(widths):
                    act.wait_ge(biased, 4 * j + idx + 1)
                    w = (qt + 1) * P
                    nc.scalar.activation(prob[:, b, off:off + w], prob[:, b, off:off + w], ACT.Exp,
                                         bias=att[:, b, qt:qt + 1], scale=-1.0,
                                         accum_out=att[:, 2 + b, qt:qt + 1]).then_inc(exp_done, 1)
                if j % 2 == 0:
                    act.wait_ge(cbiased, j // 2 + 1)
                    for qt in range(TT):
                        nc.scalar.activation(pc[:, qt, :], pc[:, qt, :], ACT.Exp, bias=att[:, 4, qt:qt + 1],
                                             scale=-1.0, accum_out=att[:, 5, qt:qt + 1]).then_inc(cexp_done, 1)

            exps(0)
            q_hi(TT - 1)
            for j in range(4):
                act.wait_ge(y_tr, 1)
                nc.scalar.activation(yhi[:, 4 + j, :], ps[:, 3 + j, :], ACT.Identity,
                                     scale=small["nw"][:, j:j + 1]).then_inc(mixs_hi, 1)
            nc.scalar.copy(kh1[:], ksD[:, :, 1, :]).then_inc(k1_hi, 1)
            split_hi(U_OUT0 + TT - 1)
            for j in range(2 * HEADS):
                if j % 4 == 1 and j > 1:
                    act.wait_ge(pv_done, j - 1)
                    nc.scalar.copy(yhi[:, j // 4 - 1, :], ps[:, 7, :]).then_inc(mixa_hi, 1)
                if j + 1 < 2 * HEADS:
                    exps(j + 1)
                act.wait_ge(p_tr, j + 1)
                if j >= 2:
                    act.wait_ge(pv_done, j - 1)
                nc.scalar.copy(probT[:, j % 2, 0:512], ps[:, 3, :]).then_inc(pt_act, 1)
                nc.scalar.copy(probT[:, j % 2, 1024:1280], ps[:, 5, 0:256]).then_inc(pt_act, 1)
                if j % 2 == 0:
                    nc.scalar.copy(pcT[0:N_CMP, :], ps[0:N_CMP, 6, :]).then_inc(pt_act, 1)
            act.wait_ge(pv_done, 2 * HEADS)
            nc.scalar.copy(yhi[:, PAIRS - 1, :], ps[:, 7, :]).then_inc(mixa_hi, 1)
            for r in range(4):
                split_hi(U_OUT0 + 4 + r)
            boundary(0, U_GU0)

            def ffn(layer, u_gu, u_dn):
                f_base = FT * layer

                def tile(i, e, first):
                    f = 2 * i + e
                    u = u_gu + 2 * e
                    n = 4 * (u // 4) + u % 4
                    act.wait_ge(unit_used, n + 4 * i + 1)
                    if not first:
                        act.wait_ge(mult_done, f_base + f - 1)
                    nc.scalar.activation(tmp[:, e, :], ps[:, 2 * e, :], ACT.Silu).then_inc(silu_done, 1)
                    split_hi(u + 4, i)
                    act.wait_ge(mult_done, f_base + f + 1)
                    nc.scalar.copy(hidhi[:, f, :] if first else hidhi[:, ds(f, 1), :].rearrange("p a n -> p (a n)"),
                                   tmp[:, 2 + e, :]).then_inc(hidhi_done, 1)
                    split_hi(u + 5, i)

                for e in range(2):
                    tile(0, e, True)
                with act.Fori(1, FT // 2) as i:
                    for e in range(2):
                        tile(i, e, False)
                for r in range(2):
                    split_hi(u_dn + 4 + r)
                with act.Fori(0, 3) as i:
                    for j in range(4):
                        split_hi(u_dn + 6 + j, i)
                for r in range(18, FT):
                    split_hi(u_dn + r)

            ffn(0, U_GU0, U_DN0)
            boundary(1, U_V)
            for qr in range(4):
                for j in range(3):
                    if qr == 0 and j == 2:
                        act.wait_ge(ws_tr, 1)
                        nc.scalar.copy(wsT[:].rearrange("p g t -> p (g t)"),
                                       ps[:, 4:6, :].rearrange("p b n -> p (b n)")).then_inc(ws_out, 1)
                    split_hi(U_V + 4 * qr + 4 + j)
                for t in range(TT):
                    if t < TT - 1:
                        act.wait_ge(v_done, 3 * qr + t + 1)
                    else:
                        act.wait_ge(unit_used, U_V + 4 * qr + 4)
                    nc.scalar.activation(vG[:, t, 512 * qr:512 * qr + 512], ps[:, 4 * (qr % 2) + t, :],
                                         ACT.Gelu).then_inc(vgelu_done, 1)
                    if t == 2:
                        split_hi(U_V + 4 * qr + 7)
            for j in range(WT):
                act.wait_ge(unit_used, U_U + j + 1)
                if j >= 2:
                    act.wait_ge(g_done, j - 1)
                nc.scalar.activation(tmp[:, j % 2, :], ps[:, j % 2, :], ACT.Gelu).then_inc(ugelu_done, 1)
                split_hi(U_U + j + 4)
                act.wait_ge(g_done, j + 1)
                nc.scalar.copy(ghi[:, j, :], tmp[:, 2 + j % 2, :]).then_inc(ghi_done, 1)
            for r in range(4, WT):
                split_hi(U_OUT1 + r)
            boundary(2, U_GU1)
            ffn(1, U_GU1, U_DN1)
            boundary(3, None)

        @block.gpsimd
        def _(pool):
            steps = [0]

            def step(ins):
                steps[0] += 1
                ins.then_inc(pool_step, 1)
                pool.wait_ge(pool_step, steps[0])

            def rstd(dst, src, scale, eps, done):
                step(nc.gpsimd.tensor_scalar(src, src, scale, eps, ALU.mult, ALU.add))
                n = src.shape[-1]
                nc.gpsimd.tensor_tensor(dst, src, half[:, 0:n], ALU.pow).then_inc(done, 1)

            def norms(k, done_sem, row, signal, t):
                n = 4 * k + t
                pool.wait_ge(done_sem, n + 1)
                c = slice(n % 16, n % 16 + 1)
                rstd(rst_t[:, row, c], stat[:, row, c], 1.0 / D_MODEL, RMS_EPS, signal)

            nc.gpsimd.memset(half[:], -0.5)
            nc.gpsimd.memset(ones[:], 1.0)
            step(nc.gpsimd.memset(ident[:], 0.0))
            nc.gpsimd.affine_select(out=ident[:], in_=ident[:], compare_op=ALU.not_equal, fill=1.0, base=0,
                                    pattern=[[-1, P]], channel_multiplier=1).then_inc(consts_made, 1)
            for t in range(TT):
                norms(0, presq_done, 1, prerstd_done, t)
            step(nc.gpsimd.memset(mneg[:], 0.0))
            nc.gpsimd.affine_select(out=small["U"][:], in_=ones[:], compare_op=ALU.is_ge, fill=0.0, base=0,
                                    pattern=[[1, P]], channel_multiplier=-1).then_inc(consts_made, 1)
            nc.gpsimd.affine_select(out=mneg[:], in_=mneg[:], compare_op=ALU.is_ge, fill=-1e30,
                                    base=0, pattern=[[1, P]], channel_multiplier=-1).then_inc(consts_made, 1)
            nc.gpsimd.tensor_copy(ident_bf[:], ident[:]).then_inc(consts_made, 1)
            pool.wait_ge(cmp_hid, 1)
            d0 = bias[:, HEADS - 1, :]
            step(nc.gpsimd.iota(d0, pattern=[[-1, SEQ]], base=SEQ - P, channel_multiplier=1,
                                allow_small_or_imprecise_dtypes=True))
            step(nc.gpsimd.affine_select(out=d0, in_=d0, compare_op=ALU.is_ge, fill=MASKED, base=SEQ - P,
                                         pattern=[[-1, SEQ]], channel_multiplier=1))
            for hd in range(HEADS):
                nc.gpsimd.tensor_scalar(bias[:, hd, :], d0, 2.0 ** -(hd + 1), None, ALU.mult).then_inc(bias_done, 1)
            step(nc.gpsimd.iota(dcmp[:], pattern=[[P, TT], [-CMP_STRIDE, N_CMP]], base=-(CMP_BLOCK - 1),
                                channel_multiplier=1, allow_small_or_imprecise_dtypes=True))
            nc.gpsimd.affine_select(out=dcmp[:], in_=dcmp[:], compare_op=ALU.is_ge, fill=MASKED,
                                    base=-(CMP_BLOCK - 1), pattern=[[P, TT], [-CMP_STRIDE, N_CMP]],
                                    channel_multiplier=1).then_inc(bias_done, 1)
            for c in range(TT):
                for g in range(2):
                    n = 2 * c + g
                    pool.wait_ge(ysq_done, n + 1)
                    rstd(rst_t[:, 2, n:n + 1], stat[:, 2, n:n + 1], 1.0 / 256, RMS_EPS, yr_done)

            def boundary(m):
                for t in range(TT):
                    norms(m, postsq_done, 0, postrstd_done, t)
                    if m < 3:
                        norms(m + 1, presq_done, 1, prerstd_done, t)

            def stage(kt, slot, hi, lo, u_prev, i):
                pool.wait_ge(unit_used, 4 * (u_prev // 4 + i) + u_prev % 4 + 1)
                nc.gpsimd.tensor_copy(yhi[:, slot, :], hi[:, ds(kt, 1), :].rearrange("p a n -> p (a n)")).then_inc(staged, 1)
                nc.gpsimd.tensor_copy(ylo[:, slot, :], lo[:, ds(kt, 1), :].rearrange("p a n -> p (a n)")).then_inc(staged, 1)

            def ffn_stage(layer, u_dn):
                pool.wait_ge(hidlo_done, FT * (layer + 1))
                with pool.Fori(0, 4) as i:
                    for j in range(4):
                        stage(4 * i + 2 + j, j % 2, hidhi, hidlo, u_dn + j, i)

            boundary(0)
            ffn_stage(0, U_DN0)
            boundary(1)
            pool.wait_ge(gmlp_loaded, 16 * 10)
            nc.gpsimd.affine_select(out=ws[:], in_=ws[:], compare_op=ALU.is_ge, fill=0.0, base=0,
                                    pattern=[[0, 8], [-1, P]], channel_multiplier=1).then_inc(ws_masked, 1)
            for t in range(TT):
                pool.wait_ge(vmv_done, t + 1)
                rstd(vmv[:, t, 2:3], vmv[:, t, 1:2], 1.0, LN_EPS, vrstd_done)
            pool.wait_ge(glo_done, WT)
            with pool.Fori(0, 2) as i:
                for j in range(4):
                    stage(4 * i + 4 + j, j % 2, ghi, glo, U_OUT1 + 2 + j, i)
            boundary(2)
            ffn_stage(1, U_DN1)
            boundary(3)

        @block.vector
        def _(dve):
            V = nc.vector
            steps = [0]

            def step(ins):
                steps[0] += 1
                ins.then_inc(dve_step, 1)
                dve.wait_ge(dve_step, steps[0])

            def split_lo(u, i=0):
                s = u % SLOTS
                dve.wait_ge(hi_done, 4 * (u // 4 + i) + s + 1)
                V.tensor_tensor(wlo[:, s, :], raw[:, s, :], whi[:, s, :].bitcast(f32), ALU.subtract).then_inc(lo_done, 1)

            def post_residual(m, t):
                n = 4 * m + t
                dve.wait_ge(postrstd_done, n + 1)
                if t == 0:
                    dve.wait_ge(gain_post_loaded, 16 * (m + 1))
                y = ps[:, 2 * t:2 * t + 2, :].rearrange("p b n -> p (b n)")
                V.scalar_tensor_tensor(y, y, rst_t[:, 0, n:n + 1], gain_post[:], ALU.mult,
                                       ALU.mult).then_inc(scaled_done, 1)
                dve.wait_ge(scaled_done, n + 1)
                V.tensor_tensor(h[:, t, :], h[:, t, :], y, ALU.add).then_inc(h_ready, 1)

            def pre_scale(k, t):
                n = 4 * k + t
                dve.wait_ge(prerstd_done, n + 1)
                if t == 0:
                    dve.wait_ge(gain_pre_loaded, 16 * (k + 1))
                if n >= 2:
                    dve.wait_ge(transposed, n - 1)
                V.scalar_tensor_tensor(hn[:, n % 2, :], h[:, t, :], rst_t[:, 1, n:n + 1], gain_pre[:], ALU.mult,
                                       ALU.mult).then_inc(hn_done, 1)

            def pre_lo(k, t):
                n = 4 * k + t
                dve.wait_ge(yhi_done, n + 1)
                sl = slice(t * P, t * P + P)
                b0 = transposed_bank(k, t)
                V.tensor_tensor(ylo[:, :, sl], ps[:, b0:b0 + 2, :].rearrange("p b (k n) -> p (b k) n", n=P),
                                yhi[:, :, sl].bitcast(f32), ALU.subtract).then_inc(ylo_done, 1)

            def boundary(m, u_next):
                if m == 3:
                    for t in range(TT):
                        post_residual(m, t)
                    return
                for t in range(3):
                    post_residual(m, t)
                    if t == 2:
                        split_lo(u_next)
                        pre_lo(m + 1, 1)
                    pre_scale(m + 1, t)
                    if t == 1:
                        pre_lo(m + 1, 0)
                post_residual(m, 3)
                split_lo(u_next + 1)
                pre_scale(m + 1, 3)
                pre_lo(m + 1, 2)
                pre_lo(m + 1, 3)
                split_lo(u_next + 2)
                split_lo(u_next + 3)

            pre_scale(0, 0)
            pre_scale(0, 1)
            pre_lo(0, 0)
            pre_scale(0, 2)
            pre_lo(0, 1)
            pre_scale(0, 3)
            split_lo(0)
            pre_lo(0, 2)
            split_lo(1)
            pre_lo(0, 3)
            for u in range(2, 4):
                split_lo(u)
            for u in range(4, U_XBC + 4):
                split_lo(u)
            dve.wait_ge(unit_used, U_VV + 3)
            dve.wait_ge(consts_loaded, 16 * 4)
            dtp = ps[:, 4:8, 256 + N_GATE:VV]

            def smv(k):
                return sm[:, k, :].rearrange("p (t n) -> p t n", t=TT)

            def rowbc(ap):
                return ap.unsqueeze(1).broadcast_to([P, TT, HEADS])

            dve.wait_ge(gate_exp, 1)
            step(V.tensor_tensor(smv(0), dtp, rowbc(small["dtb"][:]), ALU.add))
            step(V.tensor_scalar(sm[:, 1, :], sm[:, 0, :], -1.0, None, ALU.mult))
            V.tensor_tensor(sm[:, 1, :], sm[:, 1, :], sm[:, 0, :], ALU.min).then_inc(dt_in, 1)
            for t in range(TT):
                V.tensor_copy(vN[:, t, :], ps[:, 4 + t, 0:256]).then_inc(v_out, 1)
            gflat = gates[:].rearrange("p t n -> p (t n)")
            step(V.tensor_scalar(gflat, gflat, 1.0, None, ALU.add))
            V.reciprocal(gflat, gflat)
            dve.wait_ge(sp_exp, 1)
            V.tensor_scalar(sm[:, 4, :], sm[:, 2, :], 1.0, None, ALU.add).then_inc(dt_w, 1)
            dve.wait_ge(dt_w, 1)
            step(V.tensor_scalar(sm[:, 6, :], sm[:, 4, :], -1.0, 1e-30, ALU.add, ALU.add))
            step(V.reciprocal(sm[:, 6, :], sm[:, 6, :]))
            step(V.tensor_tensor(sm[:, 6, :], sm[:, 6, :], sm[:, 2, :], ALU.mult))
            dve.wait_ge(sp_ln, 1)
            step(V.scalar_tensor_tensor(sm[:, 6, :], sm[:, 5, :], 1e-30, sm[:, 6, :], ALU.add, ALU.mult))
            step(V.scalar_tensor_tensor(sm[:, 7, :], sm[:, 0, :], 0.0, sm[:, 6, :], ALU.max, ALU.add))
            dve.wait_ge(a_exp, 1)
            step(V.tensor_scalar(sm[:, 3, 0:8], sm[:, 3, 0:8], -1.0, None, ALU.mult))
            V.tensor_tensor(smv(13), smv(7), rowbc(sm[:, 3, 0:8]), ALU.mult).then_inc(da_done, 1)
            split_lo(U_XBC + 4)
            dve.wait_ge(cums_done, 2)
            dve.wait_ge(ssm_exp, 2)
            step(V.tensor_scalar(sm[:, 8, :], ps[:, 4, 0:32], -1.0, None, ALU.mult))
            V.tensor_tensor(sm[:, 12, :], sm[:, 8, :], ps[:, 4, 32:64], ALU.add).then_inc(dst_in, 1)
            split_lo(U_XBC + 5)
            cwv = small["cw"].rearrange("p (k c) -> p k c", k=CONV_TAPS)
            for j in range(8):
                dve.wait_ge(unit_used, U_XBC + j + 1)
                if j >= 2:
                    dve.wait_ge(xbc_ready, j - 1)
                src, acc = ps[:, j % 4, :], tmp[:, j % 2, :]
                step(V.tensor_scalar(acc, src, cwv[:, 3, j:j + 1], small["cb"][:, j:j + 1], ALU.mult, ALU.add))
                for lag in (1, 2, 3):
                    ins = V.scalar_tensor_tensor(acc[:, lag:], src[:, 0:SEQ - lag], cwv[:, 3 - lag, j:j + 1],
                                                 acc[:, lag:], ALU.mult, ALU.add)
                    if lag < 3:
                        step(ins)
                    else:
                        ins.then_inc(conv_done, 1)
                split_lo(U_XBC + 6 + j)
            dve.wait_ge(c_out, 2)
            dve.wait_ge(cmp_loaded, 16 * 3)
            for y in range(2):
                for g in range(2):
                    src = cT[64 * g:64 * g + 64, y, :].rearrange("p (b r) -> p r b", r=16)
                    pe3 = small["pe2"][64 * g:64 * g + 64, 32 * y:32 * y + 32]
                    for par in range(2):
                        for w in range(2):
                            pv = pe3[:, 16 * w + par:16 * w + 16:2].unsqueeze(2).broadcast_to([64, 8, N_CMP])
                            V.tensor_tensor(
                                blk[64 * par:64 * par + 64, y, 8 * w:8 * w + 8, N_CMP * g:N_CMP * g + N_CMP],
                                src[:, par::2, w:w + N_CMP], pv, ALU.add).then_inc(blk_done, 1)
            for u in range(U_KS, U_Q + 2):
                split_lo(u)
            def keys_out(kind):
                dve.wait_ge(unit_used, U_KS + kind + 1)
                for e in range(2):
                    V.tensor_copy(ksD[64 * e:64 * e + 64, kind, 1, :], ps[64:128, 2 + kind, :]).then_inc(kd_out, 1)
                dve.wait_ge(ka_out, 2 * kind + 2)
                for e in range(2):
                    V.tensor_tensor(klo[64 * e:64 * e + 64, kind, 0, :], ps[0:64, 2 + kind, :],
                                    kh0[0:64, kind, :].bitcast(f32), ALU.subtract).then_inc(kd_out, 1)

            keys_out(0)
            split_lo(U_Q + 2)
            dve.wait_ge(cmp_kv, 1)
            kc = ps[:, 1, 0:2 * N_CMP].rearrange("p (g c) -> p g c", g=GROUPS)
            step(V.tensor_copy(kch[:, :, 0:N_CMP], kc))
            V.tensor_tensor(kcl[:, :, 0:N_CMP], kc, kch[:, :, 0:N_CMP].bitcast(f32), ALU.subtract)
            dve.wait_ge(consts_made, 1)
            for part in (kch, kcl):
                one = ones[:, 0:GROUPS].unsqueeze(2)
                V.tensor_tensor(part[:, :, N_CMP:C_PAD], one, one, ALU.subtract)
            V.tensor_copy(vcb[0:N_CMP].rearrange("p g d -> p (g d)"), ps[0:N_CMP, 1, 128:256]).then_inc(cmp_out, 1)

            keys_out(1)
            split_lo(U_Q + 3)
            for c in range(TT):
                dve.wait_ge(xb_tr, c + 1)
                V.tensor_copy(BN[:, c, :], ps[:, 2 + c % 2, 0:256]).then_inc(bn_out, 1)
            dve.wait_ge(ssm_exp, 3)
            step(V.memset(prev[:], 0.0))

            def heads3(ap):
                return ap.rearrange("p (h d) -> p h d", h=HEADS)

            def colbc(k, c):
                return sm[:, k, 8 * c:8 * c + 8].unsqueeze(2).broadcast_to([P, HEADS, HEAD_DIM])

            def q_low(c):
                scale = -HEAD_DIM ** -0.5
                dve.wait_ge(q_out, 2 * c + 2)
                V.scalar_tensor_tensor(q_even[64:128, c, :], ps[0:64, 6 + c % 2, :], scale,
                                       q_even[0:64, c, :].bitcast(f32), ALU.mult, ALU.subtract).then_inc(q_lo, 1)
                V.scalar_tensor_tensor(q_odd[0:64, c, :], ps[64:128, 6 + c % 2, :], scale,
                                       q_odd[64:128, c, :].bitcast(f32), ALU.mult, ALU.subtract).then_inc(q_lo, 1)

            def y_norm(c):
                for g in range(2):
                    dve.wait_ge(yr_done, 2 * c + g + 1)
                    seg = zN[:, c, 256 * g:256 * g + 256]
                    V.tensor_scalar(seg, seg, rst_t[:, 2, 2 * c + g:2 * c + g + 1], None, ALU.mult).then_inc(yn_done, 1)

            for c in range(TT):
                if c == 0:
                    dve.wait_ge(xn_out, TT)
                if c:
                    dve.wait_ge(ssm_mm, c)
                step(V.tensor_tensor(heads3(xdt[:]), heads3(xN[:, c, :]), colbc(7, c), ALU.mult))
                V.tensor_tensor(heads3(xdd[:]), heads3(xdt[:]), colbc(11, c), ALU.mult).then_inc(xd_done, 1)
                dve.wait_ge(dec_done, 8 * (c + 1))
                for g in range(2):
                    cb = ps[:, 2, P * g:P * g + P].unsqueeze(1).broadcast_to([P, 4, P])
                    V.tensor_tensor(Mt[:, 4 * g:4 * g + 4, :], dec[:, 4 * g:4 * g + 4, :], cb,
                                    ALU.mult).then_inc(m_done, 1)
                if c < TT - 1:
                    q_low(c)
                    split_lo(U_OUT0 + c)
                t1, t2 = tmp[:, 0, :], tmp[:, 1, :]
                step(V.tensor_tensor(heads3(t2), heads3(xN[:, c, :]),
                                     small["dsk"][:].unsqueeze(2).broadcast_to([P, HEADS, HEAD_DIM]), ALU.mult))
                dve.wait_ge(ssm_mm, c + 1)
                step(V.tensor_tensor(heads3(t1), heads3(ps[:, 4, :]), colbc(9, c), ALU.mult))
                step(V.tensor_tensor(t1, t1, ps[:, 3, :], ALU.add))
                step(V.tensor_tensor(t1, t1, t2, ALU.add))
                if c == 0:
                    dve.wait_ge(z_ready, TT)
                V.tensor_tensor(zN[:, c, :], zN[:, c, :], t1, ALU.mult).then_inc(y_gated, 1)
                if c < TT - 1:
                    step(V.tensor_tensor(heads3(prev[:]), heads3(prev[:]), colbc(10, c), ALU.mult))
                    V.tensor_tensor(prev[:], prev[:], ps[:, 5, :], ALU.add).then_inc(y_gated, 1)
                    dve.wait_ge(y_gated, 2 * (c + 1))
                if c:
                    y_norm(c - 1)
            widths = [(3, 0), (2, 512), (0, 896), (1, 1024)]
            where = {3: (0, 0), 2: (1, 0), 0: (1, 384), 1: (2, 0)}

            def add_bias(j):
                hd, b = j // 2, j % 2
                dve.wait_ge(qk_done, j + 1)
                if j == 0:
                    dve.wait_ge(bias_done, HEADS + 1)
                if j >= 2:
                    dve.wait_ge(p_tr, j - 1)
                for qt, off in widths:
                    bk, c0 = where[qt]
                    w = (qt + 1) * P
                    V.tensor_tensor_reduce(out=prob[:, b, off:off + w], in0=ps[:, bk, c0:c0 + w],
                                           in1=bias[:, hd, SEQ - w:SEQ], scale=1.0, scalar=3e38, op0=ALU.add,
                                           op1=ALU.min, accum_out=att[:, b, qt:qt + 1]).then_inc(biased, 1)
                if b == 0:
                    sc = ps[:, 2, 256:256 + TT * C_PAD].rearrange("p (t c) -> p t c", t=TT)[:, :, 0:N_CMP]
                    step(V.scalar_tensor_tensor(pc[:], dcmp[:], 2.0 ** -(hd + 1), sc, ALU.mult, ALU.add))
                    step(V.tensor_reduce(out=att[:, 4, 0:4], in_=pc[:], op=ALU.min, axis=AX.X))
                    V.tensor_scalar(att[:, 4, 0:4], att[:, 4, 0:4], FLOOR, None, ALU.min).then_inc(cbiased, 1)

            def pair_lo(pr):
                dve.wait_ge(mixa_hi, pr + 1)
                V.tensor_tensor(ylo[:, pr, :], ps[:, 7, :], yhi[:, pr, :].bitcast(f32),
                                ALU.subtract).then_inc(mixa_lo, 1)

            gT = gates[:].rearrange("p t n -> p n t")
            add_bias(0)
            y_norm(TT - 1)

            def ssm_lo():
                for j in range(4):
                    dve.wait_ge(mixs_hi, j + 1)
                    V.scalar_tensor_tensor(ylo[:, 4 + j, :], ps[:, 3 + j, :], small["nw"][:, j:j + 1],
                                           yhi[:, 4 + j, :].bitcast(f32), ALU.mult, ALU.subtract).then_inc(mixs_lo, 1)
            for j in range(2 * HEADS):
                hd, b = j // 2, j % 2
                dve.wait_ge(exp_done, 4 * (j + 1))
                step(V.reciprocal(att[:, 6, 0:4], att[:, 2 + b, 0:4]))
                step(V.tensor_tensor(att[:, 6, 0:4], att[:, 6, 0:4], gT[:, 3 * hd + 1 + b, :], ALU.mult))
                for qt, off in widths:
                    w = (qt + 1) * P
                    V.tensor_scalar(prob[:, b, off:off + w], prob[:, b, off:off + w], att[:, 6, qt:qt + 1], None,
                                    ALU.mult).then_inc(scaled, 1)
                if b == 0:
                    dve.wait_ge(cexp_done, 4 * (hd + 1))
                    step(V.tensor_scalar(att[:, 7, 0:4], att[:, 5, 0:4], 1e-30, None, ALU.max))
                    step(V.reciprocal(att[:, 7, 0:4], att[:, 7, 0:4]))
                    step(V.tensor_tensor(att[:, 7, 0:4], att[:, 7, 0:4], gT[:, 3 * hd, :], ALU.mult))
                    V.tensor_tensor(pc[:], pc[:], att[:, 7, 0:4].unsqueeze(2).broadcast_to([P, TT, N_CMP]),
                                    ALU.mult).then_inc(scaled, 1)
                if j == 0:
                    q_low(TT - 1)
                    ssm_lo()
                if j == 1:
                    split_lo(U_OUT0 + TT - 1)
                    dve.wait_ge(k1_hi, 1)
                    V.tensor_tensor(klo[:, :, 1, :], ksD[:, :, 1, :], kh1[:].bitcast(f32),
                                    ALU.subtract).then_inc(k1_lo, 1)
                if j % 4 == 1 and j > 1:
                    pair_lo(j // 4 - 1)
                if j + 1 < 2 * HEADS:
                    if b == 1:
                        dve.wait_ge(p_tr, j)
                    add_bias(j + 1)
                dve.wait_ge(p_tr, j + 1)
                if j >= 2:
                    dve.wait_ge(pv_done, j - 1)
                V.tensor_copy(probT[:, b, 512:1024], ps[:, 4, :]).then_inc(pt_dve, 1)
            pair_lo(PAIRS - 1)
            for r in range(4):
                split_lo(U_OUT0 + 4 + r)
            boundary(0, U_GU0)

            def ffn(layer, u_gu, u_dn):
                f_base = FT * layer

                def tile(i, e, first):
                    f = 2 * i + e
                    u = u_gu + 2 * e
                    dve.wait_ge(unit_used, 4 * ((u + 1) // 4) + (u + 1) % 4 + 4 * i + 1)
                    dve.wait_ge(silu_done, f_base + f + 1)
                    if not first:
                        dve.wait_ge(hidlo_done, f_base + f - 1)
                    V.tensor_tensor(tmp[:, 2 + e, :], tmp[:, e, :], ps[:, 2 * e + 1, :], ALU.mult).then_inc(mult_done, 1)
                    split_lo(u + 4, i)
                    dve.wait_ge(hidhi_done, f_base + f + 1)
                    row = lambda tl: tl[:, f, :] if first else tl[:, ds(f, 1), :].rearrange("p a n -> p (a n)")
                    V.tensor_tensor(row(hidlo), tmp[:, 2 + e, :], row(hidhi).bitcast(f32),
                                    ALU.subtract).then_inc(hidlo_done, 1)
                    split_lo(u + 5, i)

                for e in range(2):
                    tile(0, e, True)
                with dve.Fori(1, FT // 2) as i:
                    for e in range(2):
                        tile(i, e, False)
                for r in range(2):
                    split_lo(u_dn + 4 + r)
                with dve.Fori(0, 3) as i:
                    for j in range(4):
                        split_lo(u_dn + 6 + j, i)
                for r in range(18, FT):
                    split_lo(u_dn + r)

            ffn(0, U_GU0, U_DN0)
            boundary(1, U_V)
            for qr in range(4):
                for j in range(3):
                    split_lo(U_V + 4 * qr + 4 + j)
                if qr == 0:
                    dve.wait_ge(rowsum_done, 1)
                    for j in range(WT):
                        g = j // 2
                        V.scalar_tensor_tensor(Rt[:, j, :], ps[:, 6 + g // 4, (g % 4) * P:(g % 4) * P + P],
                                               lnb[:, j:j + 1], bsbc[:, g, :], ALU.mult,
                                               ALU.add).then_inc(r_done, 1)
                for t in range(TT):
                    dve.wait_ge(vgelu_done, 4 * qr + t + 1)
                    V.bn_stats(vstat[:, t, qr, :], vG[:, t, 512 * qr:512 * qr + 512]).then_inc(dve_step, 1)
                    steps[0] += 1
                    if t == 2:
                        split_lo(U_V + 4 * qr + 7)
            for t in range(TT):
                if t == 0:
                    dve.wait_ge(dve_step, steps[0])
                V.bn_aggr(vmv[:, t, 0:2], vstat[:, t].rearrange("p a b -> p (a b)")).then_inc(vmv_done, 1)
            for t in range(TT):
                dve.wait_ge(vrstd_done, t + 1)
                V.tensor_scalar(vG[:, t, :], vG[:, t, :], vmv[:, t, 0:1], vmv[:, t, 2:3], ALU.subtract,
                                ALU.mult).then_inc(vnorm_done, 1)
            for j in range(WT):
                dve.wait_ge(mix_mm, j + 1)
                if j == 0:
                    dve.wait_ge(r_done, WT)
                V.scalar_tensor_tensor(mixed[:, j, :].rearrange("p (c n) -> p c n", c=TT),
                                       ps[:, 2 + j % 4, :].rearrange("p (c n) -> p c n", c=TT), lnw[:, j:j + 1],
                                       Rt[:, j, :].unsqueeze(1).broadcast_to([P, TT, P]), ALU.mult,
                                       ALU.add).then_inc(mixed_done, 1)
            dve.wait_ge(mixed_done, WT)
            for j in range(WT):
                dve.wait_ge(ugelu_done, j + 1)
                if j >= 2:
                    dve.wait_ge(glo_done, j - 1)
                V.tensor_tensor(tmp[:, 2 + j % 2, :], tmp[:, j % 2, :], mixed[:, j, :], ALU.mult).then_inc(g_done, 1)
                split_lo(U_U + j + 4)
                dve.wait_ge(ghi_done, j + 1)
                V.tensor_tensor(glo[:, j, :], tmp[:, 2 + j % 2, :], ghi[:, j, :].bitcast(f32),
                                ALU.subtract).then_inc(glo_done, 1)
            for r in range(4, WT):
                split_lo(U_OUT1 + r)
            boundary(2, U_GU1)
            ffn(1, U_GU1, U_DN1)
            boundary(3, None)

        @block.tensor
        def _(pe):
            T = nc.tensor

            def ready(u, i=0):
                pe.wait_ge(lo_done, 4 * (u // 4 + i) + u % 4 + 1)

            def col_unit(u, bank, i=0):
                s = u % SLOTS
                ready(u, i)
                for k in range(KT):
                    hi, lo = whi[:, s, k * P:k * P + P], wlo[:, s, k * P:k * P + P]
                    T.matmul(ps[:, bank, :], hi, yhi[:, k, :], start=(k == 0), stop=False)
                    T.matmul(ps[:, bank, :], hi, ylo[:, k, :], start=False, stop=False)
                    last = T.matmul(ps[:, bank, :], lo, yhi[:, k, :], start=False, stop=(k == KT - 1))
                return last

            def row_products(s, t, hi, lo, first, last_k):
                for hf in range(2):
                    o = ps[:, 2 * t + hf, :]
                    c = slice(512 * hf, 512 * hf + 512)
                    T.matmul(o, hi[:, t * P:t * P + P], whi[:, s, c], start=first, stop=False)
                    T.matmul(o, hi[:, t * P:t * P + P], wlo[:, s, c], start=False, stop=False)
                    last = T.matmul(o, lo[:, t * P:t * P + P], whi[:, s, c], start=False, stop=last_k)
                return last

            def opening(k, u, half):
                pe.wait_ge(ylo_done, 4 * k + 2)
                ready(u)
                half(0, 0)
                if k:
                    pre_transpose(k, TT - 2)
                pre_transpose(k, TT - 1)
                ready(u + 1)
                half(1, 0)
                pe.wait_ge(ylo_done, 4 * k + 4)
                half(0, 1).then_inc(unit_used, 1)
                half(1, 1).then_inc(unit_used, 1)

            def col_half(u, bank, side):
                s = u % SLOTS
                c = slice(256 * side, 256 * side + 256)
                for k in range(KT):
                    hi, lo = whi[:, s, k * P:k * P + P], wlo[:, s, k * P:k * P + P]
                    T.matmul(ps[:, bank, c], hi, yhi[:, k, c], start=(k == 0), stop=False)
                    T.matmul(ps[:, bank, c], hi, ylo[:, k, c], start=False, stop=False)
                    last = T.matmul(ps[:, bank, c], lo, yhi[:, k, c], start=False, stop=(k == KT - 1))
                return last

            def rows(m, u0, n, hi, lo, peel, second_half_free, staged_base=0):
                for r in range(peel):
                    ready(u0 + r)
                    for q, t in enumerate((2, 3, 0, 1)):
                        if r == 0 and q == 2:
                            second_half_free()
                        last = row_products((u0 + r) % SLOTS, t, hi[:, r, :], lo[:, r, :], r == 0, False)
                    last.then_inc(unit_used, 1)
                loops = (n - peel - TAIL) // 4
                if loops:
                    with pe.Fori(0, loops) as i:
                        for j in range(4):
                            u = u0 + peel + j
                            pe.wait_ge(staged, staged_base + 8 * i + 2 * (j + 1))
                            ready(u, i)
                            for t in range(TT):
                                last = row_products(u % SLOTS, t, yhi[:, j % 2, :], ylo[:, j % 2, :], False, False)
                            last.then_inc(unit_used, 1)
                for t in range(TT):
                    for r in range(n - TAIL, n):
                        if t == 0:
                            ready(u0 + r)
                        if m < 3 and t == TT - 1 and r == n - 1:
                            pre_transpose(m + 1, 1)
                        last = row_products((u0 + r) % SLOTS, t, hi[:, r, :], lo[:, r, :], peel == 0 and r == n - TAIL,
                                            r == n - 1)
                        if r == n - 1 and t < TT - 1:
                            last.then_inc(rows_done, 1)
                        if t == TT - 1:
                            last.then_inc(unit_used, 1)
                    if m < 3 and t == 2:
                        pre_transpose(m + 1, 0)

            def pre_transpose(k, t):
                n = 4 * k + t
                pe.wait_ge(hn_done, n + 1)
                b0 = transposed_bank(k, t)
                for kk in range(KT):
                    last = T.transpose(ps[:, b0 + kk // 4, (kk % 4) * P:(kk % 4) * P + P],
                                       hn[:, n % 2, kk * P:kk * P + P], ident[:])
                last.then_inc(transposed, 1)

            pe.wait_ge(consts_made, 1)
            for t in range(3):
                pre_transpose(0, t)

            def wide(u, k0, k1, width, out, tiles=range(TT)):
                ready(u)
                s = u % SLOTS
                for t in tiles:
                    for kk in range(k0, k1):
                        c = slice((kk - k0) * width, (kk - k0 + 1) * width)
                        yh, yl = yhi[:, kk, t * P:t * P + P], ylo[:, kk, t * P:t * P + P]
                        T.matmul(out(t), yh, whi[:, s, c], start=(kk == 0), stop=False)
                        T.matmul(out(t), yh, wlo[:, s, c], start=False, stop=False)
                        last = T.matmul(out(t), yl, whi[:, s, c], start=False, stop=(kk == KT - 1))
                return last

            def vv_unit(r, tiles=range(TT)):
                return wide(U_VV + r, 3 * r, min(3 * r + 3, KT), VV, lambda t: ps[:, 4 + t, 0:VV], tiles)

            opening(0, U_VV, lambda j, side: vv_unit(j, range(2 * side, 2 * side + 2)))
            vv_unit(2).then_inc(unit_used, 1)
            for j in range(8):
                if j >= 4:
                    pe.wait_ge(conv_done, j - 3)
                col_unit(U_XBC + j, j % 4).then_inc(unit_used, 1)
                if j == 1:
                    pe.wait_ge(da_done, 1)
                    pe.wait_ge(v_out, TT)
                    pe.wait_ge(consts_made, 2)
                    T.matmul(ps[:, 4, 0:32], small["U"][:], sm[:, 13, :], start=True, stop=True).then_inc(cums_done, 1)
                    T.matmul(ps[:, 4, 32:64], ones[:], sm[:, 13, :], start=True, stop=True).then_inc(cums_done, 1)
            for j in range(2):
                pe.wait_ge(conv_done, 5 + j)
                col_unit(U_C + j, j).then_inc(unit_used, 1)
            pe.wait_ge(dst_in, 1)
            pe.wait_ge(ssm_exp, 2)
            for r in range(4):
                wide(U_Z + r, 2 * r, 2 * r + 2, 512, lambda t: ps[:, 4 + t, :]).then_inc(unit_used, 1)
            pe.wait_ge(blk_done, 16)
            pe.wait_ge(c_out, 1)
            for y, w1t in ((0, w1k), (1, w1v)):
                for ht in range(2):
                    c0 = (2 * y + ht) * 2 * N_CMP
                    for pr in range(16):
                        last = T.matmul(ps[:, 0, c0:c0 + 2 * N_CMP], w1t[:, pr, ht * P:ht * P + P], blk[:, y, pr, :],
                                        start=(pr == 0), stop=(pr == 15))
            last.then_inc(cmp_hid, 1)
            pe.wait_ge(conv_done, 7)
            col_unit(U_KS, 2).then_inc(unit_used, 1)
            pe.wait_ge(c_out, 2)
            pe.wait_ge(cmp_silu, 1)
            for e in range(2):
                for ht in range(2):
                    T.matmul(ps[64 * e:64 * e + 64, 1, 0:2 * N_CMP], w2s[:, 0, ht, :], hidc[:, 0, ht, :],
                             start=(ht == 0), stop=(ht == 1))
            for g in range(2):
                for ht in range(2):
                    last = T.matmul(ps[0:N_CMP, 1, 128 + 64 * g:192 + 64 * g],
                                    hidc[:, 1, ht, N_CMP * g:N_CMP * g + N_CMP], w2s[:, 1, ht, :],
                                    start=(ht == 0), stop=(ht == 1))
            last.then_inc(cmp_kv, 1)
            pe.wait_ge(conv_done, 8)
            col_unit(U_KS + 1, 3).then_inc(unit_used, 1)
            pe.wait_ge(xbc_ready, 8)
            pe.wait_ge(cmp_out, 1)
            for c in range(TT):
                if c < 2:
                    pe.wait_ge(ka_out, 2 * c + 2)
                    pe.wait_ge(kd_out, 4 * c + 4)
                else:
                    pe.wait_ge(xn_out, c - 1)
                    pe.wait_ge(bn_out, c - 1)
                for j in range(4):
                    T.transpose(ps[:, c % 2, j * P:j * P + P], xbcT[:, j, c * P:c * P + P], ident[:])
                for g in range(2):
                    last = T.transpose(ps[:, 2 + c % 2, g * P:g * P + P], xbcT[:, 4 + g, c * P:c * P + P], ident[:])
                last.then_inc(xb_tr, 1)
            av = sm[:, 13, :]

            def segments(c):
                tok = slice(c * P, c * P + P)
                if c:
                    pe.wait_ge(dec_done, 8 * c)
                    pe.wait_ge(m_done, 2 * c)
                for g in range(2):
                    T.matmul(ps[:, g, :].rearrange("p (q n) -> p q n", q=4), ident_bf[:],
                             mneg[:].unsqueeze(1).broadcast_to([P, 4, P]), start=True, stop=False)
                    for q in range(4):
                        col = 8 * c + 4 * g + q
                        last = T.matmul(ps[:, g, q * P:q * P + P], av[:, col:col + 1].broadcast_to([P, P]),
                                        small["U"][:], start=False, stop=(q == 3))
                for g in range(2):
                    last = T.matmul(ps[:, 2, P * g:P * g + P], xbcT[:, 4 + g, tok], xbcT[:, 6 + g, tok],
                                    start=True, stop=True)
                last.then_inc(ssm_seg, 1)

            pe.wait_ge(xn_out, TT)
            pe.wait_ge(bn_out, TT)
            pe.wait_ge(consts_made, 4)
            segments(0)
            for c in range(TT):
                tok = slice(c * P, c * P + P)
                if c == 0:
                    pe.wait_ge(z_ready, 4)
                elif c == 2:
                    pe.wait_ge(q_lo, 2)
                if c < TT - 1:
                    col_unit(U_Q + c, 6 + c % 2).then_inc(unit_used, 1)
                else:
                    pe.wait_ge(q_lo, 4)
                    ready(U_Q + c)
                    col_half(U_Q + c, 6 + c % 2, 0)
                pe.wait_ge(xd_done, c + 1)
                if c:
                    pe.wait_ge(y_gated, 2 * c)
                for g in range(2):
                    T.matmul(ps[:, 4, 256 * g:256 * g + 256], xbcT[:, 6 + g, tok], prev[:, 256 * g:256 * g + 256],
                             start=True, stop=True)
                    if c < TT - 1:
                        T.matmul(ps[:, 5, 256 * g:256 * g + 256], BN[:, c, P * g:P * g + P],
                                 xdd[:, 256 * g:256 * g + 256], start=True, stop=True)
                pe.wait_ge(m_done, 2 * (c + 1))
                for hd in range(HEADS):
                    last = T.matmul(ps[:, 3, 64 * hd:64 * hd + 64], Mt[:, hd, :], xdt[:, 64 * hd:64 * hd + 64],
                                    start=True, stop=True)
                last.then_inc(ssm_mm, 1)
                if c < TT - 1:
                    segments(c + 1)

            widths = [(3, 0), (2, 512), (0, 896), (1, 1024)]
            where = {3: (0, 0), 2: (1, 0), 0: (1, 384), 1: (2, 0)}
            p_off = dict(widths)
            tr = {0: (3, 0, 0), 1: (4, 0, 512), 3: (4, 384, 896), 2: (5, 0, 1024)}

            def scaled_before(j):
                return 9 * (j // 2) + 5 * (j % 2)

            def scores(j):
                hd, kind = j // 2, j % 2
                e, g = hd % 2, hd // 4
                q = (q_odd if e else q_even)[:, hd // 2, :]
                key_parts = ((kh1 if g else kh0)[:, kind, :], klo[:, kind, g, :])
                if j == HEADS:
                    pe.wait_ge(k1_lo, 1)
                if j == 12:
                    pe.wait_ge(q_lo, 8)
                if j:
                    pe.wait_ge(biased, 4 * j)
                    pe.wait_ge(cbiased, (j + 1) // 2)
                for qt, _ in widths:
                    bk, c0 = where[qt]
                    w = (qt + 1) * P
                    for part, keys in enumerate(key_parts):
                        last = T.matmul(ps[:, bk, c0:c0 + w], q[:, qt * P:qt * P + P], keys[:, 0:w],
                                        start=(part == 0), stop=(part == 1))
                if kind == 0:
                    for qt in range(TT):
                        for part, keys in enumerate((kch[:, g, :], kcl[:, g, :])):
                            last = T.matmul(ps[:, 2, 256 + C_PAD * qt:256 + C_PAD * (qt + 1)],
                                            q[:, qt * P:qt * P + P], keys, start=(part == 0), stop=(part == 1))
                last.then_inc(qk_done, 1)

            def values(j):
                hd, b = j // 2, j % 2
                e, g = hd % 2, hd // 4
                pe.wait_ge(pt_act, (5 * (j + 1) + 1) // 2)
                pe.wait_ge(pt_dve, j + 1)
                if j == 0:
                    pe.wait_ge(q_lo, 8)
                elif j % 4 == 0:
                    pe.wait_ge(mixa_lo, j // 4)
                o = slice(64 * e, 64 * e + 64)
                for kt in (range(TT) if b == 0 else reversed(range(TT))):
                    c0 = tr[kt][2]
                    w = SEQ - kt * P
                    last = T.matmul(ps[o, 7, kt * P:SEQ], vN[:, kt, P * b + 64 * g:P * b + 64 * g + 64],
                                    probT[:, b, c0:c0 + w], start=(kt == 0 and b == 0), stop=(kt == 0 and b == 1))
                if b == 0:
                    last = T.matmul(ps[o, 7, :], vcb[0:N_CMP, g, :], pcT[0:N_CMP, :], start=False, stop=False)
                last.then_inc(pv_done, 1)

            pe.wait_ge(cmp_out, 1)
            pe.wait_ge(dec_done, 8 * TT)
            pe.wait_ge(m_done, 2 * TT)
            pe.wait_ge(q_lo, 6)
            scores(0)
            col_half(U_Q + TT - 1, 7, 1).then_inc(unit_used, 1)
            pe.wait_ge(yn_done, 8)
            for j in range(4):
                for c in range(TT):
                    last = T.transpose(ps[:, 3 + j, c * P:c * P + P], zN[:, c, j * P:j * P + P], ident[:])
            last.then_inc(y_tr, 1)
            scores(1)
            for j in range(2 * HEADS):
                hd, b = j // 2, j % 2
                if 1 <= j < 2 * HEADS - 1:
                    scores(j + 1)
                if j == 0:
                    pe.wait_ge(mixs_lo, 4)
                if j:
                    pe.wait_ge(pt_act, (5 * j + 1) // 2)
                    pe.wait_ge(pt_dve, j)
                for idx, (qt, _) in enumerate(widths):
                    pe.wait_ge(scaled, scaled_before(j) + idx + 1)
                    for kt in range(qt + 1):
                        bk, c0, _ = tr[kt]
                        last = T.transpose(ps[:, bk, c0 + (qt - kt) * P:c0 + (qt - kt) * P + P],
                                           prob[:, b, p_off[qt] + kt * P:p_off[qt] + kt * P + P], ident[:])
                if b == 0:
                    pe.wait_ge(scaled, scaled_before(j) + 5)
                    for qt in range(TT):
                        last = T.transpose(ps[0:N_CMP, 6, qt * P:qt * P + P], pc[:, qt, :], ident[:])
                last.then_inc(p_tr, 1)
                if j:
                    values(j - 1)
            values(2 * HEADS - 1)
            pe.wait_ge(mixa_lo, PAIRS)
            rows(0, U_OUT0, KT, yhi, ylo, 4, lambda: None)

            def ffn(layer, k, m, u_gu, u_dn):
                f_base = FT * layer
                def tile(i, e):
                    u = u_gu + 2 * e
                    pe.wait_ge(mult_done, f_base + 2 * i + e - 1)
                    col_unit(u, 2 * e, i).then_inc(unit_used, 1)
                    col_unit(u + 1, 2 * e + 1, i).then_inc(unit_used, 1)

                opening(k, u_gu, lambda j, side: col_half(u_gu + j, j, side))
                for j in range(2, 4):
                    col_unit(u_gu + j, j).then_inc(unit_used, 1)
                with pe.Fori(1, FT // 2) as i:
                    for e in range(2):
                        tile(i, e)
                pe.wait_ge(hidlo_done, f_base + 2)
                rows(m, u_dn, FT, hidhi, hidlo, 2,
                     lambda: pe.wait_ge(mult_done, f_base + FT), staged_base=0 if layer == 0 else 32 + 16)

            ffn(0, 1, 1, U_GU0, U_DN0)
            def v_unit(qr, j, tiles):
                u = U_V + 4 * qr + j
                ready(u)
                s = u % SLOTS
                for t in tiles:
                    if qr >= 2 and j == 0:
                        pe.wait_ge(vgelu_done, 4 * (qr - 2) + t + 1)
                    bank = 4 * (qr % 2) + t
                    for b in range(2):
                        kk = 2 * j + b
                        c = slice(512 * b, 512 * b + 512)
                        yh, yl = yhi[:, kk, t * P:t * P + P], ylo[:, kk, t * P:t * P + P]
                        T.matmul(ps[:, bank, :], yh, whi[:, s, c], start=(kk == 0), stop=False)
                        T.matmul(ps[:, bank, :], yh, wlo[:, s, c], start=False, stop=False)
                        last = T.matmul(ps[:, bank, :], yl, whi[:, s, c], start=False, stop=(kk == KT - 1))
                    if j == 3 and t < TT - 1:
                        last.then_inc(v_done, 1)
                return last

            opening(2, U_V, lambda j, side: v_unit(0, j, range(2 * side, 2 * side + 2)))
            for qr in range(4):
                if qr == 1:
                    pe.wait_ge(r_done, WT)
                for j in range(4):
                    if qr == 0 and j == 2:
                        pe.wait_ge(ws_masked, 1)
                        for g in range(8):
                            last = T.transpose(ps[:, 4 + g // 4, (g % 4) * P:(g % 4) * P + P], ws[:, g, :], ident[:])
                        last.then_inc(ws_tr, 1)
                    if qr == 0 and j == 3:
                        pe.wait_ge(ws_out, 1)
                        for b in range(2):
                            last = T.matmul(ps[:, 6 + b, :], ones[:],
                                            wsT[:, 4 * b:4 * b + 4, :].rearrange("p g t -> p (g t)"),
                                            start=True, stop=True)
                        last.then_inc(rowsum_done, 1)
                    if qr == 0 and j < 2:
                        continue
                    v_unit(qr, j, range(TT)).then_inc(unit_used, 1)
            pe.wait_ge(vgelu_done, 16)
            for j in range(2):
                col_unit(U_U + j, j).then_inc(unit_used, 1)
            pe.wait_ge(vnorm_done, 4)
            for j in range(WT):
                if j >= 4:
                    pe.wait_ge(mixed_done, j - 3)
                for c in range(TT):
                    last = T.matmul(ps[:, 2 + j % 4, c * P:c * P + P], vG[:, c, j * P:j * P + P], wsT[:, j // 2, :],
                                    start=True, stop=True)
                last.then_inc(mix_mm, 1)
            for j in range(2, WT):
                pe.wait_ge(ugelu_done, j - 1)
                col_unit(U_U + j, j % 2).then_inc(unit_used, 1)
            pe.wait_ge(mixed_done, WT)
            pe.wait_ge(glo_done, 4)
            rows(2, U_OUT1, WT, ghi, glo, 4, lambda: pe.wait_ge(ugelu_done, WT), staged_base=32)
            ffn(1, 3, 3, U_GU1, U_DN1)
    return nc


def column_units(w):
    n = w.shape[1] // P
    return w.reshape(KT, P, n, P).transpose(2, 1, 0, 3).reshape(n, P, UNIT)


def row_units(w):
    return w.reshape(-1, P, UNIT)


def wide_units(w, c0, width):
    k = UNIT // width
    return w[:, c0:c0 + width].reshape(KT // k, k, P, width).transpose(0, 2, 1, 3).reshape(KT // k, P, UNIT)


def kernel(x, norm_gains, ffn_w_gate, ffn_w_up, ffn_w_down, ev_w_in, ev_w_out, nsa_cmp_pe, nsa_cmp_w1, nsa_cmp_w2,
           ssm_conv_w, ssm_conv_b, ssm_dt_bias, ssm_a_log, ssm_d, ssm_norm_w, od_w_in, od_ln_w, od_ln_b, od_w_s,
           od_b_s, od_w_out):
    import concourse.bacc as bacc
    from concourse import mybir
    from concourse.bass_utils import run_bass_kernel_spmd

    def ffn_units(layer):
        gu = np.stack([column_units(ffn_w_gate[layer]), column_units(ffn_w_up[layer])], axis=1)
        return [gu.reshape(2 * FT, P, UNIT), row_units(ffn_w_down[layer])]

    w_in, g_in = ev_w_in[0], od_w_in[0]
    v2 = np.concatenate([w_in[:, c:c + n] for c, n in ((C_VS, P), (C_VW, P), (C_GATE, N_GATE), (C_DT, HEADS))], axis=1)
    v2 = np.concatenate([v2, np.zeros((P, VV), v2.dtype)], axis=0).reshape(3, 3, P, VV).transpose(0, 2, 1, 3)
    v2 = np.concatenate([v2.reshape(3, P, 3 * VV), np.zeros((3, P, UNIT - 3 * VV), v2.dtype)], axis=2)

    def columns(*firsts):
        return column_units(np.concatenate([w_in[:, c:c + P] for c in firsts], axis=1))

    stream = np.concatenate(
        [v2, columns(*range(C_XBC, C_XBC + 1024, P)), columns(C_KC, C_VC), wide_units(w_in, C_Z, 512),
         columns(C_KS, C_KW), columns(*range(C_Q, C_Q + 512, P)), row_units(ev_w_out[0])]
        + ffn_units(0)
        + [wide_units(g_in, WIDTH + 512 * q, 512) for q in range(4)]
        + [column_units(g_in[:, 0:WIDTH]), row_units(od_w_out[0])]
        + ffn_units(1), axis=0)
    pe = nsa_cmp_pe[0].transpose(2, 0, 1).reshape(HEAD_DIM, 2 * CMP_BLOCK)
    cols = np.concatenate(
        [ssm_conv_w[0].reshape(CONV_TAPS, 8, P).transpose(2, 0, 1).reshape(P, 32), ssm_conv_b[0].reshape(8, P).T,
         ssm_norm_w[0].reshape(4, P).T, np.concatenate([pe, pe], axis=0), od_ln_w[0].reshape(WT, P).T,
         od_ln_b[0].reshape(WT, P).T], axis=1)

    nc = bacc.Bacc("TRN2", target_bir_lowering=False, num_devices=1)
    arrays, args = {}, []
    for name, v in (("x", x), ("gains", norm_gains), ("stream", stream), ("cols", cols),
                    ("w1", nsa_cmp_w1), ("w2", nsa_cmp_w2), ("dt_bias", ssm_dt_bias), ("a_log", ssm_a_log),
                    ("d_skip", ssm_d), ("w_s", od_w_s), ("b_s", od_b_s)):
        arrays["in_" + name] = np.ascontiguousarray(v)
        args.append(nc.dram_tensor("in_" + name, v.shape, mybir.dt.float32, kind="ExternalInput").ap())
    out = nc.dram_tensor("out_h", (1, SEQ, D_MODEL), mybir.dt.float32, kind="ExternalOutput").ap()
    build(nc, *args, out)
    r = run_bass_kernel_spmd(nc, [arrays], core_ids=[0])
    return r.results[0]["out_h"]
```
